# Optimizing a Trainium2 kernel written in Bass

```python
import functools
import jax, jax.numpy as jnp
from jax import lax
import numpy as np

D_MODEL = 1024
BATCH = 1
SEQ = 256
DEPTH = 1
DEC_BATCH = 8
DEC_SEQ = 4
PAST_LEN = 1024
PAGE_SIZE = 128

MIX_W = D_MODEL
POOL_W = MIX_W // 2
POOL_WINDOWS = (2, 4, 8, 16)
N_POOL_GROUPS = 4
POOL_GW = POOL_W // N_POOL_GROUPS
POOL_STATE = 15
ATT_W = MIX_W - POOL_W
HEAD_DIM = 128
N_HEADS = ATT_W // HEAD_DIM
IDX_HEADS = 8
IDX_DIM = 64
TOPK_MAX = 256
ROPE_THETA = 10000.0
Q_BLOCK = 128
N_KEYS = 128
N_EXPERTS = N_KEYS * N_KEYS
PEER_HEADS = 8
PEER_TOPK = 16
PEER_QDIM = 256
PEER_HALF = PEER_QDIM // 2
PEER_BLOCK = 128
EPS = 1e-6
SPLIT_SIZES = (POOL_W, N_HEADS * HEAD_DIM, HEAD_DIM, HEAD_DIM, IDX_HEADS * IDX_DIM, IDX_DIM, IDX_HEADS)
IN_W = POOL_W + N_HEADS * HEAD_DIM + 2 * HEAD_DIM + IDX_HEADS * IDX_DIM + IDX_DIM + IDX_HEADS

kernel_name = "hybrid_pool_dsa_peer_step"

def rms_norm(x, g):
    xf = x.astype(jnp.float32)
    y = xf * lax.rsqrt(jnp.mean(xf * xf, axis=-1, keepdims=True) + EPS)
    return (y * g.astype(jnp.float32)).astype(x.dtype)

def rope(x, pos):
    half = x.shape[-1] // 2
    inv = ROPE_THETA ** (-jnp.arange(half, dtype=jnp.float32) / half)
    ang = pos.astype(jnp.float32)[:, None] * inv[None, :]
    cos = jnp.cos(ang)[None, :, None, :]
    sin = jnp.sin(ang)[None, :, None, :]
    xf = x.astype(jnp.float32)
    x1, x2 = xf[..., :half], xf[..., half:]
    return jnp.concatenate([x1 * cos - x2 * sin, x2 * cos + x1 * sin], axis=-1).astype(x.dtype)

def project(h, pos, w_in, q_norm_g, k_norm_g):
    B, T, _ = h.shape
    z = h @ w_in
    offs = np.cumsum(np.array(SPLIT_SIZES))[:-1].tolist()
    u, q, k, v, iq, ik, iw = jnp.split(z, offs, axis=-1)
    q = rope(rms_norm(q.reshape(B, T, N_HEADS, HEAD_DIM), q_norm_g), pos)
    k = rope(rms_norm(k[:, :, None, :], k_norm_g), pos)[:, :, 0]
    iq = rope(iq.reshape(B, T, IDX_HEADS, IDX_DIM), pos)
    ik = rope(ik[:, :, None, :], pos)[:, :, 0]
    iw = iw * (IDX_HEADS ** -0.5)
    return u, q, k, v, iq, ik, iw

def pool_mix(u, prefix, start_pos, w_pool, pool_scale):
    T = u.shape[1]
    full = jnp.concatenate([prefix, u], axis=1)
    c = jnp.cumsum(full.astype(jnp.float32), axis=1)
    c = jnp.pad(c, ((0, 0), (1, 0), (0, 0)))
    pos = start_pos + jnp.arange(T)
    outs = []
    for g, w in enumerate(POOL_WINDOWS):
        sl = slice(g * POOL_GW, (g + 1) * POOL_GW)
        hi = c[:, POOL_STATE + 1:POOL_STATE + 1 + T, sl]
        lo = c[:, POOL_STATE + 1 - w:POOL_STATE + 1 - w + T, sl]
        cnt = jnp.minimum(pos + 1, w).astype(jnp.float32)[None, :, None]
        d = ((hi - lo) / cnt - u[..., sl].astype(jnp.float32)).astype(u.dtype)
        outs.append(d @ w_pool[g])
    y = jnp.concatenate(outs, axis=-1) * pool_scale
    return y, full[:, -POOL_STATE:]

def take_rows(a, idx):
    return jax.vmap(lambda ab, ib: ab[ib])(a, idx)

def dsa_block(q, iq, iw, qpos, idx_keys, k_sel, gather_kv):
    L = idx_keys.shape[1]
    s = jnp.einsum('bqhd,bld->bqhl', iq, idx_keys)
    score = jnp.einsum('bqhl,bqh->bql', jax.nn.relu(s), iw).astype(jnp.float32)
    adm = jnp.arange(L)[None, None, :] <= qpos[None, :, None]
    score = jnp.where(adm, score, -jnp.inf)
    top_val, top_idx = lax.top_k(score, k_sel)
    valid = jnp.isfinite(top_val)
    k_rows, v_rows = gather_kv(top_idx)
    logits = jnp.einsum('bqhd,bqkd->bqhk', q, k_rows).astype(jnp.float32) * (HEAD_DIM ** -0.5)
    logits = jnp.where(valid[:, :, None, :], logits, -jnp.inf)
    p = jax.nn.softmax(logits, axis=-1).astype(v_rows.dtype)
    return jnp.einsum('bqhk,bqkd->bqhd', p, v_rows)

def dsa_prompt(q, k, v, iq, ik, iw):
    B, S = q.shape[:2]
    k_sel = min(TOPK_MAX, S // 4)
    nb = S // Q_BLOCK

    def to_blocks(a):
        return a.reshape(B, nb, Q_BLOCK, *a.shape[2:]).swapaxes(0, 1)

    qpos = jnp.arange(S).reshape(nb, Q_BLOCK)
    gather = lambda idx: (take_rows(k, idx), take_rows(v, idx))

    def body(args):
        qb, iqb, iwb, pb = args
        return dsa_block(qb, iqb, iwb, pb, ik, k_sel, gather)

    out = lax.map(body, (to_blocks(q), to_blocks(iq), to_blocks(iw), qpos))
    return out.swapaxes(0, 1).reshape(B, S, N_HEADS * HEAD_DIM)

def dsa_sample(q, k, v, iq, ik, iw, cache_k, cache_v, cache_ik, page_table):
    DB, DS = q.shape[:2]
    P = page_table.shape[1] * PAGE_SIZE
    past_ik = cache_ik[page_table].reshape(DB, P, IDX_DIM)
    idx_keys = jnp.concatenate([past_ik, ik], axis=1)
    k_sel = min(TOPK_MAX, (P + DS) // 4)

    def gather(idx):
        in_past = (idx < P)[..., None]
        pidx = jnp.minimum(idx, P - 1)
        phys = jax.vmap(lambda pt, i: pt[i])(page_table, pidx // PAGE_SIZE)
        off = pidx % PAGE_SIZE
        nidx = jnp.clip(idx - P, 0, DS - 1)
        k_rows = jnp.where(in_past, cache_k[phys, off], take_rows(k, nidx))
        v_rows = jnp.where(in_past, cache_v[phys, off], take_rows(v, nidx))
        return k_rows, v_rows

    qpos = P + jnp.arange(DS)
    out = dsa_block(q, iq, iw, qpos, idx_keys, k_sel, gather)
    return out.reshape(DB, DS, N_HEADS * HEAD_DIM)

def peer(h, w_pq, sub_keys, expert_u, expert_v):
    B, T, D = h.shape
    hf = h.reshape(-1, D)
    N = hf.shape[0]
    q = (hf @ w_pq).reshape(N, PEER_HEADS, 2, PEER_HALF)
    s = jnp.einsum('nhcd,hckd->nhck', q, sub_keys).astype(jnp.float32)
    sv, si = lax.top_k(s, PEER_TOPK)
    cand = sv[:, :, 0, :, None] + sv[:, :, 1, None, :]
    cidx = si[:, :, 0, :, None] * N_KEYS + si[:, :, 1, None, :]
    fv, fi = lax.top_k(cand.reshape(N, PEER_HEADS, PEER_TOPK * PEER_TOPK), PEER_TOPK)
    eidx = jnp.take_along_axis(cidx.reshape(N, PEER_HEADS, PEER_TOPK * PEER_TOPK), fi, axis=-1)
    g = jax.nn.softmax(fv, axis=-1).astype(h.dtype)
    E = PEER_HEADS * PEER_TOPK
    eidx = eidx.reshape(N, E)
    g = g.reshape(N, E)
    nb = -(-N // PEER_BLOCK)
    pad = nb * PEER_BLOCK - N
    xb = jnp.pad(hf, ((0, pad), (0, 0))).reshape(nb, PEER_BLOCK, D)
    eb = jnp.pad(eidx, ((0, pad), (0, 0))).reshape(nb, PEER_BLOCK, E)
    gb = jnp.pad(g, ((0, pad), (0, 0))).reshape(nb, PEER_BLOCK, E)

    def body(args):
        xt, et, gt = args
        a = jax.nn.gelu(jnp.einsum('td,ted->te', xt, expert_u[et]), approximate=False)
        return jnp.einsum('te,ted->td', gt * a, expert_v[et])

    out = lax.map(body, (xb, eb, gb)).reshape(-1, D)[:N]
    return out.reshape(B, T, D)

def trunk_layer(x, pos0, pool_prefix, attend, norm1_g, w_in, q_norm_g, k_norm_g, w_pool,
                pool_scale, w_o, norm2_g, w_pq, sub_keys, expert_u, expert_v):
    T = x.shape[1]
    pos = pos0 + jnp.arange(T)
    h = rms_norm(x, norm1_g)
    u, q, k, v, iq, ik, iw = project(h, pos, w_in, q_norm_g, k_norm_g)
    ya, pool_state = pool_mix(u, pool_prefix, pos0, w_pool, pool_scale)
    yb = attend(q, k, v, iq, ik, iw)
    x = x + jnp.concatenate([ya, yb], axis=-1) @ w_o
    x = x + peer(rms_norm(x, norm2_g), w_pq, sub_keys, expert_u, expert_v)
    return x, k, v, ik, pool_state

def setup_inputs(seed: int = 0) -> dict:
    key = jax.random.key(seed)
    ks = jax.random.split(key, 24)
    f32 = jnp.float32
    n_pages = PAST_LEN // PAGE_SIZE
    n_used = DEC_BATCH * n_pages
    n_pool = (n_used * 5 + 3) // 4
    nrm = lambda k, shape, s: jax.random.normal(k, shape, f32) * s
    perm = jax.random.permutation(ks[0], n_pool)[:n_used]
    return {
        "x_prompt": nrm(ks[1], (BATCH, SEQ, D_MODEL), 1.0),
        "x_sample": nrm(ks[2], (DEC_BATCH, DEC_SEQ, D_MODEL), 1.0),
        "cache_k": nrm(ks[3], (DEPTH, n_pool, PAGE_SIZE, HEAD_DIM), 1.0),
        "cache_v": nrm(ks[4], (DEPTH, n_pool, PAGE_SIZE, HEAD_DIM), 1.0),
        "cache_ik": nrm(ks[5], (DEPTH, n_pool, PAGE_SIZE, IDX_DIM), 1.0),
        "state_pool": nrm(ks[6], (DEPTH, DEC_BATCH, POOL_STATE, POOL_W), 1.0),
        "page_table": perm.reshape(DEC_BATCH, n_pages).astype(jnp.int32),
        "norm1_g": 1.0 + nrm(ks[7], (DEPTH, D_MODEL), 0.02),
        "w_in": nrm(ks[8], (DEPTH, D_MODEL, IN_W), D_MODEL ** -0.5),
        "q_norm_g": 1.0 + nrm(ks[9], (DEPTH, HEAD_DIM), 0.02),
        "k_norm_g": 1.0 + nrm(ks[10], (DEPTH, HEAD_DIM), 0.02),
        "w_pool": nrm(ks[11], (DEPTH, N_POOL_GROUPS, POOL_GW, POOL_GW), POOL_GW ** -0.5),
        "pool_scale": 1.0 + nrm(ks[12], (DEPTH, POOL_W), 0.1),
        "w_o": nrm(ks[13], (DEPTH, MIX_W, D_MODEL), MIX_W ** -0.5),
        "norm2_g": 1.0 + nrm(ks[14], (DEPTH, D_MODEL), 0.02),
        "w_pq": nrm(ks[15], (DEPTH, D_MODEL, PEER_HEADS * PEER_QDIM), D_MODEL ** -0.5),
        "sub_keys": nrm(ks[16], (DEPTH, PEER_HEADS, 2, N_KEYS, PEER_HALF), PEER_HALF ** -0.5),
        "expert_u": nrm(ks[17], (DEPTH, N_EXPERTS, D_MODEL), D_MODEL ** -0.5),
        "expert_v": nrm(ks[18], (DEPTH, N_EXPERTS, D_MODEL), 0.35),
    }

def reference(x_prompt, x_sample, cache_k, cache_v, cache_ik, state_pool, page_table,
              norm1_g, w_in, q_norm_g, k_norm_g, w_pool, pool_scale, w_o, norm2_g,
              w_pq, sub_keys, expert_u, expert_v):
    past = page_table.shape[1] * PAGE_SIZE
    yp, ys = x_prompt, x_sample
    kp, vp, ikp, pp, kd, vd, ikd, pd = [], [], [], [], [], [], [], []
    for l in range(DEPTH):
        lw = (norm1_g[l], w_in[l], q_norm_g[l], k_norm_g[l], w_pool[l], pool_scale[l],
              w_o[l], norm2_g[l], w_pq[l], sub_keys[l], expert_u[l], expert_v[l])
        prefix = jnp.zeros((yp.shape[0], POOL_STATE, POOL_W), yp.dtype)
        yp, k1, v1, ik1, p1 = trunk_layer(yp, 0, prefix, dsa_prompt, *lw)
        attend_s = functools.partial(dsa_sample, cache_k=cache_k[l], cache_v=cache_v[l],
                                     cache_ik=cache_ik[l], page_table=page_table)
        ys, k2, v2, ik2, p2 = trunk_layer(ys, past, state_pool[l], attend_s, *lw)
        kp.append(k1); vp.append(v1); ikp.append(ik1); pp.append(p1)
        kd.append(k2); vd.append(v2); ikd.append(ik2); pd.append(p2)
    return (yp, ys, jnp.stack(kp), jnp.stack(vp), jnp.stack(ikp), jnp.stack(pp),
            jnp.stack(kd), jnp.stack(vd), jnp.stack(ikd), jnp.stack(pd))


_drawn_inputs = setup_inputs


def setup_inputs(seed=0):
    import zlib

    import numpy as np

    out = dict(_drawn_inputs(seed))
    spreads = {}
    factors = {'q_norm_g': 5.968, 'norm2_g': 2.8}
    for name, (base, spread) in spreads.items():
        noise = np.random.default_rng([zlib.crc32(name.encode()), seed]).standard_normal(out[name].shape)
        drawn = base * np.exp(spread * noise) if base else spread * noise
        out[name] = __import__('jax').numpy.asarray(drawn.astype(out[name].dtype))
    for name, factor in factors.items():
        out[name] = (out[name] * factor).astype(out[name].dtype)
    return out
```

```python
from contextlib import ExitStack

import numpy as np

import concourse.bass as bass
from concourse import mybir

ALU = mybir.AluOpType
ACT = mybir.ActivationFunctionType
AX = mybir.AxisListType.X
F32 = mybir.dt.float32
F32R = mybir.dt.float32r
BF16 = mybir.dt.bfloat16
I32 = mybir.dt.int32
U32 = mybir.dt.uint32
P = 128
BANK = 512
EPS = 1e-6
THETA = 10000.0
NEG = -1e30
TAKEN = -3e38
WINDOWS = (2, 4, 8, 16)


def shape_constants(SEQ, DB, DS, PAST, NH, HD, IH, ID, NST):
    NT = SEQ + DB * DS
    pos = np.concatenate([np.arange(SEQ), np.tile(PAST + np.arange(DS), DB)]).astype(np.float32)
    tabs = []
    for dim in (HD, ID):
        half = dim // 2
        inv = (np.float32(THETA) ** (-np.arange(half, dtype=np.float32) / np.float32(half))).astype(np.float32)
        ang = pos[:, None] * inv[None, :]
        tabs += [np.cos(ang), np.sin(ang)]
    rope = np.concatenate(tabs, axis=1).astype(np.float32)
    NW = len(WINDOWS)
    band = np.zeros((SEQ, NW, SEQ), np.float32)
    band_state = np.zeros((DB * NST, NW, DB * DS), np.float32)
    band_new = np.zeros((DB * DS, NW, DB * DS), np.float32)
    for g, w in enumerate(WINDOWS):
        for t in range(SEQ):
            lo = max(0, t + 1 - w)
            band[lo:t + 1, g, t] = 1.0 / min(t + 1, w)
            band[t, g, t] -= 1.0
        for b in range(DB):
            for s in range(DS):
                for r in range(NST + s + 1 - w, NST + s + 1):
                    if r < NST:
                        band_state[b * NST + r, g, b * DS + s] = 1.0 / w
                    else:
                        band_new[b * DS + r - NST, g, b * DS + s] = 1.0 / w
                band_new[b * DS + s, g, b * DS + s] -= 1.0
    causal = np.where(np.arange(SEQ)[None, :] <= np.arange(SEQ)[:, None], 0.0, NEG).astype(np.float32)
    causal_new = np.where(np.arange(DS)[None, :] <= (np.arange(DB * DS) % DS)[:, None], 0.0, NEG).astype(np.float32)
    fold = np.zeros((DB * DS, DB // 4, P), np.float32)
    own = np.zeros((P, DB // 4, DB), np.float32)
    for g in range(DB // 4):
        for j in range(4):
            for h in range(IH):
                for s in range(DS):
                    row = 32 * j + h * DS + s
                    fold[(4 * g + j) * DS + s, g, row] = 1.0
                    own[row, g, 4 * g + j] = 1.0
    iota = np.tile(np.arange(P, dtype=np.float32)[None], (P, 1))
    return dict(c_rope=rope, c_band=band, c_band_state=band_state, c_band_new=band_new, c_causal=causal,
                c_causal_new=causal_new, c_fold=fold, c_own=own, c_ident=np.eye(P, dtype=np.float32), c_iota=iota)


class Named(dict):

    def __init__(self, nc, ctx):
        self.nc, self.ctx = nc, ctx

    def __missing__(self, name):
        self[name] = self.ctx.enter_context(self.nc.semaphore(name))
        return self[name]


def hybrid_kernel(nc, x_prompt, x_sample, cache_k, cache_v, cache_ik, state_pool, page_table,
                  norm1_g, w_in, q_norm_g, k_norm_g, w_pool, pool_scale, w_o, norm2_g, w_pq, sub_keys,
                  expert_u, expert_v, c_rope, c_band, c_band_state, c_band_new, c_causal, c_causal_new,
                  c_fold, c_own, c_ident, c_iota,
                  y_prompt, y_sample, k_prompt, v_prompt, ik_prompt, pool_prompt,
                  k_sample, v_sample, ik_sample, pool_sample):
    SEQ, D = x_prompt.shape[1:]
    DB, DS = x_sample.shape[:2]
    HD, ID = cache_k.shape[3], cache_ik.shape[3]
    PAGE = cache_k.shape[2]
    NPOOL = cache_k.shape[1]
    NPG = page_table.shape[1]
    PAST = NPG * PAGE
    NST, PW = state_pool.shape[2:]
    NG = w_pool.shape[1]
    NH = (D - PW) // HD
    RH = sub_keys.shape[1]
    NK = sub_keys.shape[3]
    IN_W = w_in.shape[2]
    IH = (IN_W - PW - NH * HD - 2 * HD - ID) // (ID + 1)
    TK = 16
    KC = D // P
    NS = DB * DS
    NT = SEQ + NS
    TILES = ((0, P), (P, P), (SEQ, NS))
    KEYS = PAST + DS
    KSEL_P = min(256, SEQ // 4)
    KSEL_S = min(256, KEYS // 4)
    SC = float(HD) ** -0.5
    RSLOTS = 2 * RH
    O_Q, O_K = PW, PW + NH * HD
    O_V = O_K + HD
    O_IQ = O_V + HD
    O_IK = O_IQ + IH * ID
    O_IW = O_IK + ID
    assert SEQ == 2 * P and NS == 32 and D == 8 * P and PAGE == P and HD == P and NK == P and NG == 4
    assert DS == 4 and DB == 8 and IH == 8 and ID == 64 and NH == 4 and RH == 8 and NPG == 8

    ctx = ExitStack()
    psum = ctx.enter_context(nc.psum_tensor("psum", [P, 8, BANK], F32))

    base = (nc.sbuf_base + 63) // 64 * 64
    WORDS = (nc.sbuf_usable_end // 4) - base // 4 - 8
    high = [0]

    def at(name, off, shape, dt=F32):
        n = int(np.prod(shape[1:])) * (2 if dt == BF16 else 4)
        assert off * 4 + n <= WORDS * 4, (name, off, n, WORDS)
        high[0] = max(high[0], off * 4 + n)
        return nc.alloc_sbuf_tensor_at(name, shape, dt, offset=base + off * 4)

    cur = [0]

    def take(name, shape, dt=F32):
        n = (int(np.prod(shape[1:])) * (2 if dt == BF16 else 4) + 31) // 32 * 8
        t = at(name, cur[0], shape, dt)
        cur[0] += n
        return t

    ident = take("ident", [P, P])
    iota = take("iota", [P, P])
    ones = take("ones", [P, P])
    xT = take("xT", [P, KC, NT])
    gains = take("gains", [P, 2 * KC + NG])
    iT = take("iT", [P, NT])
    jT = take("jT", [P, NT])
    gT = take("gT", [P, NT, 2], F32R)
    small = take("small", [P, 64])
    top8 = take("top8", [P, 8])
    F0 = cur[0]

    w_in_sb = take("w_in_sb", [P, KC, IN_W])
    W0 = F0
    cur[0] = W0 + 2 * KC * D
    v_cache = at("v_cache", W0, [P, DB, NPG, HD])
    k_cache = at("k_cache", W0 + KC * D, [P, DB, NPG, HD])
    w_o_sb = at("w_o_sb", W0 + KC * D, [P, KC, D])
    w_pq_lo = at("w_pq_lo", W0, [P, KC, D])
    w_pq_hi = at("w_pq_hi", W0 + KC * D, [P, KC, D])
    Z0 = cur[0]
    z = take("z", [P, 3, IN_W])
    A0 = cur[0]
    x_nat = at("x_nat", A0, [P, 3, D])
    ik_cache = at("ik_cache", A0, [P, DB, NPG, ID])
    keysT = at("keysT", A0, [P, RSLOTS, NK])
    keys_nat = at("keys_nat", A0 + RSLOTS * NK, [P, RSLOTS, HD])
    cur[0] = A0 + 4096
    A1 = cur[0]
    sq = at("sq", A1, [P, KC, NT])
    iqT = at("iqT", A1, [64, IH + 1, SEQ])
    log_s = at("log_s", A1, [P, 2, KEYS])
    cur[0] = A1 + 2304
    hT = take("hT", [P, KC, NT])
    catT = at("catT", cur[0] - KC * NT, [P, KC, NT])
    A3 = cur[0]
    ikT = take("ikT", [64, 2, KEYS])
    kT_s = at("kT_s", A3, [P, 2, KEYS])
    idx_tmp = at("idx_tmp", A3, [P, 4, (IH + 1) * ID // 2])
    sq2 = at("sq2", A3, [P, KC, NT])
    A4 = cur[0]
    dT = at("dT", A4, [P, NG, NT])
    rel_s = take("rel_s", [P, 2, KEYS])
    band = at("band", cur[0], [P, 2, NG, SEQ])
    score_s = take("score_s", [NS, KEYS])
    work_s = take("work_s", [NS, KEYS])
    A6 = cur[0]
    rel_p = take("rel_p", [P, IH, SEQ])
    A7 = cur[0]
    score_p = take("score_p", [P, SEQ])
    work_p = take("work_p", [P, SEQ])
    bias_p = take("bias_p", [P, 2, SEQ])
    prob_p = take("prob_p", [P, NH, SEQ])
    probT = take("probT", [P, NPG, P])
    rope_tmp = at("rope_tmp", A7, [P, 4, (NH + 1) * HD // 2])
    head_sq = at("head_sq", A7 + 2 * (NH + 1) * HD, [P, NH + 1, HD])
    A8 = cur[0]
    qkT = take("qkT", [P, NH + 1, NT])
    q_s = take("q_s", [P, DB, 8, DS])
    iq_s = take("iq_s", [64, DB, IH, DS])
    ik_new = take("ik_new", [64, NS])
    gain5 = take("gain5", [P, NH + 1, HD])
    band_state = take("band_state", [DB * NST, NG, NS])
    band_new = take("band_new", [NS, NG, NS])
    w_pool_sb = at("w_pool_sb", A6, [P, NG, P])
    state_sb = at("state_sb", A6 + NG * P, [DB * NST, PW])
    rope = take("rope", [P, 3, HD + ID])
    causal = take("causal", [P, 2, SEQ])
    causal_new = take("causal_new", [NS, DS])
    fold = take("fold", [NS, 2, P])
    own = take("own", [P, 2, DB])
    fold_iw = take("fold_iw", [NS, 2, P])
    w_fold = take("w_fold", [P, 2, NS])
    pnew = take("pnew", [P, NS])
    pnewT = take("pnewT", [NS, P])
    rstd_a = take("rstd_a", [P, NT])
    rstd_b = take("rstd_b", [P, NT])
    gain_rows = take("gain_rows", [2 * KC + NG, P])
    head_gain = take("head_gain", [1, 2, HD])
    pages = take("pages", [1, DB * NPG], I32)
    iw = take("iw", [P, 3, IH])

    cur[0] = A1 + 2304
    sr = at("sr", Z0, [P, 2, RSLOTS, NK])
    cur[0] = A3
    assert Z0 + 2 * RSLOTS * NK <= A0
    q_ring = take("q_ring", [P, 2, NT])
    sr_s = take("sr_s", [P, 4, NK])
    rwork = take("rwork", [P, 4, NK])
    sv = take("sv", [P, RH, 2, TK])
    si = take("si", [P, RH, 2, TK], U32)
    sib = take("sib", [P, RH, 2, TK], BF16)
    cand = take("cand", [P, RH, TK, TK])
    fv = take("fv", [P, RH, TK])
    fi = take("fi", [P, RH, TK], U32)
    fab = take("fab", [P, 2, RH, TK], U32)
    fabb = take("fabb", [P, 2, RH, TK], BF16)
    hit = take("hit", [P, RH, TK, TK], BF16)
    picked = take("picked", [P, RH, TK, TK], BF16)
    iotab = take("iotab", [P, TK], BF16)
    slots = take("slots", [P, 3, RH, TK])
    ssum = take("ssum", [P, RH])
    h2 = at("h2", A1, [P, KC, NT])
    ROUTE_END = cur[0]

    cur[0] = F0
    u_raw = take("u_raw", [P, 4, D])
    v_raw = take("v_raw", [P, 4, D])
    g_ring = take("g_ring", [P, 64, NT])
    uT_hi = take("uT_hi", [P, 2, KC, P], F32R)
    uT_lo = take("uT_lo", [P, 2, KC, P], F32R)
    v_hi = take("v_hi", [P, 2, D], F32R)
    v_lo = take("v_lo", [P, 2, D], F32R)
    NB = NT // 32
    j_hot = take("j_hot", [P, 2, NB, P], F32R)
    i_eq = take("i_eq", [P, 2, NB, 32])
    i_hot = take("i_hot", [P, 2, NB, 2, 32], F32R)
    act_g = take("act_g", [P, 2, NT])
    ag = take("ag", [P, 2, NT])
    ag_hi = take("ag_hi", [P, 2, NT], F32R)
    ag_lo = take("ag_lo", [P, 2, NT], F32R)
    MAIN_END = cur[0]
    assert ROUTE_END <= MAIN_END, (ROUTE_END, MAIN_END)
    h_hi = take("h_hi", [P, KC, NT], F32R)
    h_lo = take("h_lo", [P, KC, NT], F32R)
    yT = at("yT", F0 + 8 * D, [P, KC, NT])
    y_nat = at("y_nat", F0 + 8 * D + KC * NT, [P, 3, D])

    S = Named(nc, ctx)
    u_in = [ctx.enter_context(nc.semaphore(f"u_in{i}")) for i in range(4)]
    v_tile_in = [ctx.enter_context(nc.semaphore(f"v_tile_in{i}")) for i in range(4)]

    def bc(ap, axis, n):
        a = ap.unsqueeze(axis)
        shape = list(a.shape)
        shape[axis] = n
        return a.to_broadcast(shape)

    def flat(ap):
        return ap.rearrange("p a b -> p (a b)")

    NU = NK
    PH, QUADS = 32, 8
    u_rows = expert_u.rearrange("a (n p) d -> (a n) p d", p=P)
    v_rows = expert_v.rearrange("a (n p) d -> (a n) p d", p=P)
    Y = [(0, 0, 288, 0, 0), (1, 0, 224, 0, 288), (1, 224, 64, 1, 0), (2, 0, 288, 1, 64), (3, 0, 160, 1, 352),
         (3, 160, 128, 2, 0), (4, 0, 288, 2, 128), (5, 0, 96, 2, 416), (5, 96, 192, 3, 0), (6, 0, 288, 3, 192),
         (7, 0, 288, 4, 0)]
    Y_FIRST = {0: 0, 1: 2, 2: 5, 3: 8, 4: 10}

    const_loads = [
        (ident[:], c_ident), (iota[:], c_iota),
        (gain_rows[0:KC, :], norm1_g.rearrange("a (k p) -> (a k) p", p=P)),
        (gain_rows[KC:2 * KC, :], norm2_g.rearrange("a (k p) -> (a k) p", p=P)),
        (gain_rows[2 * KC:2 * KC + NG, :], pool_scale.rearrange("a (k p) -> (a k) p", p=P)),
        (head_gain[0:1, 0, :], q_norm_g), (head_gain[0:1, 1, :], k_norm_g),
        (rope[:, 0:2, :], c_rope[0:SEQ, :].rearrange("(t p) c -> p t c", p=P)), (rope[0:NS, 2, :], c_rope[SEQ:NT, :]),
        (causal[:], c_causal.rearrange("(t p) c -> p t c", p=P)), (causal_new[:], c_causal_new),
        (fold[:], c_fold), (own[:], c_own), (pages[0:1, :], page_table.rearrange("b n -> (b n)").unsqueeze(0)),
        (band[:, 0], c_band[0:P]), (band[:, 1], c_band[P:SEQ]), (band_state[:], c_band_state),
        (band_new[:], c_band_new), (w_pool_sb[:], w_pool[0].rearrange("g c n -> c g n")),
        (state_sb[:], state_pool[0].rearrange("b r d -> (b r) d")),
    ]

    def phases(eng, quad, before_last):
        last = NU // PH - 1
        for ph in range(last + 1):
            q0, q1 = ph * QUADS, (ph + 1) * QUADS
            if ph == last and before_last:
                before_last()
            if ph == 0:
                quad(q0, ph, start=True)
                q0 += 1
            if ph == last:
                q1 -= 1
            with eng.Fori(q0, q1) as q:
                quad(q, ph)
            if ph == last:
                quad(q1, ph, stop=True)

    def rs_copy(act, copy, q4):
        act.wait_ge(S["rs_psum"], 4 * q4 + 4)
        for t in range(2):
            a = copy(sr[:, t, 4 * q4:4 * q4 + 4, :].rearrange("p a b -> p (a b)"), psum[:, 4 + t, :])
        if q4 == 3:
            a = copy(sr_s[:].rearrange("p a b -> p (a b)"), psum[:, 6, :])
        a.then_inc(S["rs_copied"], 1)

    def slots_low(dve, t):
        dve.wait_ge(S["slots_hi"], t + 1)
        if t < 2:
            cols = slice(t * P, (t + 1) * P)
            ins = dve.tensor_tensor(gT[:, cols, 1], psum[:, 7, 2 * P:3 * P], gT[:, cols, 0].bitcast(F32),
                                    ALU.subtract)
        else:
            for j in range(4):
                rows = slice(32 * j, 32 * j + 32)
                ins = dve.tensor_tensor(gT[rows, SEQ:NT, 1], psum[0:32, 7, 2 * P + 32 * j:2 * P + 32 * j + 32],
                                        gT[rows, SEQ:NT, 0].bitcast(F32), ALU.subtract)
        ins.then_inc(S["slots_lo"], 1)

    with nc.Block() as block:
        @block.sync
        def _(sp):
            for t, (t0, n) in enumerate(TILES):
                src = x_prompt[0, t0:t0 + n, :] if t < 2 else x_sample.rearrange("b s d -> (b s) d")
                sp.dma_start(x_nat[0:n, t, :], src).then_inc(S["x_in"], 16)
            for dst, src in const_loads:
                sp.dma_start(dst, src).then_inc(S["consts_in"], 16)
            for k in range(KC):
                sp.dma_start(w_in_sb[:, k, :], w_in[0, k * P:(k + 1) * P, :]).then_inc(S["w_in_in"], 16)
            sp.dma_start(pool_sample[0, :, 0:NST - DS, :], state_pool[0, :, DS:NST, :]).then_inc(S["out_done"], 16)

            def page_loads(cache, dst, width, sem):
                with sp.Fori(0, DB * NPG) as i:
                    pg = sp.value_load(pages[0:1, bass.ds(i, 1)], min_val=0, max_val=NPOOL - 1)
                    sp.dma_start(dst[:, bass.ds(i * width, width)],
                                 cache[0, bass.ds(pg, 1), :, :].rearrange("a p d -> (a p) d")).then_inc(sem, 16)

            sp.wait_ge(S["consts_in"], 16 * len(const_loads))
            sp.wait_ge(S["xT_psum"], KC)
            page_loads(cache_ik, ik_cache[:].rearrange("p b n d -> p (b n d)"), ID, S["ik_in"])
            sp.wait_ge(S["z_done"], 3)
            page_loads(cache_k, k_cache[:].rearrange("p b n d -> p (b n d)"), HD, S["k_in"])
            page_loads(cache_v, v_cache[:].rearrange("p b n d -> p (b n d)"), HD, S["v_in"])
            sp.wait_ge(S["rope_done"], 3)
            sp.wait_ge(S["idx_rope_done"], 3)
            for outs, col, w in ((( k_prompt, k_sample), O_K, HD), ((v_prompt, v_sample), O_V, HD),
                                 ((ik_prompt, ik_sample), O_IK, ID)):
                for t, (t0, n) in enumerate(TILES):
                    dst = outs[0][0, 0, t0:t0 + n, :] if t < 2 else outs[1][0].rearrange("b s d -> (b s) d")
                    sp.dma_start(dst, z[0:n, t, col:col + w]).then_inc(S["rows_out"], 16)
            sp.dma_start(pool_prompt[0, 0], z[P - NST:P, 1, 0:PW]).then_inc(S["rows_out"], 16)
            for b in range(DB):
                sp.dma_start(pool_sample[0, b, NST - DS:NST, :], z[b * DS:(b + 1) * DS, 2, 0:PW]
                             ).then_inc(S["rows_out"], 16)
            sp.wait_ge(S["idx_s_psum"], 2)
            sp.wait_ge(S["ikT_psum"], DB)
            sp.dma_start(keys_nat[:], sub_keys[0].rearrange("h c k d -> k (h c) d")).then_inc(S["keys_in"], 16)
            sp.wait_ge(S["kT_psum"], DB)
            for k in range(KC):
                sp.dma_start(w_o_sb[:, k, :], w_o[0, k * P:(k + 1) * P, :]).then_inc(S["w_o_in"], 16)
            sp.wait_ge(S["ys_psum"], 2)
            for k in range(KC):
                sp.dma_start(w_pq_lo[:, k, :], w_pq[0, k * P:(k + 1) * P, 0:D]).then_inc(S["w_pq_lo_in"], 16)
            sp.wait_ge(S["wo_psum"], KC)
            for k in range(KC):
                sp.dma_start(w_pq_hi[:, k, :], w_pq[0, k * P:(k + 1) * P, D:2 * D]).then_inc(S["w_pq_hi_in"], 16)

            def load_tile(row, slot):
                sp.dma_start(u_raw[:, slot, :], u_rows[bass.ds(row, 1)].rearrange("a p d -> (a p) d")
                             ).then_inc(u_in[slot], 16)
                sp.dma_start(v_raw[:, slot, :], v_rows[bass.ds(row, 1)].rearrange("a p d -> (a p) d")
                             ).then_inc(v_tile_in[slot], 16)

            sp.wait_ge(S["rq_psum"], RSLOTS)
            for s in range(4):
                load_tile(s, s)
            with sp.Fori(1, NU // 4) as q:
                for s in range(4):
                    sp.wait_ge(S["tr_done"], 4 * q + (s - 3))
                    sp.wait_ge(S["v_lo_ready"], 4 * q + (s - 3))
                    load_tile(4 * q + s, s)

            sp.wait_ge(S["yn_copied"], 3)
            for t, (t0, n) in enumerate(TILES):
                dst = y_prompt[0, t0:t0 + n, :] if t < 2 else y_sample.rearrange("b s d -> (b s) d")
                sp.dma_start(dst, y_nat[0:n, t, :]).then_inc(S["out_done"], 16)
            sp.wait_ge(S["out_done"], 16 * 4)

        @block.tensor
        def _(pe):
            def tr(out, in_):
                n = in_.shape[0]
                return pe.transpose(out, in_, ident[0:n, 0:n])

            pe.wait_ge(S["x_in"], 48)
            pe.wait_ge(S["consts_in"], 16 * len(const_loads))
            for c in range(KC):
                if c >= 4:
                    pe.wait_ge(S["sq_ready"], c - 3)
                for t, (t0, n) in enumerate(TILES):
                    mm = tr(psum[:, c % 4, t0:t0 + n], x_nat[0:n, t, c * P:(c + 1) * P])
                mm.then_inc(S["xT_psum"], 1)
            tr(psum[:, 5, 0:2 * KC + NG], gain_rows[:, :])
            pe.wait_ge(S["ones_set"], 1)
            pe.matmul(psum[:, 6, 0:2 * HD], ones[0:1, :], head_gain[0:1, :, :].rearrange("p a b -> p (a b)"),
                      start=True, stop=True).then_inc(S["gains_psum"], 1)
            for c in range(KC):
                pe.wait_ge(S["sq_ready"], c + 1)
                mm = pe.matmul(psum[:, 4, 0:NT], ones[:, :], sq[:, c, :], start=(c == 0), stop=(c == KC - 1))
            mm.then_inc(S["ssq_done"], 1)
            pe.wait_ge(S["gains_copied"], 1)
            for t, (t0, n) in enumerate(TILES):
                bank0 = 4 * (t % 2)
                if t == 2:
                    pe.wait_ge(S["z_copied"], 1)
                for k in range(KC):
                    if t == 0:
                        pe.wait_ge(S["hT_ready"], k + 1)
                        if k == 0:
                            pe.wait_ge(S["w_in_in"], 16 * KC)
                    for j in range(4):
                        w = min(BANK, IN_W - BANK * j)
                        mm = pe.matmul(psum[0:n, bank0 + j, 0:w], hT[:, k, t0:t0 + n],
                                       w_in_sb[:, k, BANK * j:BANK * j + w], start=(k == 0), stop=(k == KC - 1))
                mm.then_inc(S["z_done"], 1)
            pe.wait_ge(S["z_copied"], 2)
            for t, (t0, n) in enumerate(TILES):
                pe.wait_ge(S["rope_done"], t + 1)
                pe.wait_ge(S["idx_rope_done"], t + 1)
                if t:
                    pe.wait_ge(S["heads_copied"], t)
                for h in range(NH):
                    tr(psum[:, 4, h * n:(h + 1) * n], z[0:n, t, O_Q + h * HD:O_Q + (h + 1) * HD])
                tr(psum[:, 5, 0:n], z[0:n, t, O_K:O_K + HD])
                tr(psum[0:ID, 5, n:2 * n], z[0:n, t, O_IK:O_IK + ID])
                for h in range(IH):
                    mm = tr(psum[0:ID, 6 + h // 4, (h % 4) * n:(h % 4 + 1) * n],
                            z[0:n, t, O_IQ + h * ID:O_IQ + (h + 1) * ID])
                mm.then_inc(S["heads_psum"], 1)
            pe.wait_ge(S["heads_copied"], 3)
            for g in range(NG):
                cols = slice(g * P, (g + 1) * P)
                pe.matmul(psum[:, 4 + g, 0:SEQ], z[:, 0, cols], band[:, 0, g, :], start=True, stop=False)
                pe.matmul(psum[:, 4 + g, 0:SEQ], z[:, 1, cols], band[:, 1, g, :], start=False, stop=True)
                pe.matmul(psum[:, 4 + g, SEQ:NT], state_sb[:, cols], band_state[:, g, :], start=True, stop=False)
                mm = pe.matmul(psum[:, 4 + g, SEQ:NT], z[0:NS, 2, cols], band_new[:, g, :], start=False, stop=True)
                mm.then_inc(S["pool_d_psum"], 1)
            for g in range(NG):
                pe.wait_ge(S["pool_d_copied"], g + 1)
                pe.matmul(psum[:, 4 + g, 0:NT], w_pool_sb[:, g, :], dT[:, g, :], start=True, stop=True
                          ).then_inc(S["pool_y_psum"], 1)
            pe.wait_ge(S["z_copied"], 3)
            for t in range(2):
                if t:
                    pe.wait_ge(S["idx_relu"], 1)
                for h in range(IH):
                    mm = pe.matmul(psum[:, h // 2, (h % 2) * SEQ:(h % 2 + 1) * SEQ], iqT[:, h, t * P:(t + 1) * P],
                                   iqT[:, IH, :], start=True, stop=True)
                mm.then_inc(S["idx_psum"], 1)
            pe.wait_ge(S["pool_y_copied"], NG)
            pe.wait_ge(S["ik_in"], 16 * DB * NPG)
            pe.wait_ge(S["idx_relu"], 2)

            def scores_s(b, q, keys, done):
                rows = slice(32 * (b % 4), 32 * (b % 4) + 32)
                for lo, w, bank in ((0, BANK, 0), (BANK, BANK, 1), (PAST, DS, 2)):
                    mm = pe.matmul(psum[rows, bank, 0:w], q, keys[:, lo:lo + w], start=True, stop=True,
                                   skip_group_check=True, tile_position=(0, rows.start))
                return mm

            def step_idx(b):
                if b >= 2:
                    pe.wait_ge(S["ikT_copied"], b - 1)
                for n in range(NPG):
                    mm = tr(psum[0:ID, 4 + 2 * (b % 2) + n // 4, (n % 4) * P:(n % 4 + 1) * P], ik_cache[:, b, n, :])
                mm.then_inc(S["ikT_psum"], 1)

            step_idx(0)
            for b in range(DB):
                if b + 1 < DB:
                    step_idx(b + 1)
                pe.wait_ge(S["ikT_copied"], b + 1)
                if b == 4:
                    pe.wait_ge(S["idx_s_relu"], 1)
                mm = scores_s(b, iq_s[:, b].rearrange("p h s -> p (h s)"), ikT[:, b % 2, :], None)
                if b % 4 == 3:
                    mm.then_inc(S["idx_s_psum"], 1)
            pe.wait_ge(S["fold_iw_ready"], 2)
            for g in range(2):
                mm = tr(psum[:, 3, g * NS:(g + 1) * NS], fold_iw[:, g, :])
            mm.then_inc(S["w_fold_psum"], 1)
            pe.wait_ge(S["w_fold_copied"], 1)
            pe.wait_ge(S["idx_s_relu"], 2)
            for lo, w, bank in ((0, BANK, 0), (BANK, BANK, 1), (PAST, DS, 2)):
                for g in range(2):
                    mm = pe.matmul(psum[0:NS, bank, 0:w], w_fold[:, g, :], rel_s[:, g, lo:lo + w],
                                   start=(g == 0), stop=(g == 1))
            mm.then_inc(S["score_s_psum"], 1)
            def step_k(b):
                if b == 0:
                    pe.wait_ge(S["k_in"], 16 * DB * NPG)
                if b >= 2:
                    pe.wait_ge(S["kT_copied"], b - 1)
                for n in range(NPG):
                    mm = tr(psum[:, 4 + 2 * (b % 2) + n // 4, (n % 4) * P:(n % 4 + 1) * P], k_cache[:, b, n, :])
                mm.then_inc(S["kT_psum"], 1)

            pe.wait_ge(S["score_s_copied"], 1)
            step_k(0)
            for b in range(DB):
                if b + 1 < DB:
                    step_k(b + 1)
                pe.wait_ge(S["kT_copied"], b + 1)
                if b == 4:
                    pe.wait_ge(S["log_s_copied"], 1)
                mm = scores_s(b, q_s[:, b].rearrange("p h s -> p (h s)"), kT_s[:, b % 2, :], None)
                if b % 4 == 3:
                    mm.then_inc(S["log_s_psum"], 1)
            pe.wait_ge(S["log_s_copied"], 2)
            pe.wait_ge(S["keys_in"], 16)
            for r in range(RSLOTS):
                if r % 4 == 0 and r == 0:
                    pe.wait_ge(S["kT_copied"], DB)
                mm = tr(psum[:, 4 + r // 4, (r % 4) * P:(r % 4 + 1) * P], keys_nat[:, r, :])
                if r % 4 == 3:
                    mm.then_inc(S["keysT_psum"], 1)
            pe.wait_ge(S["keysT_copied"], 4)
            for t in range(2):
                pe.wait_ge(S["bias_p_ready"], t + 1)
                if t:
                    pe.wait_ge(S["p_exp"], 1)
                for h in range(NH):
                    out = psum[:, h // 2, (h % 2) * SEQ:(h % 2 + 1) * SEQ]
                    pe.matmul(out, qkT[:, h, t * P:(t + 1) * P], qkT[:, NH, 0:SEQ], start=True, stop=False)
                    mm = pe.matmul(out, ident[:, :], bias_p[:, t, :], start=False, stop=True)
                mm.then_inc(S["log_p_psum"], 1)
                pe.wait_ge(S["p_norm"], t + 1)
                for h in range(NH):
                    for kt in range(2):
                        mm = tr(psum[:, 4 + kt, h * P:(h + 1) * P], prob_p[:, h, kt * P:(kt + 1) * P])
                mm.then_inc(S["pT_psum"], 1)
                pe.wait_ge(S["pT_copied"], t + 1)
                if t:
                    pe.wait_ge(S["yb_copied"], 1)
                for h in range(NH):
                    for kt in range(2):
                        mm = pe.matmul(psum[:, 6, h * P:(h + 1) * P], z[:, kt, O_V:O_V + HD],
                                       probT[:, kt * NH + h, :], start=(kt == 0), stop=(kt == 1))
                mm.then_inc(S["yb_psum"], 1)
            pe.wait_ge(S["p_exp"], 2)
            pe.wait_ge(S["yb_copied"], 2)
            for g in range(2):
                pe.wait_ge(S["bias_s_ready"], 1)
                if g:
                    pe.wait_ge(S["s_max"], 1)
                for lo, w, bank in ((0, BANK, 0), (BANK, BANK, 1), (PAST, DS, 2)):
                    mm = pe.matmul(psum[:, bank, 0:w], fold[:, g, :], score_s[:, lo:lo + w], start=True, stop=True)
                mm.then_inc(S["spread_psum"], 1)
                pe.wait_ge(S["pnew_ready"], g + 1)
                if g:
                    pe.wait_ge(S["ys_psum"], 1)
                for n in range(NPG):
                    tr(psum[:, 4 + n // 4, (n % 4) * P:(n % 4 + 1) * P], log_s[:, g, n * P:(n + 1) * P])
                tr(psum[0:NS, 6, 0:P], pnew[:, :]).then_inc(S["sT_psum"], 1)
                pe.wait_ge(S["sT_copied"], g + 1)
                if g == 0:
                    pe.wait_ge(S["v_in"], 16 * DB * NPG)
                for j in range(4):
                    rows = slice(32 * j, 32 * j + NH * DS)
                    out = psum[:, 7, g * P + rows.start:g * P + rows.stop]
                    pe.matmul(out, z[0:NS, 2, O_V:O_V + HD], pnewT[:, rows], start=True, stop=False)
                    for n in range(NPG):
                        mm = pe.matmul(out, v_cache[:, 4 * g + j, n, :], probT[:, n, rows], start=False,
                                       stop=(n == NPG - 1))
                mm.then_inc(S["ys_psum"], 1)
            pe.wait_ge(S["w_o_in"], 16 * KC)
            pe.wait_ge(S["ys_copied"], 2)
            pe.wait_ge(S["s_max"], 2)
            for c in range(KC):
                if c >= 4:
                    pe.wait_ge(S["x1_ready"], c - 3)
                for k in range(KC):
                    mm = pe.matmul(psum[:, c % 4, 0:NT], w_o_sb[:, k, c * P:(c + 1) * P], catT[:, k, :],
                                   start=(k == 0), stop=(k == KC - 1))
                mm.then_inc(S["wo_psum"], 1)
            for c in range(KC):
                pe.wait_ge(S["sq2_ready"], c + 1)
                mm = pe.matmul(psum[:, 4, 0:NT], ones[:, :], sq2[:, c, :], start=(c == 0), stop=(c == KC - 1))
            mm.then_inc(S["ssq2_done"], 1)
            def rq(r):
                w = w_pq_lo if r < RSLOTS // 2 else w_pq_hi
                if r == 0:
                    pe.wait_ge(S["w_pq_lo_in"], 16 * KC)
                    pe.wait_ge(S["x1_ready"], KC)
                if r == RSLOTS // 2:
                    pe.wait_ge(S["w_pq_hi_in"], 16 * KC)
                if r >= 2:
                    pe.wait_ge(S["rq_copied"], r - 1)
                c = r % (RSLOTS // 2)
                for k in range(KC):
                    if r == 0:
                        pe.wait_ge(S["h2_ready"], k + 1)
                    mm = pe.matmul(psum[:, r % 2, 0:NT], w[:, k, c * P:(c + 1) * P], h2[:, k, :],
                                   start=(k == 0), stop=(k == KC - 1))
                mm.then_inc(S["rq_psum"], 1)

            def rs(r):
                pe.wait_ge(S["rq_copied"], r + 1)
                if r == 0:
                    pe.wait_ge(S["rstd2_half"], 1)
                q4 = r // 4
                if r % 4 == 0 and r >= 4:
                    pe.wait_ge(S["rs_copied"], q4)
                for t in range(2):
                    pe.matmul(psum[:, 4 + t, (r % 4) * NK:(r % 4 + 1) * NK], q_ring[:, r % 2, t * P:(t + 1) * P],
                              keysT[:, r, :], start=True, stop=True)
                mm = pe.matmul(psum[32 * q4:32 * q4 + 32, 6, (r % 4) * NK:(r % 4 + 1) * NK],
                               q_ring[:, r % 2, SEQ:NT], keysT[:, r, :], start=True, stop=True,
                               skip_group_check=True, tile_position=(0, 32 * q4))
                mm.then_inc(S["rs_psum"], 1)

            rq(0)
            for r in range(RSLOTS):
                if r + 1 < RSLOTS:
                    rq(r + 1)
                rs(r)
            for t in range(3):
                pe.wait_ge(S["slots_ready"], t + 1)
                if t:
                    pe.wait_ge(S["slots_lo"], t)
                m = P if t < 2 else 2 * TK
                for a in range(3):
                    mm = tr(psum[0:m, 7, a * P:(a + 1) * P],
                            slots[:, a].rearrange("p h k -> p (h k)")[:, 0:m])
                mm.then_inc(S["slots_psum"], 1)
            pe.wait_ge(S["slots_lo"], 3)
            pe.wait_ge(S["h_split_lo"], 1)

            def spread(slot, n, bank0):
                pe.wait_ge(S["j_ready"], n + 1)
                pe.wait_ge(S["i_ready"], n + 1)
                for b in range(NB):
                    mm = pe.matmul(psum[:, bank0 + b // 8, (b % 8) * 64:(b % 8) * 64 + 64], j_hot[:, slot, b, :],
                                   i_hot[:, slot, b].rearrange("p a i -> p (a i)"), start=True, stop=True,
                                   skip_group_check=True)
                mm.then_inc(S["g_psum"], 1)

            spread(0, 0, 0)
            spread(1, 1, 2)
            with pe.Fori(1, PH // 2) as m:
                for s in range(2):
                    pe.wait_ge(S["g_copied"], 2 * m + (s - 1))
                    spread(s, 2 * m + s, 2 * s)
            pe.wait_ge(S["g_copied"], PH)
            pe.wait_ge(S["h_split_lo"], 1)

            def transpose_u(slot, count):
                pe.wait_ge(u_in[slot], 16 * count)
                for c in range(KC):
                    mm = tr(psum[:, 6 + c // 4, (c % 4) * P:(c % 4 + 1) * P], u_raw[:, slot, c * P:(c + 1) * P])
                mm.then_inc(S["tr_done"], 1)

            def prod_u(slot, n, start):
                pe.wait_ge(S["uT_hi_ready"], n + 1)
                pe.wait_ge(S["uT_lo_ready"], n + 1)
                if not start:
                    pe.wait_ge(S["act_ready"], n)
                i = 0
                for c in range(KC):
                    for a, b in ((uT_hi, h_hi), (uT_hi, h_lo), (uT_lo, h_hi)):
                        mm = pe.matmul(psum[:, 5, 0:NT], a[:, slot % 2, c, :], b[:, c, :], start=(i == 0),
                                       stop=(i == 3 * KC - 1))
                        i += 1
                mm.then_inc(S["a_done"], 1)

            def prod_v(slot, n, start, stop):
                pe.wait_ge(S["v_hi_ready"], n + 1)
                pe.wait_ge(S["v_lo_ready"], n + 1)
                pe.wait_ge(S["ag_hi_ready"], n + 1)
                pe.wait_ge(S["ag_lo_ready"], n + 1)
                for pi, (c, t0, w, bank, col) in enumerate(Y):
                    for i, (a, b) in enumerate(((v_hi, ag_hi), (v_hi, ag_lo), (v_lo, ag_hi))):
                        mm = pe.matmul(psum[:, bank, col:col + w], a[:, slot % 2, c * P:(c + 1) * P],
                                       b[:, slot % 2, t0:t0 + w],
                                       start=(start and i == 0 and Y_FIRST[bank] == pi), stop=stop and i == 2,
                                       skip_group_check=True)
                mm.then_inc(S["v_mm_done"], 1)

            def quad(q, ph, start=False, stop=False):
                spreads = ph < NU // PH - 1
                for s in range(4):
                    n = 4 * q + s
                    if not (stop and s == 3):
                        if spreads:
                            pe.wait_ge(S["g_copied"], n + PH)
                        pe.wait_ge(S["uT_hi_ready"], n + 1)
                        pe.wait_ge(S["uT_lo_ready"], n + 1)
                        transpose_u((s + 1) % 4, q + 1 + (s + 1) // 4)
                    prod_u(s, n, start and s == 0)
                    if spreads:
                        pe.wait_ge(S["uT_hi_ready"], n + 2)
                        pe.wait_ge(S["uT_lo_ready"], n + 2)
                        spread(s % 2, n + PH, 6)
                    if not (start and s == 0):
                        prod_v((s + 3) % 4, n - 1, start and s == 1, False)

            transpose_u(0, 1)
            phases(pe, quad, lambda: pe.wait_ge(S["g_copied"], NU))
            prod_v(3, NU - 1, False, True)
            pe.wait_ge(S["yT_ready"], 1)
            for t, (t0, n) in enumerate(TILES):
                if t:
                    pe.wait_ge(S["yn_copied"], t)
                for c in range(KC):
                    mm = tr(psum[0:n, 6 + c // 4, (c % 4) * P:(c % 4 + 1) * P], yT[:, c, t0:t0 + n])
                mm.then_inc(S["yn_psum"], 1)

        @block.scalar
        def _(act):
            def copy(out, in_):
                return act.activation(out, in_, ACT.Copy)

            for c in range(KC):
                act.wait_ge(S["xT_psum"], c + 1)
                copy(xT[:, c, :], psum[:, c % 4, 0:NT])
                act.activation(sq[:, c, :], psum[:, c % 4, 0:NT], ACT.Square).then_inc(S["sq_ready"], 1)
            act.wait_ge(S["gains_psum"], 1)
            copy(gains[:, :], psum[:, 5, 0:2 * KC + NG])
            copy(gain5[:, 0:NH, :], bc(psum[:, 6, 0:HD], 1, NH))
            copy(gain5[:, NH, :], psum[:, 6, HD:2 * HD]).then_inc(S["gains_copied"], 1)
            act.wait_ge(S["rstd_half"], 1)
            act.activation(rstd_a[:, :], rstd_b[:, :], ACT.Sqrt).then_inc(S["rstd_root"], 1)
            for t, (t0, n) in enumerate(TILES):
                act.wait_ge(S["z_done"], t + 1)
                for j in range(4):
                    w = min(BANK, IN_W - BANK * j)
                    a = copy(z[0:n, t, BANK * j:BANK * j + w], psum[0:n, 4 * (t % 2) + j, 0:w])
                a.then_inc(S["z_copied"], 1)
                act.wait_ge(S["head_var"], t + 1)
                act.activation(small[0:n, 16:16 + NH + 1], small[0:n, 8:8 + NH + 1], ACT.Sqrt
                               ).then_inc(S["head_root"], 1)
            for t, (t0, n) in enumerate(TILES):
                act.wait_ge(S["heads_psum"], t + 1)
                q_ps = psum[:, 4, 0:NH * n].rearrange("p (h t) -> p h t", h=NH)
                iq_ps = psum[0:ID, 6:8, 0:4 * n].rearrange("p a (h t) -> p a h t", h=4)
                copy(qkT[:, NH, t0:t0 + n], psum[:, 5, 0:n])
                if t < 2:
                    copy(qkT[:, 0:NH, t0:t0 + n], q_ps)
                    for a in range(2):
                        copy(iqT[:, 4 * a:4 * a + 4, t0:t0 + n], iq_ps[:, a])
                    copy(iqT[:, IH, t0:t0 + n], psum[0:ID, 5, n:2 * n]).then_inc(S["heads_copied"], 1)
                else:
                    for h in range(NH):
                        for r in (h, h + NH):
                            copy(q_s[:, :, r, :], q_ps[:, h].rearrange("p (b s) -> p b s", b=DB))
                    for h in range(IH):
                        copy(iq_s[:, :, h, :], iq_ps[:, h // 4, h % 4].rearrange("p (b s) -> p b s", b=DB))
                    copy(ik_new[:, :], psum[0:ID, 5, n:2 * n]).then_inc(S["heads_copied"], 1)
            for g in range(NG):
                act.wait_ge(S["pool_d_psum"], g + 1)
                copy(dT[:, g, :], psum[:, 4 + g, 0:NT]).then_inc(S["pool_d_copied"], 1)
            for g in range(NG):
                act.wait_ge(S["pool_y_psum"], g + 1)
                act.activation(catT[:, g, :], psum[:, 4 + g, 0:NT], ACT.Copy,
                               scale=gains[:, 2 * KC + g:2 * KC + g + 1]).then_inc(S["pool_y_copied"], 1)
            for t in range(2):
                act.wait_ge(S["idx_psum"], t + 1)
                if t:
                    act.wait_ge(S["idx_summed"], 1)
                a = act.activation(rel_p[:].rearrange("p h k -> p (h k)"),
                                   psum[:, 0:4, :].rearrange("p a b -> p (a b)"), ACT.Relu)
                a.then_inc(S["idx_relu"], 1)
            for b in range(DB):
                act.wait_ge(S["ikT_psum"], b + 1)
                if b >= 4 and b % 4 == 2 or b == 2:
                    pass
                lo = 4 + 2 * (b % 2)
                copy(ikT[:, b % 2, 0:PAST], psum[0:ID, lo:lo + 2, :].rearrange("p a b -> p (a b)"))
                copy(ikT[:, b % 2, PAST:KEYS], ik_new[:, b * DS:(b + 1) * DS]).then_inc(S["ikT_copied"], 1)
                if b % 4 == 3:
                    g = b // 4
                    act.wait_ge(S["idx_s_psum"], g + 1)
                    act.activation(rel_s[:, g, 0:PAST], psum[:, 0:2, :].rearrange("p a b -> p (a b)"), ACT.Relu)
                    act.activation(rel_s[:, g, PAST:KEYS], psum[:, 2, 0:DS], ACT.Relu
                                   ).then_inc(S["idx_s_relu"], 1)
            act.wait_ge(S["w_fold_psum"], 1)
            copy(w_fold[:].rearrange("p a b -> p (a b)"), psum[:, 3, 0:2 * NS]).then_inc(S["w_fold_copied"], 1)
            act.wait_ge(S["score_s_psum"], 1)
            copy(score_s[:, 0:PAST], psum[0:NS, 0:2, :].rearrange("p a b -> p (a b)"))
            copy(score_s[:, PAST:KEYS], psum[0:NS, 2, 0:DS]).then_inc(S["score_s_copied"], 1)
            for b in range(DB):
                act.wait_ge(S["kT_psum"], b + 1)
                lo = 4 + 2 * (b % 2)
                copy(kT_s[:, b % 2, 0:PAST], psum[:, lo:lo + 2, :].rearrange("p a b -> p (a b)"))
                copy(kT_s[:, b % 2, PAST:KEYS], qkT[:, NH, SEQ + b * DS:SEQ + (b + 1) * DS]
                     ).then_inc(S["kT_copied"], 1)
                if b % 4 == 3:
                    g = b // 4
                    act.wait_ge(S["log_s_psum"], g + 1)
                    copy(log_s[:, g, 0:PAST], psum[:, 0:2, :].rearrange("p a b -> p (a b)"))
                    copy(log_s[:, g, PAST:KEYS], psum[:, 2, 0:DS]).then_inc(S["log_s_copied"], 1)
            for r in range(4):
                act.wait_ge(S["keysT_psum"], r + 1)
                copy(keysT[:, 4 * r:4 * r + 4, :].rearrange("p a b -> p (a b)"), psum[:, 4 + r, :]
                     ).then_inc(S["keysT_copied"], 1)
            for t in range(2):
                act.wait_ge(S["p_max"], t + 1)
                for h in range(NH):
                    a = act.activation(prob_p[:, h, :], psum[:, h // 2, (h % 2) * SEQ:(h % 2 + 1) * SEQ], ACT.Exp,
                                       bias=small[:, 28 + h:29 + h], scale=SC, accum_out=small[:, 32 + h:33 + h])
                a.then_inc(S["p_exp"], 1)
                act.wait_ge(S["pT_psum"], t + 1)
                copy(probT[:].rearrange("p a b -> p (a b)"), psum[:, 4:6, :].rearrange("p a b -> p (a b)")
                     ).then_inc(S["pT_copied"], 1)
                act.wait_ge(S["yb_psum"], t + 1)
                copy(catT[:, NG:NG + NH, t * P:(t + 1) * P], psum[:, 6, :].rearrange("p (h t) -> p h t", h=NH)
                     ).then_inc(S["yb_copied"], 1)
            for g in range(2):
                act.wait_ge(S["s_max"], g + 1)
                act.activation(log_s[:, g, :], log_s[:, g, :], ACT.Exp, bias=small[:, 41:42], scale=SC,
                               accum_out=small[:, 42:43]).then_inc(S["s_exp"], 1)
                act.wait_ge(S["sT_psum"], g + 1)
                if g:
                    act.wait_ge(S["ys_psum"], 1)
                copy(probT[:].rearrange("p a b -> p (a b)"), psum[:, 4:6, :].rearrange("p a b -> p (a b)"))
                copy(pnewT[:, :], psum[0:NS, 6, 0:P]).then_inc(S["sT_copied"], 1)
                act.wait_ge(S["ys_psum"], g + 1)
                ys = psum[:, 7, g * P:(g + 1) * P].rearrange("p (j h s) -> p j h s", j=4, s=DS)
                for h in range(NH):
                    c0 = SEQ + g * 4 * DS
                    a = copy(catT[:, NG + h, c0:c0 + 4 * DS].rearrange("p (j s) -> p j s", j=4), ys[:, :, h, :])
                a.then_inc(S["ys_copied"], 1)
            for c in range(KC):
                act.wait_ge(S["x1_ready"], c + 1)
                act.activation(sq2[:, c, :], xT[:, c, :], ACT.Square).then_inc(S["sq2_ready"], 1)
            act.wait_ge(S["rstd2_half"], 1)
            act.activation(rstd_a[:, :], rstd_b[:, :], ACT.Sqrt).then_inc(S["rstd2_root"], 1)
            act.wait_ge(S["rows_out"], 16 * (9 + 1 + DB))
            for r in range(RSLOTS):
                act.wait_ge(S["rq_psum"], r + 1)
                if r >= 2:
                    act.wait_ge(S["rs_psum"], r - 1)
                copy(q_ring[:, r % 2, :], psum[:, r % 2, 0:NT]).then_inc(S["rq_copied"], 1)
                if r % 4 == 0 and r:
                    rs_copy(act, copy, r // 4 - 1)
            rs_copy(act, copy, 3)
            act.wait_ge(S["h2_ready"], KC)
            copy(h_hi[:], h2[:]).then_inc(S["h_split"], 1)
            for t in range(3):
                act.wait_ge(S["rexp_in"], t + 1)
                H = RH if t < 2 else 2
                act.activation(slots[:, 2, 0:H], slots[:, 2, 0:H], ACT.Exp).then_inc(S["rexp_out"], 1)
                act.wait_ge(S["slots_psum"], t + 1)
                if t < 2:
                    cols = slice(t * P, (t + 1) * P)
                    copy(iT[:, cols], psum[:, 7, 0:P])
                    copy(jT[:, cols], psum[:, 7, P:2 * P])
                    copy(gT[:, cols, 0], psum[:, 7, 2 * P:3 * P]).then_inc(S["slots_hi"], 1)
                else:
                    for j in range(4):
                        rows, cols = slice(32 * j, 32 * j + 32), slice(SEQ, NT)
                        copy(iT[rows, cols], psum[0:32, 7, 32 * j:32 * j + 32])
                        copy(jT[rows, cols], psum[0:32, 7, P + 32 * j:P + 32 * j + 32])
                        a = copy(gT[rows, cols, 0], psum[0:32, 7, 2 * P + 32 * j:2 * P + 32 * j + 32])
                    a.then_inc(S["slots_hi"], 1)

            def high_u(slot, n, free):
                act.wait_ge(S["tr_done"], n + 1)
                if free:
                    act.wait_ge(S["a_done"], n - 1)
                copy(uT_hi[:, slot % 2].rearrange("p a b -> p (a b)"), psum[:, 6:8, :].rearrange("p a b -> p (a b)")
                     ).then_inc(S["uT_hi_ready"], 1)

            def quad(q, ph, start=False, stop=False):
                for s in range(4):
                    n = 4 * q + s
                    old = not (start and s < 2)
                    if not (stop and s == 3):
                        high_u(s + 1, n + 1, not (start and s == 0))
                    act.wait_ge(v_tile_in[s], 16 * (q + 1))
                    if old:
                        act.wait_ge(S["v_mm_done"], n - 1)
                    copy(v_hi[:, s % 2, :], v_raw[:, s, :]).then_inc(S["v_hi_ready"], 1)
                    act.wait_ge(S["a_done"], n + 1)
                    if old:
                        act.wait_ge(S["prod_ready"], n - 1)
                    act.activation(act_g[:, s % 2, :], psum[:, 5, 0:NT], ACT.Gelu).then_inc(S["act_ready"], 1)
                    act.wait_ge(S["prod_ready"], n + 1)
                    copy(ag_hi[:, s % 2, :], ag[:, s % 2, :]).then_inc(S["ag_hi_ready"], 1)

            high_u(0, 0, False)
            phases(act, quad, None)
            for t, (t0, n) in enumerate(TILES):
                act.wait_ge(S["yn_psum"], t + 1)
                copy(y_nat[0:n, t, :], psum[0:n, 6:8, :].rearrange("p a b -> p (a b)")).then_inc(S["yn_copied"], 1)

        @block.gpsimd
        def _(pool):
            steps = [0]

            def settle(ins):
                steps[0] += 1
                ins.then_inc(S["pool_step"], 1)
                pool.wait_ge(S["pool_step"], steps[0])

            pool.memset(ones[:, :], 1.0).then_inc(S["ones_set"], 1)
            for t, (t0, n) in enumerate(TILES):
                pool.wait_ge(S["z_copied"], t + 1)
                if t:
                    pool.wait_ge(S["idx_rope_done"], t)
                x = z[0:n, t, O_IQ:O_IW].rearrange("p (h a d) -> p h a d", a=2, d=ID // 2)
                cos = bc(rope[0:n, t, HD:HD + ID // 2], 1, IH + 1)
                sin = bc(rope[0:n, t, HD + ID // 2:HD + ID], 1, IH + 1)
                tmp = [idx_tmp[0:n, i, :].rearrange("p (h d) -> p h d", h=IH + 1) for i in range(4)]
                pool.tensor_tensor(tmp[0], x[:, :, 0], cos, ALU.mult)
                pool.tensor_tensor(tmp[1], x[:, :, 1], sin, ALU.mult)
                pool.tensor_tensor(tmp[2], x[:, :, 1], cos, ALU.mult)
                settle(pool.tensor_tensor(tmp[3], x[:, :, 0], sin, ALU.mult))
                pool.tensor_tensor(x[:, :, 0], tmp[0], tmp[1], ALU.subtract)
                pool.tensor_tensor(x[:, :, 1], tmp[2], tmp[3], ALU.add)
                pool.tensor_scalar(iw[0:n, t, :], z[0:n, t, O_IW:IN_W], float(IH) ** -0.5, None, ALU.mult
                                   ).then_inc(S["idx_rope_done"], 1)
            pool.wait_ge(S["idx_rope_done"], 3)
            for g in range(2):
                pool.tensor_tensor(fold_iw[:, g, :].rearrange("t (j h s) -> t j h s", j=4, s=DS),
                                   fold[:, g, :].rearrange("t (j h s) -> t j h s", j=4, s=DS),
                                   iw[0:NS, 2, :].unsqueeze(1).unsqueeze(3).to_broadcast([NS, 4, IH, DS]), ALU.mult
                                   ).then_inc(S["fold_iw_ready"], 1)
            pool.wait_ge(S["h_split"], 1)
            pool.tensor_tensor(h_lo[:], h2[:], h_hi[:].bitcast(F32), ALU.subtract).then_inc(S["h_split_lo"], 1)

            def place_weights(slot, n, token):
                pool.wait_ge(S["i_eq_ready"], n + 1)
                pool.tensor_tensor(i_hot[:, slot], bc(i_eq[:, slot], 2, 2),
                                   bc(gT[:, bass.ds(token, NB), :].bitcast(F32), 3, PH), ALU.mult
                                   ).then_inc(S["i_ready"], 1)

            pool.wait_ge(S["slots_lo"], 3)
            place_weights(0, 0, 0)
            place_weights(1, 1, NB)
            with pool.Fori(1, PH // 2) as m:
                for s in range(2):
                    pool.wait_ge(S["g_psum"], 2 * m + (s - 1))
                    place_weights(s, 2 * m + s, NB * (2 * m + s))

            def quad(q, ph, start=False, stop=False):
                for s in range(4):
                    n = 4 * q + s
                    if ph < NU // PH - 1:
                        pool.wait_ge(S["g_psum"], n + PH - 1)
                        place_weights(s % 2, n + PH, NB * (n - ph * PH))
                    pool.wait_ge(S["v_hi_ready"], n + 1)
                    pool.tensor_tensor(v_lo[:, s % 2, :], v_raw[:, s, :], v_hi[:, s % 2, :].bitcast(F32),
                                       ALU.subtract).then_inc(S["v_lo_ready"], 1)
                    pool.wait_ge(S["ag_hi_ready"], n + 1)
                    pool.tensor_tensor(ag_lo[:, s % 2, :], ag[:, s % 2, :], ag_hi[:, s % 2, :].bitcast(F32),
                                       ALU.subtract).then_inc(S["ag_lo_ready"], 1)

            phases(pool, quad, None)

        @block.vector
        def _(dve):
            steps = [0]

            def settle(ins):
                steps[0] += 1
                ins.then_inc(S["dve_step"], 1)
                dve.wait_ge(S["dve_step"], steps[0])

            def inverse_mean(out, in_, n, half):
                settle(dve.tensor_scalar(out, in_, 1.0 / n, EPS, ALU.mult, ALU.add))
                dve.reciprocal(out, out).then_inc(half, 1)

            dve.wait_ge(S["ssq_done"], 1)
            inverse_mean(rstd_b[:, :], psum[:, 4, 0:NT], D, S["rstd_half"])
            dve.wait_ge(S["rstd_root"], 1)
            dve.wait_ge(S["gains_copied"], 1)
            for c in range(KC):
                dve.scalar_tensor_tensor(hT[:, c, :], xT[:, c, :], gains[:, c:c + 1], rstd_a[:, :], ALU.mult,
                                         ALU.mult).then_inc(S["hT_ready"], 1)
            for t, (t0, n) in enumerate(TILES):
                dve.wait_ge(S["z_copied"], t + 1)
                x = z[0:n, t, O_Q:O_V].rearrange("p (h d) -> p h d", d=HD)
                settle(dve.tensor_tensor(head_sq[0:n], x, x, ALU.mult))
                settle(dve.tensor_reduce(small[0:n, 0:NH + 1], head_sq[0:n], AX, ALU.add))
                inverse_mean(small[0:n, 8:8 + NH + 1], small[0:n, 0:NH + 1], HD, S["head_var"])
                dve.wait_ge(S["head_root"], t + 1)
                settle(dve.tensor_tensor(x, x, bc(small[0:n, 16:16 + NH + 1], 2, HD), ALU.mult))
                settle(dve.tensor_tensor(x, x, gain5[0:n], ALU.mult))
                x = z[0:n, t, O_Q:O_V].rearrange("p (h a d) -> p h a d", a=2, d=HD // 2)
                cos, sin = (bc(rope[0:n, t, o:o + HD // 2], 1, NH + 1) for o in (0, HD // 2))
                tmp = [rope_tmp[0:n, i, :].rearrange("p (h d) -> p h d", h=NH + 1) for i in range(4)]
                dve.tensor_tensor(tmp[0], x[:, :, 0], cos, ALU.mult)
                dve.tensor_tensor(tmp[1], x[:, :, 1], sin, ALU.mult)
                dve.tensor_tensor(tmp[2], x[:, :, 1], cos, ALU.mult)
                settle(dve.tensor_tensor(tmp[3], x[:, :, 0], sin, ALU.mult))
                dve.tensor_tensor(x[:, :, 0], tmp[0], tmp[1], ALU.subtract)
                dve.tensor_tensor(x[:, :, 1], tmp[2], tmp[3], ALU.add).then_inc(S["rope_done"], 1)

            def take_top(score, work, rounds):
                best = top8[0:score.shape[0], :]
                for r in rounds:
                    left = score if r == 0 else work
                    settle(dve.max(best, left))
                    settle(dve.match_replace(work, best, left, TAKEN))

            for t in range(2):
                dve.wait_ge(S["idx_relu"], t + 1)
                dve.wait_ge(S["idx_rope_done"], 3)
                settle(dve.tensor_scalar(score_p[:, :], rel_p[:, 0, :], iw[:, t, 0:1], None, ALU.mult))
                for h in range(1, IH):
                    ins = dve.scalar_tensor_tensor(score_p[:, :], rel_p[:, h, :], iw[:, t, h:h + 1], score_p[:, :],
                                                   ALU.mult, ALU.add)
                    if h < IH - 1:
                        settle(ins)
                ins.then_inc(S["idx_summed"], 1)
                dve.wait_ge(S["idx_summed"], t + 1)
                settle(dve.tensor_tensor(score_p[:, :], score_p[:, :], causal[:, t, :], ALU.add))
                take_top(score_p[:, :], work_p[:, :], range(KSEL_P // 8))
                settle(dve.tensor_tensor(work_p[:, :], work_p[:, :], score_p[:, :], ALU.is_equal))
                dve.scalar_tensor_tensor(bias_p[:, t, :], work_p[:, :], NEG, causal[:, t, :], ALU.mult, ALU.add
                                         ).then_inc(S["bias_p_ready"], 1)

            dve.wait_ge(S["score_s_copied"], 1)
            settle(dve.tensor_tensor(score_s[:, PAST:KEYS], score_s[:, PAST:KEYS], causal_new[:, :], ALU.add))
            take_top(score_s[:, :], work_s[:, :], range(KSEL_S // 16))

            def soft_p(t):
                dve.wait_ge(S["log_p_psum"], t + 1)
                settle(dve.tensor_reduce(small[:, 24:28], psum[:, 0:2, :].rearrange("p a (h k) -> p (a h) k", h=2),
                                         AX, ALU.max))
                dve.tensor_scalar(small[:, 28:32], small[:, 24:28], -SC, None, ALU.mult).then_inc(S["p_max"], 1)
                dve.wait_ge(S["p_exp"], t + 1)
                settle(dve.reciprocal(small[:, 36:40], small[:, 32:36]))
                dve.tensor_tensor(prob_p[:], prob_p[:], bc(small[:, 36:40], 2, SEQ), ALU.mult
                                  ).then_inc(S["p_norm"], 1)

            soft_p(0)
            take_top(score_s[:, :], work_s[:, :], range(KSEL_S // 16, KSEL_S // 8))
            settle(dve.tensor_tensor(work_s[:, :], work_s[:, :], score_s[:, :], ALU.is_equal))
            settle(dve.tensor_scalar(score_s[:, :], work_s[:, :], NEG, None, ALU.mult))
            dve.tensor_tensor(score_s[:, PAST:KEYS], score_s[:, PAST:KEYS], causal_new[:, :], ALU.add
                              ).then_inc(S["bias_s_ready"], 1)
            soft_p(1)
            for g in range(2):
                dve.wait_ge(S["spread_psum"], g + 1)
                dve.wait_ge(S["log_s_copied"], 2)
                dve.tensor_tensor(log_s[:, g, 0:PAST], log_s[:, g, 0:PAST],
                                  psum[:, 0:2, :].rearrange("p a b -> p (a b)"), ALU.add)
                settle(dve.tensor_tensor(log_s[:, g, PAST:KEYS], log_s[:, g, PAST:KEYS], psum[:, 2, 0:DS], ALU.add))
                settle(dve.tensor_reduce(small[:, 40:41], log_s[:, g, :], AX, ALU.max))
                dve.tensor_scalar(small[:, 41:42], small[:, 40:41], -SC, None, ALU.mult).then_inc(S["s_max"], 1)
                dve.wait_ge(S["s_exp"], g + 1)
                settle(dve.reciprocal(small[:, 43:44], small[:, 42:43]))
                settle(dve.tensor_scalar(log_s[:, g, :], log_s[:, g, :], small[:, 43:44], None, ALU.mult))
                if g:
                    dve.wait_ge(S["sT_psum"], 1)
                dve.tensor_tensor(pnew[:, :].rearrange("p (b s) -> p b s", b=DB), bc(own[:, g, :], 2, DS),
                                  bc(log_s[:, g, PAST:KEYS], 1, DB), ALU.mult).then_inc(S["pnew_ready"], 1)
            for c in range(KC):
                dve.wait_ge(S["wo_psum"], c + 1)
                dve.tensor_tensor(xT[:, c, :], xT[:, c, :], psum[:, c % 4, 0:NT], ALU.add).then_inc(S["x1_ready"], 1)
            dve.wait_ge(S["ssq2_done"], 1)
            inverse_mean(rstd_b[:, :], psum[:, 4, 0:NT], D, S["rstd2_half"])
            dve.wait_ge(S["rstd2_root"], 1)
            for c in range(KC):
                dve.scalar_tensor_tensor(h2[:, c, :], xT[:, c, :], gains[:, KC + c:KC + c + 1], rstd_a[:, :],
                                         ALU.mult, ALU.mult).then_inc(S["h2_ready"], 1)

            settle(dve.tensor_copy(iotab[:, :], iota[:, 0:TK]))
            for t in range(3):
                H = RH if t < 2 else 2
                scores = sr[:, t] if t < 2 else sr_s[:]
                svr, sir = (a[:].rearrange("p h c k -> p (h c) k") for a in (sv, si))
                for r0 in range(0, 2 * H, 4):
                    if t == 0:
                        dve.wait_ge(S["rs_copied"], r0 // 4 + 1)
                    elif t == 2:
                        dve.wait_ge(S["rs_copied"], 4)
                    four = range(4)
                    for i in four:
                        ins = dve.max(svr[:, r0 + i, 0:8], scores[:, r0 + i, :])
                    settle(ins)
                    for i in four:
                        dve.max_index(sir[:, r0 + i, 0:8], svr[:, r0 + i, 0:8], scores[:, r0 + i, :])
                        ins = dve.match_replace(rwork[:, i, :], svr[:, r0 + i, 0:8], scores[:, r0 + i, :], TAKEN)
                    settle(ins)
                    for i in four:
                        ins = dve.max(svr[:, r0 + i, 8:16], rwork[:, i, :])
                    settle(ins)
                    for i in four:
                        ins = dve.max_index(sir[:, r0 + i, 8:16], svr[:, r0 + i, 8:16], rwork[:, i, :])
                settle(ins)
                dve.tensor_copy(sib[:, 0:H], si[:, 0:H])
                for h in range(H):
                    ins = dve.tensor_tensor(cand[:, h], bc(sv[:, h, 0, :], 2, TK), bc(sv[:, h, 1, :], 1, TK), ALU.add)
                settle(ins)
                rw = rwork[:].rearrange("p (a b) k -> p a (b k)", b=2)
                cd = cand[:].rearrange("p h a b -> p h (a b)")
                for h0 in range(0, H, 2):
                    for i in range(2):
                        ins = dve.max(fv[:, h0 + i, 0:8], cd[:, h0 + i, :])
                    settle(ins)
                    for i in range(2):
                        dve.max_index(fi[:, h0 + i, 0:8], fv[:, h0 + i, 0:8], cd[:, h0 + i, :])
                        ins = dve.match_replace(rw[:, i, :], fv[:, h0 + i, 0:8], cd[:, h0 + i, :], TAKEN)
                    settle(ins)
                    for i in range(2):
                        ins = dve.max(fv[:, h0 + i, 8:16], rw[:, i, :])
                    settle(ins)
                    for i in range(2):
                        ins = dve.max_index(fi[:, h0 + i, 8:16], fv[:, h0 + i, 8:16], rw[:, i, :])
                settle(ins)
                if t:
                    dve.wait_ge(S["slots_psum"], t)
                dve.tensor_tensor(slots[:, 2, 0:H], fv[:, 0:H], fv[:, 0:H, 0:1].to_broadcast([P, H, TK]),
                                  ALU.subtract).then_inc(S["rexp_in"], 1)
                dve.tensor_scalar(fab[:, 0, 0:H], fi[:, 0:H], 4, None, ALU.logical_shift_right)
                settle(dve.tensor_scalar(fab[:, 1, 0:H], fi[:, 0:H], TK - 1, None, ALU.bitwise_and))
                dve.tensor_copy(fabb[:, 0, 0:H], fab[:, 0, 0:H])
                settle(dve.tensor_copy(fabb[:, 1, 0:H], fab[:, 1, 0:H]))
                for c in range(2):
                    m = fabb[:, c, 0:H].rearrange("p h k -> p (h k)")
                    settle(dve.tensor_tensor(hit[:, 0:H].rearrange("p h k a -> p (h k) a"), bc(m, 2, TK),
                                             bc(iotab[:, :], 1, H * TK), ALU.is_equal))
                    settle(dve.tensor_tensor(picked[:, 0:H], hit[:, 0:H], bc(sib[:, 0:H, c, :], 2, TK), ALU.mult))
                    dve.tensor_reduce(slots[:, c, 0:H].rearrange("p h k -> p (h k)"),
                                      picked[:, 0:H].rearrange("p h k a -> p (h k) a"), AX, ALU.add)
                dve.wait_ge(S["rexp_out"], t + 1)
                settle(dve.tensor_reduce(ssum[:, 0:H], slots[:, 2, 0:H], AX, ALU.add))
                settle(dve.reciprocal(ssum[:, 0:H], ssum[:, 0:H]))
                dve.tensor_tensor(slots[:, 2, 0:H], slots[:, 2, 0:H], bc(ssum[:, 0:H], 2, TK), ALU.mult
                                  ).then_inc(S["slots_ready"], 1)
                if t < 2:
                    slots_low(dve, t)
            slots_low(dve, 2)
            dve.wait_ge(S["h_split_lo"], 1)

            def weights_of(slot, n, token, ph):
                dve.tensor_tensor(i_eq[:, slot], bc(iota[:, ph * PH:(ph + 1) * PH], 1, NB),
                                  bc(iT[:, bass.ds(token, NB)], 2, PH), ALU.is_equal).then_inc(S["i_eq_ready"], 1)
                dve.tensor_tensor(j_hot[:, slot], bc(iota[:, :], 1, NB), bc(jT[:, bass.ds(token, NB)], 2, P),
                                  ALU.is_equal).then_inc(S["j_ready"], 1)

            flat_ps = psum[:].rearrange("p a b -> p (a b)")

            def collect(n, bank0, half, token):
                dve.wait_ge(S["g_psum"], n + 1)
                parts = flat_ps[:, bank0 * BANK:bank0 * BANK + NB * 64].rearrange("p (b a i) -> p b i a", b=NB, a=2)
                out = g_ring[:, half * PH:(half + 1) * PH, bass.ds(token, NB)].rearrange("p i b -> p b i")
                dve.tensor_reduce(out, parts, AX, ALU.add).then_inc(S["g_copied"], 1)

            weights_of(0, 0, 0, 0)
            weights_of(1, 1, NB, 0)
            with dve.Fori(1, PH // 2) as m:
                for s in range(2):
                    collect(2 * m + (s - 2), 2 * s, 0, NB * (2 * m + (s - 2)))
                    weights_of(s, 2 * m + s, NB * (2 * m + s), 0)
            for s in range(2):
                collect(PH - 2 + s, 2 * s, 0, NB * (PH - 2 + s))

            def low_u(slot, n):
                dve.wait_ge(S["uT_hi_ready"], n + 1)
                dve.tensor_tensor(uT_lo[:, slot % 2].rearrange("p a b -> p (a b)"), flat_ps[:, 6 * BANK:8 * BANK],
                                  uT_hi[:, slot % 2].rearrange("p a b -> p (a b)").bitcast(F32), ALU.subtract
                                  ).then_inc(S["uT_lo_ready"], 1)

            def quad(q, ph, start=False, stop=False):
                spreads = ph < NU // PH - 1
                for s in range(4):
                    n = 4 * q + s
                    in_ph = n - ph * PH
                    if not (stop and s == 3):
                        low_u(s + 1, n + 1)
                    if spreads:
                        dve.wait_ge(S["g_psum"], n + PH - 1)
                        weights_of(s % 2, n + PH, NB * in_ph, ph + 1)
                    dve.wait_ge(S["act_ready"], n + 1)
                    if not (start and s < 2):
                        dve.wait_ge(S["ag_hi_ready"], n - 1)
                        dve.wait_ge(S["ag_lo_ready"], n - 1)
                    dve.wait_ge(S["g_copied"], n + PH if spreads else NU)
                    dve.tensor_tensor(ag[:, s % 2, :], act_g[:, s % 2, :],
                                      g_ring[:, bass.ds(in_ph + (ph % 2) * PH, 1), :].rearrange("p a t -> p (a t)"),
                                      ALU.mult).then_inc(S["prod_ready"], 1)
                    if spreads:
                        collect(n + PH, 6, (ph + 1) % 2, NB * in_ph)

            low_u(0, 0)
            phases(dve, quad, None)
            dve.wait_ge(S["v_mm_done"], NU)
            for c, t0, w, bank, col in Y:
                ins = dve.tensor_tensor(yT[:, c, t0:t0 + w], xT[:, c, t0:t0 + w], psum[:, bank, col:col + w], ALU.add)
            ins.then_inc(S["yT_ready"], 1)
    ctx.close()


_INS = ["x_prompt", "x_sample", "cache_k", "cache_v", "cache_ik", "state_pool", "page_table", "norm1_g", "w_in",
        "q_norm_g", "k_norm_g", "w_pool", "pool_scale", "w_o", "norm2_g", "w_pq", "sub_keys", "expert_u", "expert_v"]


def kernel(**inputs):
    import concourse.bacc as bacc
    from concourse.bass_utils import run_bass_kernel_spmd

    nc = bacc.Bacc("TRN2", target_bir_lowering=False, num_devices=1)
    a = {n: np.ascontiguousarray(inputs[n]) for n in _INS}
    _, SEQ, D = a["x_prompt"].shape
    DB, DS, _ = a["x_sample"].shape
    HD, ID = a["cache_k"].shape[3], a["cache_ik"].shape[3]
    NST, PW = a["state_pool"].shape[2:]
    IH = (a["w_in"].shape[2] - PW - (D - PW) - 2 * HD - ID) // (ID + 1)
    PAST = a["page_table"].shape[1] * a["cache_k"].shape[2]
    a.update(shape_constants(SEQ, DB, DS, PAST, (D - PW) // HD, HD, IH, ID, NST))
    outs = [("y_prompt", (1, SEQ, D)), ("y_sample", (DB, DS, D)),
            ("k_prompt", (1, 1, SEQ, HD)), ("v_prompt", (1, 1, SEQ, HD)), ("ik_prompt", (1, 1, SEQ, ID)),
            ("pool_prompt", (1, 1, NST, PW)), ("k_sample", (1, DB, DS, HD)), ("v_sample", (1, DB, DS, HD)),
            ("ik_sample", (1, DB, DS, ID)), ("pool_sample", (1, DB, NST, PW))]
    args = {n: nc.dram_tensor(n, v.shape, mybir.dt.from_np(v.dtype), kind="ExternalInput").ap() for n, v in a.items()}
    for n, shape in outs:
        args[n] = nc.dram_tensor(n, shape, F32, kind="ExternalOutput").ap()
    hybrid_kernel(nc, **args)
    r = run_bass_kernel_spmd(nc, [a], core_ids=[0])
    return tuple(r.results[0][n] for n, _ in outs)
```

```python
from contextlib import ExitStack

import numpy as np

import concourse.bass as bass
from concourse import mybir

ALU = mybir.AluOpType
ACT = mybir.ActivationFunctionType
AX = mybir.AxisListType.X
F32 = mybir.dt.float32
F32R = mybir.dt.float32r
BF16 = mybir.dt.bfloat16
I32 = mybir.dt.int32
U32 = mybir.dt.uint32
P = 128
BANK = 512
EPS = 1e-6
THETA = 10000.0
NEG = -1e30
TAKEN = -3e38
WINDOWS = (2, 4, 8, 16)


def shape_constants(SEQ, DB, DS, PAST, NH, HD, IH, ID, NST):
    NT = SEQ + DB * DS
    pos = np.concatenate([np.arange(SEQ), np.tile(PAST + np.arange(DS), DB)]).astype(np.float32)
    tabs = []
    for dim in (HD, ID):
        half = dim // 2
        inv = (np.float32(THETA) ** (-np.arange(half, dtype=np.float32) / np.float32(half))).astype(np.float32)
        ang = pos[:, None] * inv[None, :]
        tabs += [np.cos(ang), np.sin(ang)]
    rope = np.concatenate(tabs, axis=1).astype(np.float32)
    NW = len(WINDOWS)
    band = np.zeros((SEQ, NW, SEQ), np.float32)
    band_state = np.zeros((DB * NST, NW, DB * DS), np.float32)
    band_new = np.zeros((DB * DS, NW, DB * DS), np.float32)
    for g, w in enumerate(WINDOWS):
        for t in range(SEQ):
            lo = max(0, t + 1 - w)
            band[lo:t + 1, g, t] = 1.0 / min(t + 1, w)
            band[t, g, t] -= 1.0
        for b in range(DB):
            for s in range(DS):
                for r in range(NST + s + 1 - w, NST + s + 1):
                    if r < NST:
                        band_state[b * NST + r, g, b * DS + s] = 1.0 / w
                    else:
                        band_new[b * DS + r - NST, g, b * DS + s] = 1.0 / w
                band_new[b * DS + s, g, b * DS + s] -= 1.0
    causal = np.where(np.arange(SEQ)[None, :] <= np.arange(SEQ)[:, None], 0.0, NEG).astype(np.float32)
    causal_new = np.where(np.arange(DS)[None, :] <= (np.arange(DB * DS) % DS)[:, None], 0.0, NEG).astype(np.float32)
    fold = np.zeros((DB * DS, DB // 4, P), np.float32)
    own = np.zeros((P, DB // 4, DB), np.float32)
    for g in range(DB // 4):
        for j in range(4):
            for h in range(IH):
                for s in range(DS):
                    row = 32 * j + h * DS + s
                    fold[(4 * g + j) * DS + s, g, row] = 1.0
                    own[row, g, 4 * g + j] = 1.0
    iota = np.tile(np.arange(P, dtype=np.float32)[None], (P, 1))
    return dict(c_rope=rope, c_band=band, c_band_state=band_state, c_band_new=band_new, c_causal=causal,
                c_causal_new=causal_new, c_fold=fold, c_own=own, c_ident=np.eye(P, dtype=np.float32), c_iota=iota)


class Named(dict):

    def __init__(self, nc, ctx):
        self.nc, self.ctx = nc, ctx

    def __missing__(self, name):
        self[name] = self.ctx.enter_context(self.nc.semaphore(name))
        return self[name]


def hybrid_kernel(nc, x_prompt, x_sample, cache_k, cache_v, cache_ik, state_pool, page_table,
                  norm1_g, w_in, q_norm_g, k_norm_g, w_pool, pool_scale, w_o, norm2_g, w_pq, sub_keys,
                  expert_u, expert_v, c_rope, c_band, c_band_state, c_band_new, c_causal, c_causal_new,
                  c_fold, c_own, c_ident, c_iota,
                  y_prompt, y_sample, k_prompt, v_prompt, ik_prompt, pool_prompt,
                  k_sample, v_sample, ik_sample, pool_sample):
    SEQ, D = x_prompt.shape[1:]
    DB, DS = x_sample.shape[:2]
    HD, ID = cache_k.shape[3], cache_ik.shape[3]
    PAGE = cache_k.shape[2]
    NPOOL = cache_k.shape[1]
    NPG = page_table.shape[1]
    PAST = NPG * PAGE
    NST, PW = state_pool.shape[2:]
    NG = w_pool.shape[1]
    NH = (D - PW) // HD
    RH = sub_keys.shape[1]
    NK = sub_keys.shape[3]
    IN_W = w_in.shape[2]
    IH = (IN_W - PW - NH * HD - 2 * HD - ID) // (ID + 1)
    TK = 16
    KC = D // P
    NS = DB * DS
    NT = SEQ + NS
    TILES = ((0, P), (P, P), (SEQ, NS))
    KEYS = PAST + DS
    KSEL_P = min(256, SEQ // 4)
    KSEL_S = min(256, KEYS // 4)
    SC = float(HD) ** -0.5
    RSLOTS = 2 * RH
    O_Q, O_K = PW, PW + NH * HD
    O_V = O_K + HD
    O_IQ = O_V + HD
    O_IK = O_IQ + IH * ID
    O_IW = O_IK + ID
    assert SEQ == 2 * P and NS == 32 and D == 8 * P and PAGE == P and HD == P and NK == P and NG == 4
    assert DS == 4 and DB == 8 and IH == 8 and ID == 64 and NH == 4 and RH == 8 and NPG == 8

    ctx = ExitStack()
    psum = ctx.enter_context(nc.psum_tensor("psum", [P, 8, BANK], F32))

    base = (nc.sbuf_base + 63) // 64 * 64
    WORDS = (nc.sbuf_usable_end // 4) - base // 4 - 8
    high = [0]

    def at(name, off, shape, dt=F32):
        n = int(np.prod(shape[1:])) * (2 if dt == BF16 else 4)
        assert off * 4 + n <= WORDS * 4, (name, off, n, WORDS)
        high[0] = max(high[0], off * 4 + n)
        return nc.alloc_sbuf_tensor_at(name, shape, dt, offset=base + off * 4)

    cur = [0]

    def take(name, shape, dt=F32):
        n = (int(np.prod(shape[1:])) * (2 if dt == BF16 else 4) + 31) // 32 * 8
        t = at(name, cur[0], shape, dt)
        cur[0] += n
        return t

    ident = take("ident", [P, P])
    iota = take("iota", [P, P])
    ones = take("ones", [P, P])
    xT = take("xT", [P, KC, NT])
    gains = take("gains", [P, 2 * KC + NG])
    NB = NT // 32
    iT = take("iT", [P, NT], BF16)
    jT = take("jT", [P, NT], BF16)
    wT = take("wT", [P, NT])
    w_rest = take("w_rest", [P, NT])
    w3 = take("w3", [P, 3, NT], BF16)
    counts = take("counts", [P, P, NB], BF16)
    small = take("small", [P, 64])
    top8 = take("top8", [P, 8])
    F0 = cur[0]

    w_in_sb = take("w_in_sb", [P, KC, IN_W])
    W0 = F0
    cur[0] = W0 + 2 * KC * D
    v_cache = at("v_cache", W0, [P, DB, NPG, HD])
    k_cache = at("k_cache", W0 + KC * D, [P, DB, NPG, HD])
    w_o_sb = at("w_o_sb", W0 + KC * D, [P, KC, D])
    w_pq_lo = at("w_pq_lo", W0, [P, KC, D])
    w_pq_hi = at("w_pq_hi", W0 + KC * D, [P, KC, D])
    Z0 = cur[0]
    z = take("z", [P, 3, IN_W])
    A0 = cur[0]
    x_nat = at("x_nat", A0, [P, 3, D])
    ik_cache = at("ik_cache", A0, [P, DB, NPG, ID])
    keysT = at("keysT", A0, [P, RSLOTS, NK])
    keys_nat = at("keys_nat", A0 + RSLOTS * NK, [P, RSLOTS, HD])
    cur[0] = A0 + 4096
    A1 = cur[0]
    sq = at("sq", A1, [P, KC, NT])
    iqT = at("iqT", A1, [64, IH + 1, SEQ])
    log_s = at("log_s", A1, [P, 2, KEYS])
    cur[0] = A1 + 2304
    hT = take("hT", [P, KC, NT])
    catT = at("catT", cur[0] - KC * NT, [P, KC, NT])
    A3 = cur[0]
    ikT = take("ikT", [64, 2, KEYS])
    kT_s = at("kT_s", A3, [P, 2, KEYS])
    idx_tmp = at("idx_tmp", A3, [P, 4, (IH + 1) * ID // 2])
    sq2 = at("sq2", A3, [P, KC, NT])
    A4 = cur[0]
    dT = at("dT", A4, [P, NG, NT])
    rel_s = take("rel_s", [P, 2, KEYS])
    band = at("band", cur[0], [P, 2, NG, SEQ])
    score_s = take("score_s", [NS, KEYS])
    work_s = take("work_s", [NS, KEYS])
    A6 = cur[0]
    rel_p = take("rel_p", [P, IH, SEQ])
    A7 = cur[0]
    score_p = take("score_p", [P, SEQ])
    work_p = take("work_p", [P, SEQ])
    bias_p = take("bias_p", [P, 2, SEQ])
    prob_p = take("prob_p", [P, NH, SEQ])
    probT = take("probT", [P, NPG, P])
    rope_tmp = at("rope_tmp", A7, [P, 4, (NH + 1) * HD // 2])
    head_sq = at("head_sq", A7 + 2 * (NH + 1) * HD, [P, NH + 1, HD])
    A8 = cur[0]
    qkT = take("qkT", [P, NH + 1, NT])
    q_s = take("q_s", [P, DB, 8, DS])
    iq_s = take("iq_s", [64, DB, IH, DS])
    ik_new = take("ik_new", [64, NS])
    gain5 = take("gain5", [P, NH + 1, HD])
    band_state = take("band_state", [DB * NST, NG, NS])
    band_new = take("band_new", [NS, NG, NS])
    w_pool_sb = at("w_pool_sb", A6, [P, NG, P])
    state_sb = at("state_sb", A6 + NG * P, [DB * NST, PW])
    rope = take("rope", [P, 3, HD + ID])
    causal = take("causal", [P, 2, SEQ])
    causal_new = take("causal_new", [NS, DS])
    fold = take("fold", [NS, 2, P])
    own = take("own", [P, 2, DB])
    fold_iw = take("fold_iw", [NS, 2, P])
    w_fold = take("w_fold", [P, 2, NS])
    pnew = take("pnew", [P, NS])
    pnewT = take("pnewT", [NS, P])
    rstd_a = take("rstd_a", [P, NT])
    rstd_b = take("rstd_b", [P, NT])
    gain_rows = take("gain_rows", [2 * KC + NG, P])
    head_gain = take("head_gain", [1, 2, HD])
    pages = take("pages", [1, DB * NPG], I32)
    iw = take("iw", [P, 3, IH])

    cur[0] = A1 + 2304
    sr = at("sr", Z0, [P, 2, RSLOTS, NK])
    cur[0] = A3
    assert Z0 + 2 * RSLOTS * NK <= A0
    q_ring = take("q_ring", [P, 2, NT])
    sr_s = take("sr_s", [P, 4, NK])
    rwork = take("rwork", [P, 4, NK])
    sv = take("sv", [P, RH, 2, TK])
    si = take("si", [P, RH, 2, TK], U32)
    sib = take("sib", [P, RH, 2, TK], BF16)
    cand = take("cand", [P, RH, TK, TK])
    fv = take("fv", [P, RH, TK])
    fi = take("fi", [P, RH, TK], U32)
    fab = take("fab", [P, 2, RH, TK], U32)
    fabb = take("fabb", [P, 2, RH, TK], BF16)
    hit = take("hit", [P, RH, TK, TK], BF16)
    picked = take("picked", [P, RH, TK, TK], BF16)
    iotab = take("iotab", [P, TK], BF16)
    slots = take("slots", [P, 3, RH, TK])
    ssum = take("ssum", [P, RH])
    h2 = at("h2", A1, [P, KC, NT])
    ROUTE_END = cur[0]

    cur[0] = F0
    u_raw = take("u_raw", [P, 2, D])
    v_raw = take("v_raw", [P, 4, D])
    g_ring = take("g_ring", [P, 64, NT])
    uT_hi = take("uT_hi", [P, 2, KC, P], F32R)
    uT_lo = take("uT_lo", [P, 2, KC, P], F32R)
    v_hi = take("v_hi", [P, 4, D], F32R)
    v_lo = take("v_lo", [P, 4, D], F32R)
    j_hot = take("j_hot", [P, 2, P, NB], BF16)
    i_eq = take("i_eq", [P, 2, 32, NB], BF16)
    i_hot = take("i_hot", [P, 2, 3, 32, NB], BF16)
    act_g = take("act_g", [P, 2, NT])
    ag = take("ag", [P, 2, NT])
    ag_hi = take("ag_hi", [P, 4, NT], F32R)
    ag_lo = take("ag_lo", [P, 4, NT], F32R)
    MAIN_END = cur[0]
    assert ROUTE_END <= MAIN_END, (ROUTE_END, MAIN_END)
    h_hi = take("h_hi", [P, KC, NT], F32R)
    h_lo = take("h_lo", [P, KC, NT], F32R)
    y_nat = at("y_nat", F0 + 8 * D, [P, 3, D])

    S = Named(nc, ctx)
    u_in = [ctx.enter_context(nc.semaphore(f"u_in{i}")) for i in range(2)]
    v_tile_in = [ctx.enter_context(nc.semaphore(f"v_tile_in{i}")) for i in range(4)]

    def bc(ap, axis, n):
        a = ap.unsqueeze(axis)
        shape = list(a.shape)
        shape[axis] = n
        return a.to_broadcast(shape)

    def flat(ap):
        return ap.rearrange("p a b -> p (a b)")

    NU = NK
    PH, QUADS = 32, 8
    u_rows = expert_u.rearrange("a (n p) d -> (a n) p d", p=P)
    v_rows = expert_v.rearrange("a (n p) d -> (a n) p d", p=P)
    const_loads = [
        (ident[:], c_ident), (iota[:], c_iota),
        (gain_rows[0:KC, :], norm1_g.rearrange("a (k p) -> (a k) p", p=P)),
        (gain_rows[KC:2 * KC, :], norm2_g.rearrange("a (k p) -> (a k) p", p=P)),
        (gain_rows[2 * KC:2 * KC + NG, :], pool_scale.rearrange("a (k p) -> (a k) p", p=P)),
        (head_gain[0:1, 0, :], q_norm_g), (head_gain[0:1, 1, :], k_norm_g),
        (rope[:, 0:2, :], c_rope[0:SEQ, :].rearrange("(t p) c -> p t c", p=P)), (rope[0:NS, 2, :], c_rope[SEQ:NT, :]),
        (causal[:], c_causal.rearrange("(t p) c -> p t c", p=P)), (causal_new[:], c_causal_new),
        (fold[:], c_fold), (own[:], c_own), (pages[0:1, :], page_table.rearrange("b n -> (b n)").unsqueeze(0)),
        (band[:, 0], c_band[0:P]), (band[:, 1], c_band[P:SEQ]), (band_state[:], c_band_state),
        (band_new[:], c_band_new), (w_pool_sb[:], w_pool[0].rearrange("g c n -> c g n")),
        (state_sb[:], state_pool[0].rearrange("b r d -> (b r) d")),
    ]

    def phases(eng, quad):
        last = NU // PH - 1
        for ph in range(last + 1):
            q0, q1 = ph * QUADS, (ph + 1) * QUADS
            if ph == 0:
                quad(q0, ph, start=True)
                q0 += 1
            if ph == last:
                q1 -= 1
            with eng.Fori(q0, q1) as q:
                quad(q, ph)
            if ph == last:
                quad(q1, ph, stop=True)

    def rs_copy(act, copy, q4):
        act.wait_ge(S["rs_psum"], 4 * q4 + 4)
        for t in range(2):
            a = copy(sr[:, t, 4 * q4:4 * q4 + 4, :].rearrange("p a b -> p (a b)"), psum[:, 4 + t, :])
        if q4 == 3:
            a = copy(sr_s[:].rearrange("p a b -> p (a b)"), psum[:, 6, :])
        a.then_inc(S["rs_copied"], 1)

    with nc.Block() as block:
        @block.sync
        def _(sp):
            for t, (t0, n) in enumerate(TILES):
                src = x_prompt[0, t0:t0 + n, :] if t < 2 else x_sample.rearrange("b s d -> (b s) d")
                sp.dma_start(x_nat[0:n, t, :], src).then_inc(S["x_in"], 16)
            for dst, src in const_loads:
                sp.dma_start(dst, src).then_inc(S["consts_in"], 16)
            for k in range(KC):
                sp.dma_start(w_in_sb[:, k, :], w_in[0, k * P:(k + 1) * P, :]).then_inc(S["w_in_in"], 16)
            sp.dma_start(pool_sample[0, :, 0:NST - DS, :], state_pool[0, :, DS:NST, :]).then_inc(S["out_done"], 16)

            def page_loads(cache, dst, width, sem):
                with sp.Fori(0, DB * NPG) as i:
                    pg = sp.value_load(pages[0:1, bass.ds(i, 1)], min_val=0, max_val=NPOOL - 1)
                    sp.dma_start(dst[:, bass.ds(i * width, width)],
                                 cache[0, bass.ds(pg, 1), :, :].rearrange("a p d -> (a p) d")).then_inc(sem, 16)

            sp.wait_ge(S["consts_in"], 16 * len(const_loads))
            sp.wait_ge(S["xT_psum"], KC)
            page_loads(cache_ik, ik_cache[:].rearrange("p b n d -> p (b n d)"), ID, S["ik_in"])
            sp.wait_ge(S["z_done"], 3)
            page_loads(cache_k, k_cache[:].rearrange("p b n d -> p (b n d)"), HD, S["k_in"])
            page_loads(cache_v, v_cache[:].rearrange("p b n d -> p (b n d)"), HD, S["v_in"])
            sp.wait_ge(S["rope_done"], 3)
            sp.wait_ge(S["idx_rope_done"], 3)
            for outs, col, w in ((( k_prompt, k_sample), O_K, HD), ((v_prompt, v_sample), O_V, HD),
                                 ((ik_prompt, ik_sample), O_IK, ID)):
                for t, (t0, n) in enumerate(TILES):
                    dst = outs[0][0, 0, t0:t0 + n, :] if t < 2 else outs[1][0].rearrange("b s d -> (b s) d")
                    sp.dma_start(dst, z[0:n, t, col:col + w]).then_inc(S["rows_out"], 16)
            sp.dma_start(pool_prompt[0, 0], z[P - NST:P, 1, 0:PW]).then_inc(S["rows_out"], 16)
            for b in range(DB):
                sp.dma_start(pool_sample[0, b, NST - DS:NST, :], z[b * DS:(b + 1) * DS, 2, 0:PW]
                             ).then_inc(S["rows_out"], 16)
            sp.wait_ge(S["idx_s_psum"], 2)
            sp.wait_ge(S["ikT_psum"], DB)
            sp.dma_start(keys_nat[:], sub_keys[0].rearrange("h c k d -> k (h c) d")).then_inc(S["keys_in"], 16)
            sp.wait_ge(S["kT_psum"], DB)
            for k in range(KC):
                sp.dma_start(w_o_sb[:, k, :], w_o[0, k * P:(k + 1) * P, :]).then_inc(S["w_o_in"], 16)
            sp.wait_ge(S["ys_psum"], 2)
            for k in range(KC):
                sp.dma_start(w_pq_lo[:, k, :], w_pq[0, k * P:(k + 1) * P, 0:D]).then_inc(S["w_pq_lo_in"], 16)
            sp.wait_ge(S["wo_psum"], KC)
            for k in range(KC):
                sp.dma_start(w_pq_hi[:, k, :], w_pq[0, k * P:(k + 1) * P, D:2 * D]).then_inc(S["w_pq_hi_in"], 16)

            def load_u(row, slot):
                sp.dma_start(u_raw[:, slot, :], u_rows[bass.ds(row, 1)].rearrange("a p d -> (a p) d")
                             ).then_inc(u_in[slot], 16)

            def load_v(row, slot):
                sp.dma_start(v_raw[:, slot, :], v_rows[bass.ds(row, 1)].rearrange("a p d -> (a p) d")
                             ).then_inc(v_tile_in[slot], 16)

            sp.wait_ge(S["rq_psum"], RSLOTS)
            for s in range(4):
                if s < 2:
                    load_u(s, s)
                load_v(s, s)

            def quad(q, stop=False):
                for s in range(4):
                    sp.wait_ge(S["tr_done"], 4 * q + (s + 1))
                    if not (stop and s >= 2):
                        load_u(4 * q + (s + 2), s % 2)
                    if not stop:
                        sp.wait_ge(S["v_lo_ready"], 4 * q + (s + 1))
                        load_v(4 * q + (s + 4), s)

            with sp.Fori(0, NU // 4 - 1) as q:
                quad(q)
            quad(NU // 4 - 1, True)

            sp.wait_ge(S["yn_copied"], 3)
            for t, (t0, n) in enumerate(TILES):
                dst = y_prompt[0, t0:t0 + n, :] if t < 2 else y_sample.rearrange("b s d -> (b s) d")
                sp.dma_start(dst, y_nat[0:n, t, :]).then_inc(S["out_done"], 16)
            sp.wait_ge(S["out_done"], 16 * 4)

        @block.tensor
        def _(pe):
            def tr(out, in_):
                n = in_.shape[0]
                return pe.transpose(out, in_, ident[0:n, 0:n])

            pe.wait_ge(S["x_in"], 48)
            pe.wait_ge(S["consts_in"], 16 * len(const_loads))
            for c in range(KC):
                if c >= 4:
                    pe.wait_ge(S["sq_ready"], c - 3)
                for t, (t0, n) in enumerate(TILES):
                    mm = tr(psum[:, c % 4, t0:t0 + n], x_nat[0:n, t, c * P:(c + 1) * P])
                mm.then_inc(S["xT_psum"], 1)
            tr(psum[:, 5, 0:2 * KC + NG], gain_rows[:, :])
            pe.wait_ge(S["ones_set"], 1)
            pe.matmul(psum[:, 6, 0:2 * HD], ones[0:1, :], head_gain[0:1, :, :].rearrange("p a b -> p (a b)"),
                      start=True, stop=True).then_inc(S["gains_psum"], 1)
            for c in range(KC):
                pe.wait_ge(S["sq_ready"], c + 1)
                mm = pe.matmul(psum[:, 4, 0:NT], ones[:, :], sq[:, c, :], start=(c == 0), stop=(c == KC - 1))
            mm.then_inc(S["ssq_done"], 1)
            pe.wait_ge(S["gains_copied"], 1)
            for t, (t0, n) in enumerate(TILES):
                bank0 = 4 * (t % 2)
                if t == 2:
                    pe.wait_ge(S["z_copied"], 1)
                for k in range(KC):
                    if t == 0:
                        pe.wait_ge(S["hT_ready"], k + 1)
                        if k == 0:
                            pe.wait_ge(S["w_in_in"], 16 * KC)
                    for j in range(4):
                        w = min(BANK, IN_W - BANK * j)
                        mm = pe.matmul(psum[0:n, bank0 + j, 0:w], hT[:, k, t0:t0 + n],
                                       w_in_sb[:, k, BANK * j:BANK * j + w], start=(k == 0), stop=(k == KC - 1))
                mm.then_inc(S["z_done"], 1)
            pe.wait_ge(S["z_copied"], 2)
            for t, (t0, n) in enumerate(TILES):
                pe.wait_ge(S["rope_done"], t + 1)
                pe.wait_ge(S["idx_rope_done"], t + 1)
                if t:
                    pe.wait_ge(S["heads_copied"], t)
                for h in range(NH):
                    tr(psum[:, 4, h * n:(h + 1) * n], z[0:n, t, O_Q + h * HD:O_Q + (h + 1) * HD])
                tr(psum[:, 5, 0:n], z[0:n, t, O_K:O_K + HD])
                tr(psum[0:ID, 5, n:2 * n], z[0:n, t, O_IK:O_IK + ID])
                for h in range(IH):
                    mm = tr(psum[0:ID, 6 + h // 4, (h % 4) * n:(h % 4 + 1) * n],
                            z[0:n, t, O_IQ + h * ID:O_IQ + (h + 1) * ID])
                mm.then_inc(S["heads_psum"], 1)
            pe.wait_ge(S["heads_copied"], 3)
            for g in range(NG):
                cols = slice(g * P, (g + 1) * P)
                pe.matmul(psum[:, 4 + g, 0:SEQ], z[:, 0, cols], band[:, 0, g, :], start=True, stop=False)
                pe.matmul(psum[:, 4 + g, 0:SEQ], z[:, 1, cols], band[:, 1, g, :], start=False, stop=True)
                pe.matmul(psum[:, 4 + g, SEQ:NT], state_sb[:, cols], band_state[:, g, :], start=True, stop=False)
                mm = pe.matmul(psum[:, 4 + g, SEQ:NT], z[0:NS, 2, cols], band_new[:, g, :], start=False, stop=True)
                mm.then_inc(S["pool_d_psum"], 1)
            for g in range(NG):
                pe.wait_ge(S["pool_d_copied"], g + 1)
                pe.matmul(psum[:, 4 + g, 0:NT], w_pool_sb[:, g, :], dT[:, g, :], start=True, stop=True
                          ).then_inc(S["pool_y_psum"], 1)
            pe.wait_ge(S["z_copied"], 3)
            for t in range(2):
                if t:
                    pe.wait_ge(S["idx_relu"], 1)
                for h in range(IH):
                    mm = pe.matmul(psum[:, h // 2, (h % 2) * SEQ:(h % 2 + 1) * SEQ], iqT[:, h, t * P:(t + 1) * P],
                                   iqT[:, IH, :], start=True, stop=True)
                mm.then_inc(S["idx_psum"], 1)
            pe.wait_ge(S["pool_y_copied"], NG)
            pe.wait_ge(S["ik_in"], 16 * DB * NPG)
            pe.wait_ge(S["idx_relu"], 2)

            def scores_s(b, q, keys, done):
                rows = slice(32 * (b % 4), 32 * (b % 4) + 32)
                for lo, w, bank in ((0, BANK, 0), (BANK, BANK, 1), (PAST, DS, 2)):
                    mm = pe.matmul(psum[rows, bank, 0:w], q, keys[:, lo:lo + w], start=True, stop=True,
                                   skip_group_check=True, tile_position=(0, rows.start))
                return mm

            def step_idx(b):
                if b >= 2:
                    pe.wait_ge(S["ikT_copied"], b - 1)
                for n in range(NPG):
                    mm = tr(psum[0:ID, 4 + 2 * (b % 2) + n // 4, (n % 4) * P:(n % 4 + 1) * P], ik_cache[:, b, n, :])
                mm.then_inc(S["ikT_psum"], 1)

            step_idx(0)
            for b in range(DB):
                if b + 1 < DB:
                    step_idx(b + 1)
                pe.wait_ge(S["ikT_copied"], b + 1)
                if b == 4:
                    pe.wait_ge(S["idx_s_relu"], 1)
                mm = scores_s(b, iq_s[:, b].rearrange("p h s -> p (h s)"), ikT[:, b % 2, :], None)
                if b % 4 == 3:
                    mm.then_inc(S["idx_s_psum"], 1)
            pe.wait_ge(S["fold_iw_ready"], 2)
            for g in range(2):
                mm = tr(psum[:, 3, g * NS:(g + 1) * NS], fold_iw[:, g, :])
            mm.then_inc(S["w_fold_psum"], 1)
            pe.wait_ge(S["w_fold_copied"], 1)
            pe.wait_ge(S["idx_s_relu"], 2)
            for lo, w, bank in ((0, BANK, 0), (BANK, BANK, 1), (PAST, DS, 2)):
                for g in range(2):
                    mm = pe.matmul(psum[0:NS, bank, 0:w], w_fold[:, g, :], rel_s[:, g, lo:lo + w],
                                   start=(g == 0), stop=(g == 1))
            mm.then_inc(S["score_s_psum"], 1)
            def step_k(b):
                if b == 0:
                    pe.wait_ge(S["k_in"], 16 * DB * NPG)
                if b >= 2:
                    pe.wait_ge(S["kT_copied"], b - 1)
                for n in range(NPG):
                    mm = tr(psum[:, 4 + 2 * (b % 2) + n // 4, (n % 4) * P:(n % 4 + 1) * P], k_cache[:, b, n, :])
                mm.then_inc(S["kT_psum"], 1)

            pe.wait_ge(S["score_s_copied"], 1)
            step_k(0)
            for b in range(DB):
                if b + 1 < DB:
                    step_k(b + 1)
                pe.wait_ge(S["kT_copied"], b + 1)
                if b == 4:
                    pe.wait_ge(S["log_s_copied"], 1)
                mm = scores_s(b, q_s[:, b].rearrange("p h s -> p (h s)"), kT_s[:, b % 2, :], None)
                if b % 4 == 3:
                    mm.then_inc(S["log_s_psum"], 1)
            pe.wait_ge(S["log_s_copied"], 2)
            pe.wait_ge(S["keys_in"], 16)
            for r in range(RSLOTS):
                if r % 4 == 0 and r == 0:
                    pe.wait_ge(S["kT_copied"], DB)
                mm = tr(psum[:, 4 + r // 4, (r % 4) * P:(r % 4 + 1) * P], keys_nat[:, r, :])
                if r % 4 == 3:
                    mm.then_inc(S["keysT_psum"], 1)
            pe.wait_ge(S["keysT_copied"], 4)
            for t in range(2):
                pe.wait_ge(S["bias_p_ready"], t + 1)
                if t:
                    pe.wait_ge(S["p_exp"], 1)
                for h in range(NH):
                    out = psum[:, h // 2, (h % 2) * SEQ:(h % 2 + 1) * SEQ]
                    pe.matmul(out, qkT[:, h, t * P:(t + 1) * P], qkT[:, NH, 0:SEQ], start=True, stop=False)
                    mm = pe.matmul(out, ident[:, :], bias_p[:, t, :], start=False, stop=True)
                mm.then_inc(S["log_p_psum"], 1)
                pe.wait_ge(S["p_norm"], t + 1)
                for h in range(NH):
                    for kt in range(2):
                        mm = tr(psum[:, 4 + kt, h * P:(h + 1) * P], prob_p[:, h, kt * P:(kt + 1) * P])
                mm.then_inc(S["pT_psum"], 1)
                pe.wait_ge(S["pT_copied"], t + 1)
                if t:
                    pe.wait_ge(S["yb_copied"], 1)
                for h in range(NH):
                    for kt in range(2):
                        mm = pe.matmul(psum[:, 6, h * P:(h + 1) * P], z[:, kt, O_V:O_V + HD],
                                       probT[:, kt * NH + h, :], start=(kt == 0), stop=(kt == 1))
                mm.then_inc(S["yb_psum"], 1)
            pe.wait_ge(S["p_exp"], 2)
            pe.wait_ge(S["yb_copied"], 2)
            for g in range(2):
                pe.wait_ge(S["bias_s_ready"], 1)
                if g:
                    pe.wait_ge(S["s_max"], 1)
                for lo, w, bank in ((0, BANK, 0), (BANK, BANK, 1), (PAST, DS, 2)):
                    mm = pe.matmul(psum[:, bank, 0:w], fold[:, g, :], score_s[:, lo:lo + w], start=True, stop=True)
                mm.then_inc(S["spread_psum"], 1)
                pe.wait_ge(S["pnew_ready"], g + 1)
                if g:
                    pe.wait_ge(S["ys_psum"], 1)
                for n in range(NPG):
                    tr(psum[:, 4 + n // 4, (n % 4) * P:(n % 4 + 1) * P], log_s[:, g, n * P:(n + 1) * P])
                tr(psum[0:NS, 6, 0:P], pnew[:, :]).then_inc(S["sT_psum"], 1)
                pe.wait_ge(S["sT_copied"], g + 1)
                if g == 0:
                    pe.wait_ge(S["v_in"], 16 * DB * NPG)
                for j in range(4):
                    rows = slice(32 * j, 32 * j + NH * DS)
                    out = psum[:, 7, g * P + rows.start:g * P + rows.stop]
                    pe.matmul(out, z[0:NS, 2, O_V:O_V + HD], pnewT[:, rows], start=True, stop=False)
                    for n in range(NPG):
                        mm = pe.matmul(out, v_cache[:, 4 * g + j, n, :], probT[:, n, rows], start=False,
                                       stop=(n == NPG - 1))
                mm.then_inc(S["ys_psum"], 1)
            pe.wait_ge(S["w_o_in"], 16 * KC)
            pe.wait_ge(S["ys_copied"], 2)
            pe.wait_ge(S["s_max"], 2)
            for c in range(KC):
                if c >= 4:
                    pe.wait_ge(S["x1_ready"], c - 3)
                for k in range(KC):
                    mm = pe.matmul(psum[:, c % 4, 0:NT], w_o_sb[:, k, c * P:(c + 1) * P], catT[:, k, :],
                                   start=(k == 0), stop=(k == KC - 1))
                mm.then_inc(S["wo_psum"], 1)
            for c in range(KC):
                pe.wait_ge(S["sq2_ready"], c + 1)
                mm = pe.matmul(psum[:, 4, 0:NT], ones[:, :], sq2[:, c, :], start=(c == 0), stop=(c == KC - 1))
            mm.then_inc(S["ssq2_done"], 1)
            def rq(r):
                w = w_pq_lo if r < RSLOTS // 2 else w_pq_hi
                if r == 0:
                    pe.wait_ge(S["w_pq_lo_in"], 16 * KC)
                    pe.wait_ge(S["x1_ready"], KC)
                if r == RSLOTS // 2:
                    pe.wait_ge(S["w_pq_hi_in"], 16 * KC)
                if r >= 2:
                    pe.wait_ge(S["rq_copied"], r - 1)
                c = r % (RSLOTS // 2)
                for k in range(KC):
                    if r == 0:
                        pe.wait_ge(S["h2_ready"], k + 1)
                    mm = pe.matmul(psum[:, r % 2, 0:NT], w[:, k, c * P:(c + 1) * P], h2[:, k, :],
                                   start=(k == 0), stop=(k == KC - 1))
                mm.then_inc(S["rq_psum"], 1)

            def rs(r):
                pe.wait_ge(S["rq_copied"], r + 1)
                if r == 0:
                    pe.wait_ge(S["rstd2_half"], 1)
                q4 = r // 4
                if r % 4 == 0 and r >= 4:
                    pe.wait_ge(S["rs_copied"], q4)
                for t in range(2):
                    pe.matmul(psum[:, 4 + t, (r % 4) * NK:(r % 4 + 1) * NK], q_ring[:, r % 2, t * P:(t + 1) * P],
                              keysT[:, r, :], start=True, stop=True)
                mm = pe.matmul(psum[32 * q4:32 * q4 + 32, 6, (r % 4) * NK:(r % 4 + 1) * NK],
                               q_ring[:, r % 2, SEQ:NT], keysT[:, r, :], start=True, stop=True,
                               skip_group_check=True, tile_position=(0, 32 * q4))
                mm.then_inc(S["rs_psum"], 1)

            rq(0)
            for r in range(RSLOTS):
                if r + 1 < RSLOTS:
                    rq(r + 1)
                rs(r)
            for t in range(3):
                pe.wait_ge(S["slots_ready"], t + 1)
                if t:
                    pe.wait_ge(S["slots_copied"], t)
                m = P if t < 2 else 2 * TK
                for a in range(3):
                    mm = tr(psum[0:m, 7, a * P:(a + 1) * P],
                            slots[:, a].rearrange("p h k -> p (h k)")[:, 0:m])
                mm.then_inc(S["slots_psum"], 1)
            pe.wait_ge(S["slots_copied"], 3)
            pe.wait_ge(S["h_split_lo"], 1)

            def spread(slot, n, bank0):
                pe.wait_ge(S["j_ready"], n + 1)
                pe.wait_ge(S["i_ready"], n + 1)
                for b in range(NB):
                    mm = pe.matmul(psum[:, bank0 + b // 5, (b % 5) * 96:(b % 5) * 96 + 96], j_hot[:, slot, :, b],
                                   i_hot[:, slot, :, :, b], start=True, stop=True, skip_group_check=True)
                mm.then_inc(S["g_psum"], 1)

            spread(0, 0, 4)
            spread(1, 1, 6)
            with pe.Fori(1, PH // 2) as m:
                for s in range(2):
                    pe.wait_ge(S["g_copied"], 2 * m + (s - 1))
                    spread(s, 2 * m + s, 4 + 2 * s)
            pe.wait_ge(S["g_copied"], PH)
            pe.wait_ge(S["h_split_lo"], 1)

            def transpose_u(slot, count):
                pe.wait_ge(u_in[slot], 16 * count)
                for c in range(KC):
                    mm = tr(psum[:, 4 + c // 4, (c % 4) * P:(c % 4 + 1) * P], u_raw[:, slot, c * P:(c + 1) * P])
                mm.then_inc(S["tr_done"], 1)

            def prod_u(slot, n, start):
                pe.wait_ge(S["uT_hi_ready"], n + 1)
                pe.wait_ge(S["uT_lo_ready"], n + 1)
                if not start:
                    pe.wait_ge(S["act_ready"], n - 1)
                i = 0
                for c in range(KC):
                    for a, b in ((uT_hi, h_hi), (uT_hi, h_lo), (uT_lo, h_hi)):
                        mm = pe.matmul(psum[:, 2 + slot % 2, 0:NT], a[:, slot % 2, c, :], b[:, c, :],
                                       start=(i == 0), stop=(i == 3 * KC - 1))
                        i += 1
                mm.then_inc(S["a_done"], 1)

            def prod_v(s, n, start):
                pe.wait_ge(S["ag_lo_ready"], n - s % 2)
                for i in range(4):
                    c = 4 * (s % 2) + i
                    if not (start and s % 2 == 0 and i < 2):
                        pe.wait_ge(S["y_added"], 4 * n + (i - 9))
                    k = 0
                    for slot in ((s + 2) // 2 * 2 % 4, (s + 2) // 2 * 2 % 4 + 1):
                        for a, b in ((v_hi, ag_hi), (v_hi, ag_lo), (v_lo, ag_hi)):
                            mm = pe.matmul(psum[:, i % 2, 0:NT], a[:, slot, c * P:(c + 1) * P], b[:, slot, :],
                                           start=(k == 0), stop=(k == 5))
                            k += 1
                    mm.then_inc(S["y_psum"], 1)

            def quad(q, ph, start=False, stop=False):
                spreads = ph < NU // PH - 1
                for s in range(4):
                    n = 4 * q + s
                    if not (stop and s == 3):
                        pe.wait_ge(S["uT_hi_ready"], n + 1)
                        pe.wait_ge(S["uT_lo_ready"], n + 1)
                        transpose_u((s + 1) % 2, 2 * q + 1 + (s + 1) // 2)
                    prod_u(s, n, start and s < 2)
                    if spreads:
                        pe.wait_ge(S["g_copied"], n + PH)
                        spread(s % 2, n + PH, 6)
                    if not (start and s < 2):
                        prod_v(s, n, start and s == 2)

            transpose_u(0, 1)
            phases(pe, quad)
            for s in range(2):
                prod_v(s, NU + s, False)
            pe.wait_ge(S["y_added"], 4 * NU)
            for t, (t0, n) in enumerate(TILES):
                if t:
                    pe.wait_ge(S["yn_copied"], t)
                for c in range(KC):
                    mm = tr(psum[0:n, 6 + c // 4, (c % 4) * P:(c % 4 + 1) * P], xT[:, c, t0:t0 + n])
                mm.then_inc(S["yn_psum"], 1)

        @block.scalar
        def _(act):
            def copy(out, in_):
                return act.activation(out, in_, ACT.Copy)

            for c in range(KC):
                act.wait_ge(S["xT_psum"], c + 1)
                copy(xT[:, c, :], psum[:, c % 4, 0:NT])
                act.activation(sq[:, c, :], psum[:, c % 4, 0:NT], ACT.Square).then_inc(S["sq_ready"], 1)
            act.wait_ge(S["gains_psum"], 1)
            copy(gains[:, :], psum[:, 5, 0:2 * KC + NG])
            copy(gain5[:, 0:NH, :], bc(psum[:, 6, 0:HD], 1, NH))
            copy(gain5[:, NH, :], psum[:, 6, HD:2 * HD]).then_inc(S["gains_copied"], 1)
            act.wait_ge(S["rstd_half"], 1)
            act.activation(rstd_a[:, :], rstd_b[:, :], ACT.Sqrt).then_inc(S["rstd_root"], 1)
            for t, (t0, n) in enumerate(TILES):
                act.wait_ge(S["z_done"], t + 1)
                for j in range(4):
                    w = min(BANK, IN_W - BANK * j)
                    a = copy(z[0:n, t, BANK * j:BANK * j + w], psum[0:n, 4 * (t % 2) + j, 0:w])
                a.then_inc(S["z_copied"], 1)
                act.wait_ge(S["head_var"], t + 1)
                act.activation(small[0:n, 16:16 + NH + 1], small[0:n, 8:8 + NH + 1], ACT.Sqrt
                               ).then_inc(S["head_root"], 1)
            for t, (t0, n) in enumerate(TILES):
                act.wait_ge(S["heads_psum"], t + 1)
                q_ps = psum[:, 4, 0:NH * n].rearrange("p (h t) -> p h t", h=NH)
                iq_ps = psum[0:ID, 6:8, 0:4 * n].rearrange("p a (h t) -> p a h t", h=4)
                copy(qkT[:, NH, t0:t0 + n], psum[:, 5, 0:n])
                if t < 2:
                    copy(qkT[:, 0:NH, t0:t0 + n], q_ps)
                    for a in range(2):
                        copy(iqT[:, 4 * a:4 * a + 4, t0:t0 + n], iq_ps[:, a])
                    copy(iqT[:, IH, t0:t0 + n], psum[0:ID, 5, n:2 * n]).then_inc(S["heads_copied"], 1)
                else:
                    for h in range(NH):
                        for r in (h, h + NH):
                            copy(q_s[:, :, r, :], q_ps[:, h].rearrange("p (b s) -> p b s", b=DB))
                    for h in range(IH):
                        copy(iq_s[:, :, h, :], iq_ps[:, h // 4, h % 4].rearrange("p (b s) -> p b s", b=DB))
                    copy(ik_new[:, :], psum[0:ID, 5, n:2 * n]).then_inc(S["heads_copied"], 1)
            for g in range(NG):
                act.wait_ge(S["pool_d_psum"], g + 1)
                copy(dT[:, g, :], psum[:, 4 + g, 0:NT]).then_inc(S["pool_d_copied"], 1)
            for g in range(NG):
                act.wait_ge(S["pool_y_psum"], g + 1)
                act.activation(catT[:, g, :], psum[:, 4 + g, 0:NT], ACT.Copy,
                               scale=gains[:, 2 * KC + g:2 * KC + g + 1]).then_inc(S["pool_y_copied"], 1)
            for t in range(2):
                act.wait_ge(S["idx_psum"], t + 1)
                if t:
                    act.wait_ge(S["idx_summed"], 1)
                a = act.activation(rel_p[:].rearrange("p h k -> p (h k)"),
                                   psum[:, 0:4, :].rearrange("p a b -> p (a b)"), ACT.Relu)
                a.then_inc(S["idx_relu"], 1)
            for b in range(DB):
                act.wait_ge(S["ikT_psum"], b + 1)
                if b >= 4 and b % 4 == 2 or b == 2:
                    pass
                lo = 4 + 2 * (b % 2)
                copy(ikT[:, b % 2, 0:PAST], psum[0:ID, lo:lo + 2, :].rearrange("p a b -> p (a b)"))
                copy(ikT[:, b % 2, PAST:KEYS], ik_new[:, b * DS:(b + 1) * DS]).then_inc(S["ikT_copied"], 1)
                if b % 4 == 3:
                    g = b // 4
                    act.wait_ge(S["idx_s_psum"], g + 1)
                    act.activation(rel_s[:, g, 0:PAST], psum[:, 0:2, :].rearrange("p a b -> p (a b)"), ACT.Relu)
                    act.activation(rel_s[:, g, PAST:KEYS], psum[:, 2, 0:DS], ACT.Relu
                                   ).then_inc(S["idx_s_relu"], 1)
            act.wait_ge(S["w_fold_psum"], 1)
            copy(w_fold[:].rearrange("p a b -> p (a b)"), psum[:, 3, 0:2 * NS]).then_inc(S["w_fold_copied"], 1)
            act.wait_ge(S["score_s_psum"], 1)
            copy(score_s[:, 0:PAST], psum[0:NS, 0:2, :].rearrange("p a b -> p (a b)"))
            copy(score_s[:, PAST:KEYS], psum[0:NS, 2, 0:DS]).then_inc(S["score_s_copied"], 1)
            for b in range(DB):
                act.wait_ge(S["kT_psum"], b + 1)
                lo = 4 + 2 * (b % 2)
                copy(kT_s[:, b % 2, 0:PAST], psum[:, lo:lo + 2, :].rearrange("p a b -> p (a b)"))
                copy(kT_s[:, b % 2, PAST:KEYS], qkT[:, NH, SEQ + b * DS:SEQ + (b + 1) * DS]
                     ).then_inc(S["kT_copied"], 1)
                if b % 4 == 3:
                    g = b // 4
                    act.wait_ge(S["log_s_psum"], g + 1)
                    copy(log_s[:, g, 0:PAST], psum[:, 0:2, :].rearrange("p a b -> p (a b)"))
                    copy(log_s[:, g, PAST:KEYS], psum[:, 2, 0:DS]).then_inc(S["log_s_copied"], 1)
            for r in range(4):
                act.wait_ge(S["keysT_psum"], r + 1)
                copy(keysT[:, 4 * r:4 * r + 4, :].rearrange("p a b -> p (a b)"), psum[:, 4 + r, :]
                     ).then_inc(S["keysT_copied"], 1)
            for t in range(2):
                act.wait_ge(S["p_max"], t + 1)
                for h in range(NH):
                    a = act.activation(prob_p[:, h, :], psum[:, h // 2, (h % 2) * SEQ:(h % 2 + 1) * SEQ], ACT.Exp,
                                       bias=small[:, 28 + h:29 + h], scale=SC, accum_out=small[:, 32 + h:33 + h])
                a.then_inc(S["p_exp"], 1)
                act.wait_ge(S["pT_psum"], t + 1)
                copy(probT[:].rearrange("p a b -> p (a b)"), psum[:, 4:6, :].rearrange("p a b -> p (a b)")
                     ).then_inc(S["pT_copied"], 1)
                act.wait_ge(S["yb_psum"], t + 1)
                copy(catT[:, NG:NG + NH, t * P:(t + 1) * P], psum[:, 6, :].rearrange("p (h t) -> p h t", h=NH)
                     ).then_inc(S["yb_copied"], 1)
            for g in range(2):
                act.wait_ge(S["s_max"], g + 1)
                act.activation(log_s[:, g, :], log_s[:, g, :], ACT.Exp, bias=small[:, 41:42], scale=SC,
                               accum_out=small[:, 42:43]).then_inc(S["s_exp"], 1)
                act.wait_ge(S["sT_psum"], g + 1)
                if g:
                    act.wait_ge(S["ys_psum"], 1)
                copy(probT[:].rearrange("p a b -> p (a b)"), psum[:, 4:6, :].rearrange("p a b -> p (a b)"))
                copy(pnewT[:, :], psum[0:NS, 6, 0:P]).then_inc(S["sT_copied"], 1)
                act.wait_ge(S["ys_psum"], g + 1)
                ys = psum[:, 7, g * P:(g + 1) * P].rearrange("p (j h s) -> p j h s", j=4, s=DS)
                for h in range(NH):
                    c0 = SEQ + g * 4 * DS
                    a = copy(catT[:, NG + h, c0:c0 + 4 * DS].rearrange("p (j s) -> p j s", j=4), ys[:, :, h, :])
                a.then_inc(S["ys_copied"], 1)
            for c in range(KC):
                act.wait_ge(S["x1_ready"], c + 1)
                act.activation(sq2[:, c, :], xT[:, c, :], ACT.Square).then_inc(S["sq2_ready"], 1)
            act.wait_ge(S["rstd2_half"], 1)
            act.activation(rstd_a[:, :], rstd_b[:, :], ACT.Sqrt).then_inc(S["rstd2_root"], 1)
            act.wait_ge(S["rows_out"], 16 * (9 + 1 + DB))
            for r in range(RSLOTS):
                act.wait_ge(S["rq_psum"], r + 1)
                if r >= 2:
                    act.wait_ge(S["rs_psum"], r - 1)
                copy(q_ring[:, r % 2, :], psum[:, r % 2, 0:NT]).then_inc(S["rq_copied"], 1)
                if r % 4 == 0 and r:
                    rs_copy(act, copy, r // 4 - 1)
            rs_copy(act, copy, 3)
            act.wait_ge(S["h2_ready"], KC)
            copy(h_hi[:], h2[:]).then_inc(S["h_split"], 1)
            for t in range(3):
                act.wait_ge(S["rexp_in"], t + 1)
                H = RH if t < 2 else 2
                act.activation(slots[:, 2, 0:H], slots[:, 2, 0:H], ACT.Exp).then_inc(S["rexp_out"], 1)
                act.wait_ge(S["slots_psum"], t + 1)
                if t < 2:
                    for i, dst in enumerate((iT, jT, wT)):
                        a = copy(dst[:, t * P:(t + 1) * P], psum[:, 7, i * P:(i + 1) * P])
                else:
                    for j in range(4):
                        for i, dst in enumerate((iT, jT, wT)):
                            a = copy(dst[32 * j:32 * j + 32, SEQ:NT],
                                     psum[0:32, 7, i * P + 32 * j:i * P + 32 * j + 32])
                a.then_inc(S["slots_copied"], 1)

            def high_u(slot, n, free):
                act.wait_ge(S["tr_done"], n + 1)
                if free:
                    act.wait_ge(S["a_done"], n - 1)
                copy(uT_hi[:, slot % 2].rearrange("p a b -> p (a b)"), psum[:, 4:6, :].rearrange("p a b -> p (a b)")
                     ).then_inc(S["uT_hi_ready"], 1)

            def quad(q, ph, start=False, stop=False):
                for s in range(4):
                    n = 4 * q + s
                    if not (stop and s == 3):
                        high_u(s + 1, n + 1, not (start and s == 0))
                    act.wait_ge(v_tile_in[s], 16 * (q + 1))
                    if not start:
                        act.wait_ge(S["y_psum"], 4 * n - 8)
                    copy(v_hi[:, s, :], v_raw[:, s, :]).then_inc(S["v_hi_ready"], 1)
                    act.wait_ge(S["a_done"], n + 1)
                    if not (start and s < 2):
                        act.wait_ge(S["prod_ready"], n - 1)
                    act.activation(act_g[:, s % 2, :], psum[:, 2 + s % 2, 0:NT], ACT.Gelu
                                   ).then_inc(S["act_ready"], 1)
                    act.wait_ge(S["prod_ready"], n + 1)
                    copy(ag_hi[:, s, :], ag[:, s % 2, :]).then_inc(S["ag_hi_ready"], 1)

            high_u(0, 0, False)
            phases(act, quad)
            for t, (t0, n) in enumerate(TILES):
                act.wait_ge(S["yn_psum"], t + 1)
                copy(y_nat[0:n, t, :], psum[0:n, 6:8, :].rearrange("p a b -> p (a b)")).then_inc(S["yn_copied"], 1)

        @block.gpsimd
        def _(pool):
            steps = [0]

            def settle(ins):
                steps[0] += 1
                ins.then_inc(S["pool_step"], 1)
                pool.wait_ge(S["pool_step"], steps[0])

            pool.memset(ones[:, :], 1.0).then_inc(S["ones_set"], 1)
            for t, (t0, n) in enumerate(TILES):
                pool.wait_ge(S["z_copied"], t + 1)
                if t:
                    pool.wait_ge(S["idx_rope_done"], t)
                x = z[0:n, t, O_IQ:O_IW].rearrange("p (h a d) -> p h a d", a=2, d=ID // 2)
                cos = bc(rope[0:n, t, HD:HD + ID // 2], 1, IH + 1)
                sin = bc(rope[0:n, t, HD + ID // 2:HD + ID], 1, IH + 1)
                tmp = [idx_tmp[0:n, i, :].rearrange("p (h d) -> p h d", h=IH + 1) for i in range(4)]
                pool.tensor_tensor(tmp[0], x[:, :, 0], cos, ALU.mult)
                pool.tensor_tensor(tmp[1], x[:, :, 1], sin, ALU.mult)
                pool.tensor_tensor(tmp[2], x[:, :, 1], cos, ALU.mult)
                settle(pool.tensor_tensor(tmp[3], x[:, :, 0], sin, ALU.mult))
                pool.tensor_tensor(x[:, :, 0], tmp[0], tmp[1], ALU.subtract)
                pool.tensor_tensor(x[:, :, 1], tmp[2], tmp[3], ALU.add)
                pool.tensor_scalar(iw[0:n, t, :], z[0:n, t, O_IW:IN_W], float(IH) ** -0.5, None, ALU.mult
                                   ).then_inc(S["idx_rope_done"], 1)
            pool.wait_ge(S["idx_rope_done"], 3)
            for g in range(2):
                pool.tensor_tensor(fold_iw[:, g, :].rearrange("t (j h s) -> t j h s", j=4, s=DS),
                                   fold[:, g, :].rearrange("t (j h s) -> t j h s", j=4, s=DS),
                                   iw[0:NS, 2, :].unsqueeze(1).unsqueeze(3).to_broadcast([NS, 4, IH, DS]), ALU.mult
                                   ).then_inc(S["fold_iw_ready"], 1)
            pool.wait_ge(S["h_split"], 1)
            pool.tensor_tensor(h_lo[:], h2[:], h_hi[:].bitcast(F32), ALU.subtract).then_inc(S["h_split_lo"], 1)

            def quad(q, ph, start=False, stop=False):
                for s in range(4):
                    n = 4 * q + s
                    pool.wait_ge(S["v_hi_ready"], n + 1)
                    pool.tensor_tensor(v_lo[:, s, :], v_raw[:, s, :], v_hi[:, s, :].bitcast(F32),
                                       ALU.subtract).then_inc(S["v_lo_ready"], 1)
                    pool.wait_ge(S["ag_hi_ready"], n + 1)
                    pool.tensor_tensor(ag_lo[:, s, :], ag[:, s % 2, :], ag_hi[:, s, :].bitcast(F32),
                                       ALU.subtract).then_inc(S["ag_lo_ready"], 1)

            phases(pool, quad)

        @block.vector
        def _(dve):
            steps = [0]

            def settle(ins):
                steps[0] += 1
                ins.then_inc(S["dve_step"], 1)
                dve.wait_ge(S["dve_step"], steps[0])

            def inverse_mean(out, in_, n, half):
                settle(dve.tensor_scalar(out, in_, 1.0 / n, EPS, ALU.mult, ALU.add))
                dve.reciprocal(out, out).then_inc(half, 1)

            dve.wait_ge(S["ssq_done"], 1)
            inverse_mean(rstd_b[:, :], psum[:, 4, 0:NT], D, S["rstd_half"])
            dve.wait_ge(S["rstd_root"], 1)
            dve.wait_ge(S["gains_copied"], 1)
            for c in range(KC):
                dve.scalar_tensor_tensor(hT[:, c, :], xT[:, c, :], gains[:, c:c + 1], rstd_a[:, :], ALU.mult,
                                         ALU.mult).then_inc(S["hT_ready"], 1)
            for t, (t0, n) in enumerate(TILES):
                dve.wait_ge(S["z_copied"], t + 1)
                x = z[0:n, t, O_Q:O_V].rearrange("p (h d) -> p h d", d=HD)
                settle(dve.tensor_tensor(head_sq[0:n], x, x, ALU.mult))
                settle(dve.tensor_reduce(small[0:n, 0:NH + 1], head_sq[0:n], AX, ALU.add))
                inverse_mean(small[0:n, 8:8 + NH + 1], small[0:n, 0:NH + 1], HD, S["head_var"])
                dve.wait_ge(S["head_root"], t + 1)
                settle(dve.tensor_tensor(x, x, bc(small[0:n, 16:16 + NH + 1], 2, HD), ALU.mult))
                settle(dve.tensor_tensor(x, x, gain5[0:n], ALU.mult))
                x = z[0:n, t, O_Q:O_V].rearrange("p (h a d) -> p h a d", a=2, d=HD // 2)
                cos, sin = (bc(rope[0:n, t, o:o + HD // 2], 1, NH + 1) for o in (0, HD // 2))
                tmp = [rope_tmp[0:n, i, :].rearrange("p (h d) -> p h d", h=NH + 1) for i in range(4)]
                dve.tensor_tensor(tmp[0], x[:, :, 0], cos, ALU.mult)
                dve.tensor_tensor(tmp[1], x[:, :, 1], sin, ALU.mult)
                dve.tensor_tensor(tmp[2], x[:, :, 1], cos, ALU.mult)
                settle(dve.tensor_tensor(tmp[3], x[:, :, 0], sin, ALU.mult))
                dve.tensor_tensor(x[:, :, 0], tmp[0], tmp[1], ALU.subtract)
                dve.tensor_tensor(x[:, :, 1], tmp[2], tmp[3], ALU.add).then_inc(S["rope_done"], 1)

            def take_top(score, work, rounds):
                best = top8[0:score.shape[0], :]
                for r in rounds:
                    left = score if r == 0 else work
                    settle(dve.max(best, left))
                    settle(dve.match_replace(work, best, left, TAKEN))

            for t in range(2):
                dve.wait_ge(S["idx_relu"], t + 1)
                dve.wait_ge(S["idx_rope_done"], 3)
                settle(dve.tensor_scalar(score_p[:, :], rel_p[:, 0, :], iw[:, t, 0:1], None, ALU.mult))
                for h in range(1, IH):
                    ins = dve.scalar_tensor_tensor(score_p[:, :], rel_p[:, h, :], iw[:, t, h:h + 1], score_p[:, :],
                                                   ALU.mult, ALU.add)
                    if h < IH - 1:
                        settle(ins)
                ins.then_inc(S["idx_summed"], 1)
                dve.wait_ge(S["idx_summed"], t + 1)
                settle(dve.tensor_tensor(score_p[:, :], score_p[:, :], causal[:, t, :], ALU.add))
                take_top(score_p[:, :], work_p[:, :], range(KSEL_P // 8))
                settle(dve.tensor_tensor(work_p[:, :], work_p[:, :], score_p[:, :], ALU.is_equal))
                dve.scalar_tensor_tensor(bias_p[:, t, :], work_p[:, :], NEG, causal[:, t, :], ALU.mult, ALU.add
                                         ).then_inc(S["bias_p_ready"], 1)

            dve.wait_ge(S["score_s_copied"], 1)
            settle(dve.tensor_tensor(score_s[:, PAST:KEYS], score_s[:, PAST:KEYS], causal_new[:, :], ALU.add))
            take_top(score_s[:, :], work_s[:, :], range(KSEL_S // 16))

            def soft_p(t):
                dve.wait_ge(S["log_p_psum"], t + 1)
                settle(dve.tensor_reduce(small[:, 24:28], psum[:, 0:2, :].rearrange("p a (h k) -> p (a h) k", h=2),
                                         AX, ALU.max))
                dve.tensor_scalar(small[:, 28:32], small[:, 24:28], -SC, None, ALU.mult).then_inc(S["p_max"], 1)
                dve.wait_ge(S["p_exp"], t + 1)
                settle(dve.reciprocal(small[:, 36:40], small[:, 32:36]))
                dve.tensor_tensor(prob_p[:], prob_p[:], bc(small[:, 36:40], 2, SEQ), ALU.mult
                                  ).then_inc(S["p_norm"], 1)

            soft_p(0)
            take_top(score_s[:, :], work_s[:, :], range(KSEL_S // 16, KSEL_S // 8))
            settle(dve.tensor_tensor(work_s[:, :], work_s[:, :], score_s[:, :], ALU.is_equal))
            settle(dve.tensor_scalar(score_s[:, :], work_s[:, :], NEG, None, ALU.mult))
            dve.tensor_tensor(score_s[:, PAST:KEYS], score_s[:, PAST:KEYS], causal_new[:, :], ALU.add
                              ).then_inc(S["bias_s_ready"], 1)
            soft_p(1)
            for g in range(2):
                dve.wait_ge(S["spread_psum"], g + 1)
                dve.wait_ge(S["log_s_copied"], 2)
                dve.tensor_tensor(log_s[:, g, 0:PAST], log_s[:, g, 0:PAST],
                                  psum[:, 0:2, :].rearrange("p a b -> p (a b)"), ALU.add)
                settle(dve.tensor_tensor(log_s[:, g, PAST:KEYS], log_s[:, g, PAST:KEYS], psum[:, 2, 0:DS], ALU.add))
                settle(dve.tensor_reduce(small[:, 40:41], log_s[:, g, :], AX, ALU.max))
                dve.tensor_scalar(small[:, 41:42], small[:, 40:41], -SC, None, ALU.mult).then_inc(S["s_max"], 1)
                dve.wait_ge(S["s_exp"], g + 1)
                settle(dve.reciprocal(small[:, 43:44], small[:, 42:43]))
                settle(dve.tensor_scalar(log_s[:, g, :], log_s[:, g, :], small[:, 43:44], None, ALU.mult))
                if g:
                    dve.wait_ge(S["sT_psum"], 1)
                dve.tensor_tensor(pnew[:, :].rearrange("p (b s) -> p b s", b=DB), bc(own[:, g, :], 2, DS),
                                  bc(log_s[:, g, PAST:KEYS], 1, DB), ALU.mult).then_inc(S["pnew_ready"], 1)
            for c in range(KC):
                dve.wait_ge(S["wo_psum"], c + 1)
                dve.tensor_tensor(xT[:, c, :], xT[:, c, :], psum[:, c % 4, 0:NT], ALU.add).then_inc(S["x1_ready"], 1)
            dve.wait_ge(S["ssq2_done"], 1)
            inverse_mean(rstd_b[:, :], psum[:, 4, 0:NT], D, S["rstd2_half"])
            dve.wait_ge(S["rstd2_root"], 1)
            for c in range(KC):
                dve.scalar_tensor_tensor(h2[:, c, :], xT[:, c, :], gains[:, KC + c:KC + c + 1], rstd_a[:, :],
                                         ALU.mult, ALU.mult).then_inc(S["h2_ready"], 1)

            settle(dve.tensor_copy(iotab[:, :], iota[:, 0:TK]))
            for t in range(3):
                H = RH if t < 2 else 2
                scores = sr[:, t] if t < 2 else sr_s[:]
                svr, sir = (a[:].rearrange("p h c k -> p (h c) k") for a in (sv, si))
                for r0 in range(0, 2 * H, 4):
                    if t == 0:
                        dve.wait_ge(S["rs_copied"], r0 // 4 + 1)
                    elif t == 2:
                        dve.wait_ge(S["rs_copied"], 4)
                    four = range(4)
                    for i in four:
                        ins = dve.max(svr[:, r0 + i, 0:8], scores[:, r0 + i, :])
                    settle(ins)
                    for i in four:
                        dve.max_index(sir[:, r0 + i, 0:8], svr[:, r0 + i, 0:8], scores[:, r0 + i, :])
                        ins = dve.match_replace(rwork[:, i, :], svr[:, r0 + i, 0:8], scores[:, r0 + i, :], TAKEN)
                    settle(ins)
                    for i in four:
                        ins = dve.max(svr[:, r0 + i, 8:16], rwork[:, i, :])
                    settle(ins)
                    for i in four:
                        ins = dve.max_index(sir[:, r0 + i, 8:16], svr[:, r0 + i, 8:16], rwork[:, i, :])
                settle(ins)
                dve.tensor_copy(sib[:, 0:H], si[:, 0:H])
                for h in range(H):
                    ins = dve.tensor_tensor(cand[:, h], bc(sv[:, h, 0, :], 2, TK), bc(sv[:, h, 1, :], 1, TK), ALU.add)
                settle(ins)
                rw = rwork[:].rearrange("p (a b) k -> p a (b k)", b=2)
                cd = cand[:].rearrange("p h a b -> p h (a b)")
                for h0 in range(0, H, 2):
                    for i in range(2):
                        ins = dve.max(fv[:, h0 + i, 0:8], cd[:, h0 + i, :])
                    settle(ins)
                    for i in range(2):
                        dve.max_index(fi[:, h0 + i, 0:8], fv[:, h0 + i, 0:8], cd[:, h0 + i, :])
                        ins = dve.match_replace(rw[:, i, :], fv[:, h0 + i, 0:8], cd[:, h0 + i, :], TAKEN)
                    settle(ins)
                    for i in range(2):
                        ins = dve.max(fv[:, h0 + i, 8:16], rw[:, i, :])
                    settle(ins)
                    for i in range(2):
                        ins = dve.max_index(fi[:, h0 + i, 8:16], fv[:, h0 + i, 8:16], rw[:, i, :])
                settle(ins)
                if t:
                    dve.wait_ge(S["slots_psum"], t)
                dve.tensor_tensor(slots[:, 2, 0:H], fv[:, 0:H], fv[:, 0:H, 0:1].to_broadcast([P, H, TK]),
                                  ALU.subtract).then_inc(S["rexp_in"], 1)
                dve.tensor_scalar(fab[:, 0, 0:H], fi[:, 0:H], 4, None, ALU.logical_shift_right)
                settle(dve.tensor_scalar(fab[:, 1, 0:H], fi[:, 0:H], TK - 1, None, ALU.bitwise_and))
                dve.tensor_copy(fabb[:, 0, 0:H], fab[:, 0, 0:H])
                settle(dve.tensor_copy(fabb[:, 1, 0:H], fab[:, 1, 0:H]))
                for c in range(2):
                    m = fabb[:, c, 0:H].rearrange("p h k -> p (h k)")
                    settle(dve.tensor_tensor(hit[:, 0:H].rearrange("p h k a -> p (h k) a"), bc(m, 2, TK),
                                             bc(iotab[:, :], 1, H * TK), ALU.is_equal))
                    settle(dve.tensor_tensor(picked[:, 0:H], hit[:, 0:H], bc(sib[:, 0:H, c, :], 2, TK), ALU.mult))
                    dve.tensor_reduce(slots[:, c, 0:H].rearrange("p h k -> p (h k)"),
                                      picked[:, 0:H].rearrange("p h k a -> p (h k) a"), AX, ALU.add)
                dve.wait_ge(S["rexp_out"], t + 1)
                settle(dve.tensor_reduce(ssum[:, 0:H], slots[:, 2, 0:H], AX, ALU.add))
                settle(dve.reciprocal(ssum[:, 0:H], ssum[:, 0:H]))
                dve.tensor_tensor(slots[:, 2, 0:H], slots[:, 2, 0:H], bc(ssum[:, 0:H], 2, TK), ALU.mult
                                  ).then_inc(S["slots_ready"], 1)
            dve.wait_ge(S["slots_copied"], 3)
            settle(dve.tensor_copy(w3[:, 0, :], wT[:, :]))
            settle(dve.tensor_tensor(w_rest[:, :], wT[:, :], w3[:, 0, :], ALU.subtract))
            settle(dve.tensor_copy(w3[:, 1, :], w_rest[:, :]))
            settle(dve.tensor_tensor(w3[:, 2, :], w_rest[:, :], w3[:, 1, :], ALU.subtract))
            settle(dve.tensor_copy(counts[:], bc(iota[:, :], 2, NB)))
            dve.wait_ge(S["h_split_lo"], 1)

            def hits(slot, n, token, ph):
                dve.tensor_tensor(i_eq[:, slot], counts[:, ph * PH:(ph + 1) * PH, :],
                                  bc(iT[:, bass.ds(token, NB)], 1, PH), ALU.is_equal).then_inc(S["i_eq_ready"], 1)
                dve.tensor_tensor(j_hot[:, slot], counts[:], bc(jT[:, bass.ds(token, NB)], 1, P),
                                  ALU.is_equal).then_inc(S["j_ready"], 1)
                dve.wait_ge(S["i_eq_ready"], n + 1)
                dve.tensor_tensor(i_hot[:, slot], bc(i_eq[:, slot], 1, 3), bc(w3[:, :, bass.ds(token, NB)], 2, PH),
                                  ALU.mult).then_inc(S["i_ready"], 1)

            flat_ps = psum[:].rearrange("p a b -> p (a b)")

            def collect(n, bank0, half, token):
                dve.wait_ge(S["g_psum"], n + 1)
                for b0, nb in ((0, 5), (5, 4)):
                    lo = (bank0 + b0 // 5) * BANK
                    parts = flat_ps[:, lo:lo + nb * 96].rearrange("p (b a i) -> p b i a", b=nb, a=3)
                    out = g_ring[:, half * PH:(half + 1) * PH, bass.ds(token + b0, nb)].rearrange("p i b -> p b i")
                    ins = dve.tensor_reduce(out, parts, AX, ALU.add)
                ins.then_inc(S["g_copied"], 1)

            hits(0, 0, 0, 0)
            hits(1, 1, NB, 0)
            with dve.Fori(1, PH // 2) as m:
                for s in range(2):
                    collect(2 * m + (s - 2), 4 + 2 * s, 0, NB * (2 * m + (s - 2)))
                    hits(s, 2 * m + s, NB * (2 * m + s), 0)
            for s in range(2):
                collect(PH - 2 + s, 4 + 2 * s, 0, NB * (PH - 2 + s))

            def low_u(slot, n):
                dve.wait_ge(S["uT_hi_ready"], n + 1)
                dve.tensor_tensor(uT_lo[:, slot % 2].rearrange("p a b -> p (a b)"), flat_ps[:, 4 * BANK:6 * BANK],
                                  uT_hi[:, slot % 2].rearrange("p a b -> p (a b)").bitcast(F32), ALU.subtract
                                  ).then_inc(S["uT_lo_ready"], 1)

            def add_y(s, n):
                for i in range(4):
                    c = 4 * (s % 2) + i
                    dve.wait_ge(S["y_psum"], 4 * n + (i - 7))
                    dve.tensor_tensor(xT[:, c, :], xT[:, c, :], psum[:, i % 2, 0:NT], ALU.add
                                      ).then_inc(S["y_added"], 1)

            def quad(q, ph, start=False, stop=False):
                spreads = ph < NU // PH - 1
                for s in range(4):
                    n = 4 * q + s
                    in_ph = n - ph * PH
                    if spreads:
                        dve.wait_ge(S["g_psum"], n + PH - 1)
                        hits(s % 2, n + PH, NB * in_ph, ph + 1)
                    if not (stop and s == 3):
                        low_u(s + 1, n + 1)
                    dve.wait_ge(S["act_ready"], n + 1)
                    if not (start and s < 2):
                        dve.wait_ge(S["ag_lo_ready"], n - 1)
                    dve.wait_ge(S["g_copied"], n + PH if spreads else NU)
                    dve.tensor_tensor(ag[:, s % 2, :], act_g[:, s % 2, :],
                                      g_ring[:, bass.ds(in_ph + (ph % 2) * PH, 1), :].rearrange("p a t -> p (a t)"),
                                      ALU.mult).then_inc(S["prod_ready"], 1)
                    if not (start and s < 2):
                        add_y(s, n)
                    if spreads:
                        collect(n + PH, 6, (ph + 1) % 2, NB * in_ph)

            low_u(0, 0)
            phases(dve, quad)
            for s in range(2):
                add_y(s, NU + s)
    ctx.close()


_INS = ["x_prompt", "x_sample", "cache_k", "cache_v", "cache_ik", "state_pool", "page_table", "norm1_g", "w_in",
        "q_norm_g", "k_norm_g", "w_pool", "pool_scale", "w_o", "norm2_g", "w_pq", "sub_keys", "expert_u", "expert_v"]


def kernel(**inputs):
    import concourse.bacc as bacc
    from concourse.bass_utils import run_bass_kernel_spmd

    nc = bacc.Bacc("TRN2", target_bir_lowering=False, num_devices=1)
    a = {n: np.ascontiguousarray(inputs[n]) for n in _INS}
    _, SEQ, D = a["x_prompt"].shape
    DB, DS, _ = a["x_sample"].shape
    HD, ID = a["cache_k"].shape[3], a["cache_ik"].shape[3]
    NST, PW = a["state_pool"].shape[2:]
    IH = (a["w_in"].shape[2] - PW - (D - PW) - 2 * HD - ID) // (ID + 1)
    PAST = a["page_table"].shape[1] * a["cache_k"].shape[2]
    a.update(shape_constants(SEQ, DB, DS, PAST, (D - PW) // HD, HD, IH, ID, NST))
    outs = [("y_prompt", (1, SEQ, D)), ("y_sample", (DB, DS, D)),
            ("k_prompt", (1, 1, SEQ, HD)), ("v_prompt", (1, 1, SEQ, HD)), ("ik_prompt", (1, 1, SEQ, ID)),
            ("pool_prompt", (1, 1, NST, PW)), ("k_sample", (1, DB, DS, HD)), ("v_sample", (1, DB, DS, HD)),
            ("ik_sample", (1, DB, DS, ID)), ("pool_sample", (1, DB, NST, PW))]
    args = {n: nc.dram_tensor(n, v.shape, mybir.dt.from_np(v.dtype), kind="ExternalInput").ap() for n, v in a.items()}
    for n, shape in outs:
        args[n] = nc.dram_tensor(n, shape, F32, kind="ExternalOutput").ap()
    hybrid_kernel(nc, **args)
    r = run_bass_kernel_spmd(nc, [a], core_ids=[0])
    return tuple(r.results[0][n] for n, _ in outs)
```

```python
from contextlib import ExitStack

import numpy as np

import concourse.bass as bass
from concourse import mybir

ALU = mybir.AluOpType
ACT = mybir.ActivationFunctionType
AX = mybir.AxisListType.X
F32 = mybir.dt.float32
F32R = mybir.dt.float32r
BF16 = mybir.dt.bfloat16
I32 = mybir.dt.int32
U32 = mybir.dt.uint32
P = 128
BANK = 512
EPS = 1e-6
THETA = 10000.0
NEG = -1e30
TAKEN = -3e38
WINDOWS = (2, 4, 8, 16)


def shape_constants(SEQ, DB, DS, PAST, NH, HD, IH, ID, NST):
    NT = SEQ + DB * DS
    pos = np.concatenate([np.arange(SEQ), np.tile(PAST + np.arange(DS), DB)]).astype(np.float32)
    tabs = []
    for dim in (HD, ID):
        half = dim // 2
        inv = (np.float32(THETA) ** (-np.arange(half, dtype=np.float32) / np.float32(half))).astype(np.float32)
        ang = pos[:, None] * inv[None, :]
        tabs += [np.cos(ang), np.sin(ang)]
    rope = np.concatenate(tabs, axis=1).astype(np.float32)
    NW = len(WINDOWS)
    band = np.zeros((SEQ, NW, SEQ), np.float32)
    band_state = np.zeros((DB * NST, NW, DB * DS), np.float32)
    band_new = np.zeros((DB * DS, NW, DB * DS), np.float32)
    for g, w in enumerate(WINDOWS):
        for t in range(SEQ):
            lo = max(0, t + 1 - w)
            band[lo:t + 1, g, t] = 1.0 / min(t + 1, w)
            band[t, g, t] -= 1.0
        for b in range(DB):
            for s in range(DS):
                for r in range(NST + s + 1 - w, NST + s + 1):
                    if r < NST:
                        band_state[b * NST + r, g, b * DS + s] = 1.0 / w
                    else:
                        band_new[b * DS + r - NST, g, b * DS + s] = 1.0 / w
                band_new[b * DS + s, g, b * DS + s] -= 1.0
    causal = np.where(np.arange(SEQ)[None, :] <= np.arange(SEQ)[:, None], 0.0, NEG).astype(np.float32)
    causal_new = np.where(np.arange(DS)[None, :] <= (np.arange(DB * DS) % DS)[:, None], 0.0, NEG).astype(np.float32)
    fold = np.zeros((DB * DS, DB // 4, P), np.float32)
    own = np.zeros((P, DB // 4, DB), np.float32)
    for g in range(DB // 4):
        for j in range(4):
            for h in range(IH):
                for s in range(DS):
                    row = 32 * j + h * DS + s
                    fold[(4 * g + j) * DS + s, g, row] = 1.0
                    own[row, g, 4 * g + j] = 1.0
    iota = np.tile(np.arange(P, dtype=np.float32)[None], (P, 1))
    return dict(c_rope=rope, c_band=band, c_band_state=band_state, c_band_new=band_new, c_causal=causal,
                c_causal_new=causal_new, c_fold=fold, c_own=own, c_ident=np.eye(P, dtype=np.float32), c_iota=iota)


class Named(dict):

    def __init__(self, nc, ctx):
        self.nc, self.ctx = nc, ctx

    def __missing__(self, name):
        self[name] = self.ctx.enter_context(self.nc.semaphore(name))
        return self[name]


def hybrid_kernel(nc, x_prompt, x_sample, cache_k, cache_v, cache_ik, state_pool, page_table,
                  norm1_g, w_in, q_norm_g, k_norm_g, w_pool, pool_scale, w_o, norm2_g, w_pq, sub_keys,
                  expert_u, expert_v, c_rope, c_band, c_band_state, c_band_new, c_causal, c_causal_new,
                  c_fold, c_own, c_ident, c_iota,
                  y_prompt, y_sample, k_prompt, v_prompt, ik_prompt, pool_prompt,
                  k_sample, v_sample, ik_sample, pool_sample):
    SEQ, D = x_prompt.shape[1:]
    DB, DS = x_sample.shape[:2]
    HD, ID = cache_k.shape[3], cache_ik.shape[3]
    PAGE = cache_k.shape[2]
    NPOOL = cache_k.shape[1]
    NPG = page_table.shape[1]
    PAST = NPG * PAGE
    NST, PW = state_pool.shape[2:]
    NG = w_pool.shape[1]
    NH = (D - PW) // HD
    RH = sub_keys.shape[1]
    NK = sub_keys.shape[3]
    IN_W = w_in.shape[2]
    IH = (IN_W - PW - NH * HD - 2 * HD - ID) // (ID + 1)
    TK = 16
    KC = D // P
    NS = DB * DS
    NT = SEQ + NS
    TILES = ((0, P), (P, P), (SEQ, NS))
    KEYS = PAST + DS
    KSEL_P = min(256, SEQ // 4)
    KSEL_S = min(256, KEYS // 4)
    SC = float(HD) ** -0.5
    RSLOTS = 2 * RH
    O_Q, O_K = PW, PW + NH * HD
    O_V = O_K + HD
    O_IQ = O_V + HD
    O_IK = O_IQ + IH * ID
    O_IW = O_IK + ID
    assert SEQ == 2 * P and NS == 32 and D == 8 * P and PAGE == P and HD == P and NK == P and NG == 4
    assert DS == 4 and DB == 8 and IH == 8 and ID == 64 and NH == 4 and RH == 8 and NPG == 8

    ctx = ExitStack()
    psum = ctx.enter_context(nc.psum_tensor("psum", [P, 8, BANK], F32))

    base = (nc.sbuf_base + 63) // 64 * 64
    WORDS = (nc.sbuf_usable_end // 4) - base // 4 - 8

    def at(name, off, shape, dt=F32):
        n = int(np.prod(shape[1:])) * (2 if dt == BF16 else 4)
        assert off * 4 + n <= WORDS * 4, (name, off, n, WORDS)
        return nc.alloc_sbuf_tensor_at(name, shape, dt, offset=base + off * 4)

    cur = [0]

    def take(name, shape, dt=F32):
        n = (int(np.prod(shape[1:])) * (2 if dt == BF16 else 4) + 31) // 32 * 8
        t = at(name, cur[0], shape, dt)
        cur[0] += n
        return t

    ident = take("ident", [P, P])
    iota = take("iota", [P, P])
    ones = take("ones", [P, P])
    xT = take("xT", [P, KC, NT])
    gains = take("gains", [P, 2 * KC + NG])
    NU, PH = NK, 32
    NB = NT // PH
    iT = take("iT", [P, NT], BF16)
    jT = take("jT", [P, NT], BF16)
    wT = take("wT", [P, NT])
    w_rest = take("w_rest", [P, NT])
    w3 = take("w3", [P, 3, NT], BF16)
    counts = take("counts", [P, P, NB], BF16)
    small = take("small", [P, 64])
    top8 = take("top8", [P, 8])
    F0 = cur[0]

    k_cache = take("k_cache", [P, DB, NPG, HD])
    w_o_sb = at("w_o_sb", F0, [P, KC, D])
    w_pq_hi = at("w_pq_hi", F0, [P, KC, D])
    W0 = cur[0]
    w_in_sb = take("w_in_sb", [P, KC, IN_W])
    Z0 = cur[0]
    v_cache = at("v_cache", W0, [P, DB, NPG, HD])
    w_pq_lo = at("w_pq_lo", W0, [P, KC, D])
    W1 = W0 + DB * NPG * HD
    cur[0] = W1
    ikT = at("ikT", W0, [ID, DB, PAST])
    rel_p = take("rel_p", [P, IH, SEQ])
    score_p = take("score_p", [P, SEQ])
    work_p = take("work_p", [P, SEQ])
    bias_p = take("bias_p", [P, 2, SEQ])
    causal = take("causal", [P, 2, SEQ])
    band = at("band", cur[0], [P, 2, NG, SEQ])
    ys_rows = at("ys_rows", W1, [P, 2, HD])
    wo_rows = at("wo_rows", W1 + 2 * HD, [P, D // 4])
    prob_p = take("prob_p", [P, NH, SEQ])
    probT = take("probT", [P, NPG, P])
    probT_s = take("probT_s", [P, NPG, P])
    assert cur[0] <= Z0
    cur[0] = Z0
    z = take("z", [P, 3, IN_W])
    A0 = cur[0]
    x_nat = at("x_nat", A0, [P, 3, D])
    keysT = at("keysT", A0, [P, RSLOTS, NK])
    keys_nat = at("keys_nat", A0 + RSLOTS * NK, [P, RSLOTS, HD])
    w_pool_sb = at("w_pool_sb", A0 + RSLOTS * NK, [P, NG, P])
    state_sb = at("state_sb", A0 + RSLOTS * NK + NG * P, [DB * NST, PW])
    ik_cache = take("ik_cache", [P, DB, NPG, ID])
    A1 = cur[0]
    iqT = at("iqT", A1, [64, IH + 1, SEQ])
    log_s = at("log_s", A1, [P, 2, KEYS])
    h2 = at("h2", A1, [P, KC, NT])
    sq = take("sq", [P, KC, NT])
    A2 = cur[0]
    catT = at("catT", A2, [P, KC, NT])
    hT = take("hT", [P, KC, NT])
    A3 = cur[0]
    gain_rows = at("gain_rows", A3, [2 * KC + NG, P])
    head_gain = at("head_gain", A3 + P, [1, 2, HD])
    rope_tmp = at("rope_tmp", A3, [P, 4, (NH + 1) * HD // 2])
    head_sq = at("head_sq", A3 + 2 * (NH + 1) * HD, [P, NH + 1, HD])
    kT_s = at("kT_s", A3, [P, 4, PAST])
    sq2 = at("sq2", A3, [P, KC, NT])
    band_new = at("band_new", A3 + 3 * (NH + 1) * HD, [NS, NG, NS])
    cur[0] += 2 * KEYS
    assert 3 * (NH + 1) * HD + NG * NS <= 2 * KEYS
    A4 = cur[0]
    idx_tmp = at("idx_tmp", A4 + 2 * KEYS, [P, 4, (IH + 1) * ID // 2])
    dT = at("dT", A4, [P, NG, NT])
    rel_s = take("rel_s", [P, 2, KEYS])
    score_s = take("score_s", [NS, KEYS])
    work_s = take("work_s", [NS, KEYS])
    qkT = take("qkT", [P, NH + 1, NT])
    q_s = take("q_s", [P, DB, 8, DS])
    iq_s = take("iq_s", [64, DB, IH, DS])
    ik_new = take("ik_new", [64, NS])
    gain5 = take("gain5", [P, NH + 1, HD])
    rope = take("rope", [P, 3, HD + ID])
    causal_new = take("causal_new", [NS, DS])
    fold = take("fold", [NS, 2, P])
    own = take("own", [P, 2, DB])
    fold_iw = take("fold_iw", [NS, 2, P])
    w_fold = take("w_fold", [P, 2, NS])
    pnew = take("pnew", [P, 2, NS])
    pnewT = take("pnewT", [NS, 2, P])
    rstd_a = take("rstd_a", [P, NT])
    rstd_b = take("rstd_b", [P, NT])
    pages = take("pages", [1, DB * NPG], I32)
    iw = take("iw", [P, 3, IH])
    fold16 = at("fold16", A4 + 13 * P, [NS, 2, P], BF16)
    bias_s = at("bias_s", A4 + 4 * P, [NS, KEYS], BF16)
    band_state = take("band_state", [DB * NST, NG, NS])

    sr = at("sr", Z0, [P, 2, RSLOTS, NK])
    assert Z0 + 2 * RSLOTS * NK <= A0
    cur[0] = W1
    hit = take("hit", [P, TK, RH * TK], BF16)
    picked = take("picked", [P, TK, RH * TK], BF16)
    half_sum = take("half_sum", [P, TK // 2, RH * TK], BF16)
    ranks = take("ranks", [P, TK, RH * TK], BF16)
    cand = take("cand", [P, 2, 2, TK, TK])
    slots = take("slots", [P, 3, 3, RH, TK])
    assert cur[0] <= Z0
    cur[0] = A2
    q_ring = take("q_ring", [P, 2, NT])
    sr_s = take("sr_s", [P, 4, NK])
    rwork = take("rwork", [P, 2, 4, NK])
    sv = take("sv", [P, 3, RSLOTS, TK])
    si = take("si", [P, 3, RSLOTS, TK], U32)
    sib = take("sib", [P, 3, RSLOTS, TK], BF16)
    fv = take("fv", [P, 3, RH, TK])
    fi = take("fi", [P, 3, RH, TK], U32)
    fab = take("fab", [P, 2, RH * TK], U32)
    fabb = take("fabb", [P, 2, RH * TK], BF16)
    ssum = take("ssum", [P, RH])
    ROUTE_END = cur[0]

    cur[0] = F0
    u_raw = take("u_raw", [P, 2, D])
    uT_hi = take("uT_hi", [P, 2, KC, P], F32R)
    uT_lo = take("uT_lo", [P, 2, KC, P], F32R)
    g_odd = take("g_odd", [P, PH, PH, NB])
    uT_raw = at("uT_raw", cur[0], [P, KC, P])
    assert cur[0] + D <= W1
    v_raw = take("v_raw", [P, 4, D])
    g_even = take("g_even", [P, PH, PH, NB])
    g_phase = (g_even, g_odd)
    v_hi = take("v_hi", [P, 4, D], F32R)
    v_lo = take("v_lo", [P, 4, D], F32R)
    j_hot = take("j_hot", [P, 2, P, NB], BF16)
    i_eq = take("i_eq", [P, 2, PH, NB], BF16)
    i_hot = take("i_hot", [P, 2, 3, PH, NB], BF16)
    act_g = take("act_g", [P, 2, NT])
    ag = take("ag", [P, 2, NT])
    ag_hi = take("ag_hi", [P, 4, NT], F32R)
    ag_lo = take("ag_lo", [P, 4, NT], F32R)
    MAIN_END = cur[0]
    assert ROUTE_END <= MAIN_END, (ROUTE_END, MAIN_END)
    h_hi = take("h_hi", [P, KC, NT], F32R)
    h_lo = take("h_lo", [P, KC, NT], F32R)
    y_nat = at("y_nat", F0 + 8 * D, [P, 3, D])

    S = Named(nc, ctx)
    u_in = [ctx.enter_context(nc.semaphore(f"u_in{i}")) for i in range(2)]
    v_tile_in = [ctx.enter_context(nc.semaphore(f"v_tile_in{i}")) for i in range(4)]

    def bc(ap, axis, n):
        a = ap.unsqueeze(axis)
        shape = list(a.shape)
        shape[axis] = n
        return a.to_broadcast(shape)

    QUADS = PH // 4
    EXP_AT = 8
    SLOTS_AT = PH // 2
    u_rows = expert_u.rearrange("a (n p) d -> (a n) p d", p=P)
    v_rows = expert_v.rearrange("a (n p) d -> (a n) p d", p=P)
    gain_loads = [
        (pages[0:1, :], page_table.rearrange("b n -> (b n)").unsqueeze(0)),
        (gain_rows[0:KC, :], norm1_g.rearrange("a (k p) -> (a k) p", p=P)),
        (gain_rows[KC:2 * KC, :], norm2_g.rearrange("a (k p) -> (a k) p", p=P)),
        (gain_rows[2 * KC:2 * KC + NG, :], pool_scale.rearrange("a (k p) -> (a k) p", p=P)),
        (head_gain[0:1, 0, :], q_norm_g), (head_gain[0:1, 1, :], k_norm_g),
    ]
    early_loads = [
        (rope[0:NS, 2, :], c_rope[SEQ:NT, :]), (rope[:, 0:2, :], c_rope[0:SEQ, :].rearrange("(t p) c -> p t c", p=P)),
        (fold[:], c_fold), (causal_new[:], c_causal_new), (own[:], c_own), (iota[:], c_iota),
    ]
    late_loads = [
        (band[:, 0], c_band[0:P]), (band[:, 1], c_band[P:SEQ]), (band_state[:], c_band_state),
        (band_new[:], c_band_new), (w_pool_sb[:], w_pool[0].rearrange("g c n -> c g n")),
        (state_sb[:], state_pool[0].rearrange("b r d -> (b r) d")),
        (causal[:], c_causal.rearrange("(t p) c -> p t c", p=P)),
    ]
    ZQ = IN_W // 4
    ORDER = (2, 0, 1)

    def page_loads(eng, first, cache, dst, width, sem, pages_n):
        with eng.Fori(0, pages_n // 4) as i:
            pg = [eng.value_load(pages[0:1, bass.ds(4 * i + (first + u), 1)], min_val=0, max_val=NPOOL - 1)
                  for u in range(4)]
            for u in range(4):
                eng.dma_start(dst[:, bass.ds((4 * i + (first + u)) * width, width)],
                              cache[0, bass.ds(pg[u], 1), :, :].rearrange("a p d -> (a p) d")).then_inc(sem, 16)

    def ik_loads(eng, g, half):
        page_loads(eng, (4 * g + 2 * half) * NPG, cache_ik, ik_cache[:].rearrange("p b n d -> p (b n d)"), ID,
                   S[f"ik_in{g}"], 2 * NPG)

    def phases(eng, quad):
        last = NU // PH - 1
        for ph in range(last + 1):
            q0, q1 = ph * QUADS, (ph + 1) * QUADS
            if ph == 0:
                quad(q0, ph, start=True)
                q0 += 1
            if ph in (0, last):
                q1 -= 1
            with eng.Fori(q0, q1) as q:
                quad(q, ph)
            if ph in (0, last):
                quad(q1, ph, stop=True)

    def rs_copy(act, copy, q4):
        act.wait_ge(S["rs_psum"], 4 * q4 + 4)
        for t in range(2):
            a = copy(sr[:, t, 4 * q4:4 * q4 + 4, :].rearrange("p a b -> p (a b)"), psum[:, 4 + t, :])
        if q4 == 3:
            a = copy(sr_s[:].rearrange("p a b -> p (a b)"), psum[:, 6, :])
        a.then_inc(S["rs_copied"], 1)

    with nc.Block() as block:
        @block.sync
        def _(sp):
            sp.dma_start(ident[:], c_ident).then_inc(S["ident_in"], 16)
            for t, (t0, n) in enumerate(TILES):
                src = x_prompt[0, t0:t0 + n, :] if t < 2 else x_sample.rearrange("b s d -> (b s) d")
                sp.dma_start(x_nat[0:n, t, :], src).then_inc(S["x_in"], 16)
            sp.wait_ge(S["gains_in"], 16 * len(gain_loads))
            for k in range(KC):
                sp.dma_start(w_in_sb[:, k, :], w_in[0, k * P:(k + 1) * P, :]).then_inc(S[f"w_in_in{k}"], 16)

            sp.wait_ge(S["xT_psum"], KC)
            for g in range(2):
                ik_loads(sp, g, 0)
            page_loads(sp, 0, cache_k, k_cache[:].rearrange("p b n d -> p (b n d)"), HD, S["k_in"], DB * NPG)
            sp.dma_start(pool_sample[0, :, 0:NST - DS, :], state_pool[0, :, DS:NST, :]).then_inc(S["out_done"], 16)
            sp.wait_ge(S["rope_done"], 3)
            sp.wait_ge(S["idx_rope_done"], 3)
            for outs, col, w in ((( k_prompt, k_sample), O_K, HD), ((v_prompt, v_sample), O_V, HD),
                                 ((ik_prompt, ik_sample), O_IK, ID)):
                for t, (t0, n) in enumerate(TILES):
                    dst = outs[0][0, 0, t0:t0 + n, :] if t < 2 else outs[1][0].rearrange("b s d -> (b s) d")
                    sp.dma_start(dst, z[0:n, t, col:col + w]).then_inc(S["rows_out"], 16)
            sp.dma_start(pool_prompt[0, 0], z[P - NST:P, 1, 0:PW]).then_inc(S["rows_out"], 16)
            for b in range(DB):
                sp.dma_start(pool_sample[0, b, NST - DS:NST, :], z[b * DS:(b + 1) * DS, 2, 0:PW]
                             ).then_inc(S["rows_out"], 16)
            sp.wait_ge(S["pool_y_psum"], NG)
            sp.dma_start(keys_nat[:], sub_keys[0].rearrange("h c k d -> k (h c) d")).then_inc(S["keys_in"], 16)
            sp.wait_ge(S["kT_psum"], DB)
            for k in range(KC):
                sp.dma_start(w_o_sb[:, k, :], w_o[0, k * P:(k + 1) * P, :]).then_inc(S["w_o_in"], 16)
            sp.wait_ge(S["ys_psum"], 2)
            for k in range(KC):
                sp.dma_start(w_pq_lo[:, k, :], w_pq[0, k * P:(k + 1) * P, 0:D]).then_inc(S["w_pq_lo_in"], 16)
            sp.wait_ge(S["wo_s_psum"], 1)
            for k in range(KC):
                sp.dma_start(w_pq_hi[:, k, :], w_pq[0, k * P:(k + 1) * P, D:2 * D]).then_inc(S["w_pq_hi_in"], 16)

            def load_u(row, slot):
                sp.dma_start(u_raw[:, slot, :], u_rows[bass.ds(row, 1)].rearrange("a p d -> (a p) d")
                             ).then_inc(u_in[slot], 16)

            def load_v(row, slot):
                sp.dma_start(v_raw[:, slot, :], v_rows[bass.ds(row, 1)].rearrange("a p d -> (a p) d")
                             ).then_inc(v_tile_in[slot], 16)

            sp.wait_ge(S["rq_psum"], RSLOTS)
            for s in range(2):
                load_u(s, s)
            with sp.Fori(0, PH // 2) as m:
                for s in range(2):
                    sp.wait_ge(S["tr_done"], 2 * m + (s + 1))
                    load_u(2 * m + (s + 2), s)
            sp.wait_ge(S["uT_lo_ready"], PH + 1)
            sp.wait_ge(S["w3_ready"], 1)
            for s in range(4):
                load_v(s, s)

            def quad(q, ph, start=False, stop=False):
                end = stop and ph > 0
                for s in range(4):
                    if ph > 0 and not (end and s >= 2):
                        sp.wait_ge(S["tr_done"], 4 * q + (s + 1))
                        load_u(4 * q + (s + 2), s % 2)
                    if not end:
                        sp.wait_ge(S["v_lo_ready"], 4 * q + (s + 1))
                        load_v(4 * q + (s + 4), s)

            phases(sp, quad)

            sp.wait_ge(S["yn_copied"], 3)
            for t, (t0, n) in enumerate(TILES):
                dst = y_prompt[0, t0:t0 + n, :] if t < 2 else y_sample.rearrange("b s d -> (b s) d")
                sp.dma_start(dst, y_nat[0:n, t, :]).then_inc(S["out_done"], 16)
            sp.wait_ge(S["out_done"], 16 * 4)

        @block.tensor
        def _(pe):
            def tr(out, in_):
                n = in_.shape[0]
                return pe.transpose(out, in_, ident[0:n, 0:n])

            pe.wait_ge(S["ident_in"], 16)
            pe.wait_ge(S["x_in"], 48)
            for c in range(KC):
                if c >= 4:
                    pe.wait_ge(S["sq_ready"], c - 3)
                for t, (t0, n) in enumerate(TILES):
                    mm = tr(psum[:, c % 4, t0:t0 + n], x_nat[0:n, t, c * P:(c + 1) * P])
                mm.then_inc(S["xT_psum"], 1)
            pe.wait_ge(S["ones_set"], 1)
            for c in range(KC):
                pe.wait_ge(S["sq_ready"], c + 1)
                mm = pe.matmul(psum[:, 4, 0:NT], ones[:, :], sq[:, c, :], start=(c == 0), stop=(c == KC - 1))
            mm.then_inc(S["ssq_done"], 1)
            pe.wait_ge(S["gains_in"], 16 * len(gain_loads))
            tr(psum[:, 5, 0:2 * KC + NG], gain_rows[:, :])
            pe.matmul(psum[:, 6, 0:2 * HD], ones[0:1, :], head_gain[0:1, :, :].rearrange("p a b -> p (a b)"),
                      start=True, stop=True).then_inc(S["gains_psum"], 1)
            for k in range(KC):
                pe.wait_ge(S["hT_ready"], k + 1)
                pe.wait_ge(S[f"w_in_in{k}"], 16)
                for j in range(4):
                    mm = pe.matmul(psum[32 * j:32 * j + 32, 0, 0:ZQ], hT[:, k, SEQ:NT],
                                   w_in_sb[:, k, ZQ * j:ZQ * (j + 1)], start=(k == 0), stop=(k == KC - 1),
                                   tile_position=(0, 32 * j), skip_group_check=True)
            mm.then_inc(S["z_done"], 1)

            for t in range(2):
                if t:
                    pe.wait_ge(S["z_copied"], 1)
                for k in range(KC):
                    for j in range(4):
                        w = min(BANK, IN_W - BANK * j)
                        mm = pe.matmul(psum[:, 4 - 4 * t + j, 0:w], hT[:, k, t * P:(t + 1) * P],
                                       w_in_sb[:, k, BANK * j:BANK * j + w], start=(k == 0), stop=(k == KC - 1))
                mm.then_inc(S["z_done"], 1)

            def step_idx(b):
                if b % 4 == 0:
                    pe.wait_ge(S[f"ik_in{b // 4}"], 16 * 4 * NPG)
                if b >= 2:
                    pe.wait_ge(S["ikT_odd" if b % 2 else "ikT_even"], b // 2)
                for n in range(NPG):
                    mm = tr(psum[0:ID, 4 + 2 * (b % 2) + n // 4, (n % 4) * P:(n % 4 + 1) * P], ik_cache[:, b, n, :])
                mm.then_inc(S["ikT_psum"], 1)

            def scores_s(g, q, keys, new, bank0):
                for lo, w, bank in ((0, BANK, 0), (BANK, BANK, 1), (PAST, DS, 2)):
                    for j in range(4):
                        k = new(4 * g + j) if lo == PAST else keys(j)[:, lo:lo + w]
                        mm = pe.matmul(psum[32 * j:32 * j + 32, bank0 + bank, 0:w],
                                       q[:, 4 * g + j].rearrange("p h s -> p (h s)"), k, start=True, stop=True,
                                       skip_group_check=True, tile_position=(0, 32 * j))
                return mm

            pe.wait_ge(S["z_copied"], 2)
            step_idx(0)
            step_idx(1)
            t, n = 2, NS
            pe.wait_ge(S["rope_done"], 1)
            pe.wait_ge(S["idx_rope_done"], 1)
            pe.wait_ge(S["z_copied"], 3)
            for h in range(NH):
                tr(psum[:, 3, h * n:(h + 1) * n], z[0:n, t, O_Q + h * HD:O_Q + (h + 1) * HD])
            tr(psum[:, 3, NH * n:(NH + 1) * n], z[0:n, t, O_K:O_K + HD])
            for h in range(IH + 1):
                c0 = (NH + 1 + h) * n
                mm = tr(psum[0:ID, 3, c0:c0 + n], z[0:n, t, O_IQ + h * ID:O_IQ + (h + 1) * ID])
            mm.then_inc(S["heads_psum"], 1)
            for b in range(2, DB):
                step_idx(b)
            pe.wait_ge(S["heads_copied"], 1)
            for g in range(2):
                pe.wait_ge(S["ikT_even"], 2 + 2 * g)
                pe.wait_ge(S["ikT_odd"], 2 + 2 * g)
                scores_s(g, iq_s, lambda j: ikT[:, 4 * g + j, :], lambda b: ik_new[:, b * DS:(b + 1) * DS], 4 * g
                         ).then_inc(S["idx_g_done"], 1)
            pe.wait_ge(S["fold_iw_ready"], 2)
            for g in range(2):
                mm = tr(psum[:, 3, g * NS:(g + 1) * NS], fold_iw[:, g, :])
            mm.then_inc(S["w_fold_psum"], 1)
            pe.wait_ge(S["w_fold_copied"], 1)
            pe.wait_ge(S["idx_s_relu"], 2)
            for lo, w, bank in ((0, BANK, 0), (BANK, BANK, 1), (PAST, DS, 2)):
                for g in range(2):
                    mm = pe.matmul(psum[0:NS, bank, 0:w], w_fold[:, g, :], rel_s[:, g, lo:lo + w],
                                   start=(g == 0), stop=(g == 1))
            mm.then_inc(S["score_s_psum"], 1)
            n = P
            for t in range(2):
                pe.wait_ge(S["rope_done"], t + 2)
                pe.wait_ge(S["idx_rope_done"], t + 2)
                if t:
                    pe.wait_ge(S["heads_copied"], 2)
                for h in range(NH):
                    tr(psum[:, 4, h * n:(h + 1) * n], z[:, t, O_Q + h * HD:O_Q + (h + 1) * HD])
                tr(psum[:, 5, 0:n], z[:, t, O_K:O_K + HD])
                tr(psum[0:ID, 5, n:2 * n], z[:, t, O_IK:O_IK + ID])
                for h in range(IH):
                    mm = tr(psum[0:ID, 6 + h // 4, (h % 4) * n:(h % 4 + 1) * n],
                            z[:, t, O_IQ + h * ID:O_IQ + (h + 1) * ID])
                mm.then_inc(S["heads_psum"], 1)
            pe.wait_ge(S["score_s_copied"], 1)
            pe.wait_ge(S["heads_copied"], 3)
            for t in range(2):
                if t:
                    pe.wait_ge(S["idx_relu"], 1)
                for h in range(IH):
                    mm = pe.matmul(psum[:, h // 2, (h % 2) * SEQ:(h % 2 + 1) * SEQ], iqT[:, h, t * P:(t + 1) * P],
                                   iqT[:, IH, :], start=True, stop=True)
                mm.then_inc(S["idx_psum"], 1)
            pe.wait_ge(S["late_in"], 16 * len(late_loads))
            for g in range(NG):
                cols = slice(g * P, (g + 1) * P)
                pe.matmul(psum[:, 4 + g, 0:SEQ], z[:, 0, cols], band[:, 0, g, :], start=True, stop=False)
                pe.matmul(psum[:, 4 + g, 0:SEQ], z[:, 1, cols], band[:, 1, g, :], start=False, stop=True)
                pe.matmul(psum[:, 4 + g, SEQ:NT], state_sb[:, cols], band_state[:, g, :], start=True, stop=False)
                mm = pe.matmul(psum[:, 4 + g, SEQ:NT], z[0:NS, 2, cols], band_new[:, g, :], start=False, stop=True)
                mm.then_inc(S["pool_d_psum"], 1)
            for g in range(NG):
                pe.wait_ge(S["pool_d_copied"], g + 1)
                pe.matmul(psum[:, 4 + g, 0:NT], w_pool_sb[:, g, :], dT[:, g, :], start=True, stop=True
                          ).then_inc(S["pool_y_psum"], 1)
            pe.wait_ge(S["k_in"], 16 * DB * NPG)
            pe.wait_ge(S["pool_y_copied"], NG)
            pe.wait_ge(S["idx_relu"], 2)
            for b in range(DB):
                if b >= 2:
                    pe.wait_ge(S["kT_copied"], b - 1)
                for n in range(NPG):
                    mm = tr(psum[:, 4 + 2 * (b % 2) + n // 4, (n % 4) * P:(n % 4 + 1) * P], k_cache[:, b, n, :])
                mm.then_inc(S["kT_psum"], 1)
                if b % 4 == 3:
                    pe.wait_ge(S["kT_copied"], b + 1)
                    if b == DB - 1:
                        pe.wait_ge(S["log_s_copied"], 1)
                    scores_s(b // 4, q_s, lambda j: kT_s[:, j, :],
                             lambda b: qkT[:, NH, SEQ + b * DS:SEQ + (b + 1) * DS], 0).then_inc(S["log_g_done"], 1)
            pe.wait_ge(S["keys_in"], 16)
            for r in range(RSLOTS):
                mm = tr(psum[:, 4 + r // 4, (r % 4) * P:(r % 4 + 1) * P], keys_nat[:, r, :])
                if r % 4 == 3:
                    mm.then_inc(S["keysT_psum"], 1)
            pe.wait_ge(S["log_s_copied"], 2)
            for t in range(2):
                pe.wait_ge(S["bias_p_ready"], t + 1)
                for h in range(NH):
                    out = psum[:, 2 - 2 * t + h // 2, (h % 2) * SEQ:(h % 2 + 1) * SEQ]
                    pe.matmul(out, qkT[:, h, t * P:(t + 1) * P], qkT[:, NH, 0:SEQ], start=True, stop=False)
                    mm = pe.matmul(out, ident[:, :], bias_p[:, t, :], start=False, stop=True)
                mm.then_inc(S["log_p_psum"], 1)
            pe.wait_ge(S["keysT_copied"], 4)
            for t in range(2):
                pe.wait_ge(S["p_norm"], t + 1)
                if t:
                    pe.wait_ge(S["pT_copied"], 1)
                for h in range(NH):
                    for kt in range(2):
                        mm = tr(psum[:, 4 + kt, h * P:(h + 1) * P], prob_p[:, h, kt * P:(kt + 1) * P])
                mm.then_inc(S["pT_psum"], 1)
                pe.wait_ge(S["pT_copied"], t + 1)
                for h in range(NH):
                    for kt in range(2):
                        mm = pe.matmul(psum[:, 6 + t, h * P:(h + 1) * P], z[:, kt, O_V:O_V + HD],
                                       probT[:, kt * NH + h, :], start=(kt == 0), stop=(kt == 1))
                mm.then_inc(S["yb_psum"], 1)
            pe.wait_ge(S["w_o_in"], 16 * KC)
            pe.wait_ge(S["yb_copied"], 2)
            for c in range(KC):
                if c >= 4:
                    pe.wait_ge(S["x1_prompt"], c - 3)
                for k in range(KC):
                    mm = pe.matmul(psum[:, c % 4, 0:SEQ], w_o_sb[:, k, c * P:(c + 1) * P], catT[:, k, 0:SEQ],
                                   start=(k == 0), stop=(k == KC - 1))
                mm.then_inc(S["wo_psum"], 1)
            pe.wait_ge(S["bias_s_ready"], 1)
            pe.wait_ge(S["x1_prompt"], KC)
            for g in range(2):
                for lo, w, bank in ((0, BANK, 2 * g), (BANK, BANK, 2 * g + 1), (PAST, DS, 6 + g)):
                    mm = pe.matmul(psum[:, bank, 0:w], fold16[:, g, :], bias_s[:, lo:lo + w], start=True, stop=True)
                mm.then_inc(S["spread_psum"], 1)
            for g in range(2):
                pe.wait_ge(S["pnew_ready"], g + 1)
                if g:
                    pe.wait_ge(S["sT_copied"], 1)
                for n in range(NPG):
                    tr(psum[:, 4 + n // 4, (n % 4) * P:(n % 4 + 1) * P], log_s[:, g, n * P:(n + 1) * P])
                tr(psum[0:NS, 6 + g, P:2 * P], pnew[:, g, :]).then_inc(S["sT_psum"], 1)
            pe.wait_ge(S["v_in"], 16 * DB * NPG)
            for g in range(2):
                pe.wait_ge(S["sT_copied"], g + 1)
                for n in range(-1, NPG):
                    for j in range(4):
                        rows = slice(32 * j, 32 * j + 32)
                        a, b = ((pnewT[:, g, rows], z[0:NS, 2, O_V:O_V + HD]) if n < 0 else
                                ((probT_s, probT)[g][:, n, rows], v_cache[:, 4 * g + j, n, :]))
                        mm = pe.matmul(psum[rows, g, 0:HD], a, b, start=(n < 0), stop=(n == NPG - 1),
                                       tile_position=(0, 32 * j), skip_group_check=True)
                mm.then_inc(S["ys_psum"], 1)
            for g in range(2):
                pe.wait_ge(S["ys_rows_copied"], g + 1)
                tr(psum[:, 2 + g, 0:P], ys_rows[:, g, :]).then_inc(S["ysT_psum"], 1)
            pe.wait_ge(S["ys_copied"], 2)
            W4 = D // 4
            for k in range(KC):
                for j in range(4):
                    mm = pe.matmul(psum[32 * j:32 * j + 32, 4, 0:W4], catT[:, k, SEQ:NT],
                                   w_o_sb[:, k, W4 * j:W4 * (j + 1)], start=(k == 0), stop=(k == KC - 1),
                                   tile_position=(0, 32 * j), skip_group_check=True)
            mm.then_inc(S["wo_s_psum"], 1)
            pe.wait_ge(S["wo_rows_copied"], 1)
            for a in range(2):
                mm = tr(psum[:, 5, a * P:(a + 1) * P], wo_rows[:, a * P:(a + 1) * P])
            mm.then_inc(S["wo_sT_psum"], 1)
            for c in range(KC):
                pe.wait_ge(S["sq2_ready"], KC + 1)
                mm = pe.matmul(psum[:, 4, 0:NT], ones[:, :], sq2[:, c, :], start=(c == 0), stop=(c == KC - 1))
            mm.then_inc(S["ssq2_done"], 1)
            def rq(r):
                w = w_pq_lo if r < RSLOTS // 2 else w_pq_hi
                if r == 0:
                    pe.wait_ge(S["w_pq_lo_in"], 16 * KC)
                    pe.wait_ge(S["x1_ready"], 1)
                if r == RSLOTS // 2:
                    pe.wait_ge(S["w_pq_hi_in"], 16 * KC)
                if r >= 2:
                    pe.wait_ge(S["rq_copied"], r - 1)
                c = r % (RSLOTS // 2)
                for k in range(KC):
                    if r == 0:
                        pe.wait_ge(S["h2_ready"], k + 1)
                    mm = pe.matmul(psum[:, r % 2, 0:NT], w[:, k, c * P:(c + 1) * P], h2[:, k, :],
                                   start=(k == 0), stop=(k == KC - 1))
                mm.then_inc(S["rq_psum"], 1)

            def rs(r):
                pe.wait_ge(S["rq_copied"], r + 1)
                if r == 0:
                    pe.wait_ge(S["rstd2_half"], 1)
                q4 = r // 4
                if r % 4 == 0 and r >= 4:
                    pe.wait_ge(S["rs_copied"], q4)
                for t in range(2):
                    pe.matmul(psum[:, 4 + t, (r % 4) * NK:(r % 4 + 1) * NK], q_ring[:, r % 2, t * P:(t + 1) * P],
                              keysT[:, r, :], start=True, stop=True)
                mm = pe.matmul(psum[32 * q4:32 * q4 + 32, 6, (r % 4) * NK:(r % 4 + 1) * NK],
                               q_ring[:, r % 2, SEQ:NT], keysT[:, r, :], start=True, stop=True,
                               skip_group_check=True, tile_position=(0, 32 * q4))
                mm.then_inc(S["rs_psum"], 1)

            rq(0)
            for r in range(RSLOTS):
                if r + 1 < RSLOTS:
                    rq(r + 1)
                rs(r)
            def transpose_u(slot, count):
                pe.wait_ge(u_in[slot], 16 * count)
                for c in range(KC):
                    mm = tr(psum[:, 4 + c // 4, (c % 4) * P:(c % 4 + 1) * P], u_raw[:, slot, c * P:(c + 1) * P])
                mm.then_inc(S["tr_done"], 1)

            def prod_u(slot, n, start=False):
                pe.wait_ge(S["uT_hi_ready"], n + 1)
                pe.wait_ge(S["uT_lo_ready"], n + 1)
                if not start:
                    pe.wait_ge(S["act_ready"], n - 1)
                i = 0
                for c in range(KC):
                    for a, b in ((uT_hi, h_hi), (uT_hi, h_lo), (uT_lo, h_hi)):
                        mm = pe.matmul(psum[:, 2 + slot % 2, 0:NT], a[:, slot % 2, c, :], b[:, c, :],
                                       start=(i == 0), stop=(i == 3 * KC - 1))
                        i += 1
                mm.then_inc(S["a_done"], 1)

            def spread(slot, n, bank0, i_step=None):
                pe.wait_ge(S["j_ready"], n + 1)
                if i_step is None:
                    pe.wait_ge(S["i_ready"], n + (1 - PH))
                else:
                    pe.wait_ge(S["i_ready_odd" if slot else "i_ready"], i_step + 1)
                for b in range(NB):
                    c0 = (b % 5) * 3 * PH
                    mm = pe.matmul(psum[:, bank0 + b // 5, c0:c0 + 3 * PH], j_hot[:, slot, :, b],
                                   i_hot[:, slot, :, :, b], start=True, stop=True, skip_group_check=True)
                mm.then_inc(S["g_psum"], 1)

            def spread_first(s, n, m):
                pe.wait_ge(S["g_copied"], n)
                spread(s, n, 6, m)

            def ahead(m, start=False, weights=False):
                for s in range(2):
                    pe.wait_ge(S["uT_raw_ready"], 4 * m + (2 * s + 2))
                    transpose_u((s + 1) % 2, m + (1 + s))
                    pair = 2 * m + (s - SLOTS_AT)
                    if weights:
                        spread_first(0, 2 * pair, pair)
                    prod_u(s, 2 * m + s, start)
                    if weights:
                        spread_first(1, 2 * pair + 1, pair)

            pe.wait_ge(S["rs_copied"], 4)
            pe.wait_ge(S["h_split_lo"], 1)
            transpose_u(0, 1)
            ahead(0, start=True)
            with pe.Fori(1, SLOTS_AT // 2) as m:
                ahead(m)
            for t in range(3):
                pe.wait_ge(S["slots_ready"], t + 1)
                if t:
                    pe.wait_ge(S["slots_copied"], t)
                m = P if t < 2 else 2 * TK
                for a in range(3):
                    mm = tr(psum[0:m, 7, a * P:(a + 1) * P],
                            slots[:, t, a].rearrange("p h k -> p (h k)")[:, 0:m])
                mm.then_inc(S["slots_psum"], 1)
            pe.wait_ge(S["slots_copied"], 3)
            with pe.Fori(SLOTS_AT // 2, PH // 2) as m:
                ahead(m, weights=True)

            def prod_v(s, n, start):
                pe.wait_ge(S["ag_lo_ready"], n - s % 2)
                for i in range(4):
                    c = 4 * (s % 2) + i
                    if not (start and s % 2 == 0 and i < 2):
                        pe.wait_ge(S["y_added"], 4 * n + (i - 9))
                    k = 0
                    for slot in ((s + 2) // 2 * 2 % 4, (s + 2) // 2 * 2 % 4 + 1):
                        for a, b in ((v_hi, ag_hi), (v_hi, ag_lo), (v_lo, ag_hi)):
                            mm = pe.matmul(psum[:, i % 2, 0:NT], a[:, slot, c * P:(c + 1) * P], b[:, slot, :],
                                           start=(k == 0), stop=(k == 5))
                            k += 1
                    mm.then_inc(S["y_psum"], 1)

            def quad(q, ph, start=False, stop=False):
                spreads = ph < NU // PH - 1
                end = stop and ph > 0
                for s in range(4):
                    n = 4 * q + s
                    if ph > 0:
                        if not (end and s == 3):
                            pe.wait_ge(S["uT_hi_ready"], n + 1)
                            pe.wait_ge(S["uT_lo_ready"], n + 1)
                            transpose_u((s + 1) % 2, 2 * q + 1 + (s + 1) // 2)
                        prod_u(s, n)
                    elif not (start and s < 2):
                        prod_v(s, n, start and s == 2)
                    if spreads:
                        pe.wait_ge(S["g_copied"], n + PH)
                        spread(s % 2, n + PH, 6, None if ph else 2 * q + (s // 2 + PH // 2))
                    if ph > 0:
                        prod_v(s, n, False)

            phases(pe, quad)
            for s in range(2):
                prod_v(s, NU + s, False)
            pe.wait_ge(S["y_added"], 4 * NU)
            for t, (t0, n) in enumerate(TILES):
                if t:
                    pe.wait_ge(S["yn_copied"], t)
                for c in range(KC):
                    mm = tr(psum[0:n, 6 + c // 4, (c % 4) * P:(c % 4 + 1) * P], xT[:, c, t0:t0 + n])
                mm.then_inc(S["yn_psum"], 1)

        @block.scalar
        def _(act):
            def copy(out, in_):
                return act.activation(out, in_, ACT.Copy)

            for c in range(KC):
                act.wait_ge(S["xT_psum"], c + 1)
                copy(xT[:, c, :], psum[:, c % 4, 0:NT])
                act.activation(sq[:, c, :], psum[:, c % 4, 0:NT], ACT.Square).then_inc(S["sq_ready"], 1)
            act.wait_ge(S["gains_psum"], 1)
            copy(gains[:, :], psum[:, 5, 0:2 * KC + NG])
            copy(gain5[:, 0:NH, :], bc(psum[:, 6, 0:HD], 1, NH))
            copy(gain5[:, NH, :], psum[:, 6, HD:2 * HD]).then_inc(S["gains_copied"], 1)
            act.wait_ge(S["rstd_half"], 1)
            act.activation(rstd_a[:, :], rstd_b[:, :], ACT.Sqrt).then_inc(S["rstd_root"], 1)

            def head_root(i, n):
                act.wait_ge(S["head_var"], i + 1)
                act.activation(small[0:n, 16:16 + NH + 1], small[0:n, 8:8 + NH + 1], ACT.Sqrt
                               ).then_inc(S["head_root"], 1)

            act.wait_ge(S["gains_in"], 16 * len(gain_loads))
            act.wait_ge(S["xT_psum"], KC)
            for g in range(2):
                ik_loads(act, g, 1)
            def copy_z(t):
                act.wait_ge(S["z_done"], t + 2)
                for j in range(4):
                    w = min(BANK, IN_W - BANK * j)
                    a = copy(z[:, t, BANK * j:BANK * j + w], psum[:, 4 - 4 * t + j, 0:w])
                a.then_inc(S["z_copied"], 1)

            def copy_ikT(b):
                act.wait_ge(S["ikT_psum"], b + 1)
                copy(ikT[:, b, :], psum[0:ID, 4:6, :].rearrange("p a b -> p (a b)")).then_inc(S["ikT_even"], 1)

            head_root(0, NS)
            act.wait_ge(S["z_copied"], 1)
            copy_z(0)
            head_root(1, P)
            copy_z(1)
            copy_ikT(0)
            act.wait_ge(S["heads_psum"], 1)
            copy(qkT[:, NH, SEQ:NT], psum[:, 3, NH * NS:(NH + 1) * NS])
            for a in range(2):
                copy(q_s[:, :, NH * a:NH * (a + 1), :],
                     psum[:, 3, 0:NH * NS].rearrange("p (h b s) -> p b h s", h=NH, b=DB))
            c0 = (NH + 1) * NS
            copy(ik_new[:, :], psum[0:ID, 3, c0 + IH * NS:c0 + (IH + 1) * NS])
            copy(iq_s[:], psum[0:ID, 3, c0:c0 + IH * NS].rearrange("p (h b s) -> p b h s", h=IH, b=DB)
                 ).then_inc(S["heads_copied"], 1)
            for b in range(2, DB, 2):
                copy_ikT(b)
            for dst, src in late_loads:
                act.dma_start(dst, src).then_inc(S["late_in"], 16)
            for g in range(2):
                act.wait_ge(S["idx_g_done"], g + 1)
                act.activation(rel_s[:, g, 0:PAST], psum[:, 4 * g:4 * g + 2, :].rearrange("p a b -> p (a b)"),
                               ACT.Relu)
                act.activation(rel_s[:, g, PAST:KEYS], psum[:, 4 * g + 2, 0:DS], ACT.Relu
                               ).then_inc(S["idx_s_relu"], 1)
            act.wait_ge(S["w_fold_psum"], 1)
            copy(w_fold[:].rearrange("p a b -> p (a b)"), psum[:, 3, 0:2 * NS]).then_inc(S["w_fold_copied"], 1)
            act.wait_ge(S["score_s_psum"], 1)
            act.wait_ge(S["idx_rope_done"], 3)
            copy(score_s[:, 0:PAST], psum[0:NS, 0:2, :].rearrange("p a b -> p (a b)"))
            copy(score_s[:, PAST:KEYS], psum[0:NS, 2, 0:DS]).then_inc(S["score_s_copied"], 1)
            head_root(2, P)
            for t in range(2):
                act.wait_ge(S["heads_psum"], t + 2)
                cols = slice(t * P, (t + 1) * P)
                copy(qkT[:, NH, cols], psum[:, 5, 0:P])
                copy(qkT[:, 0:NH, cols], psum[:, 4, :].rearrange("p (h t) -> p h t", h=NH))
                for a in range(2):
                    copy(iqT[:, 4 * a:4 * a + 4, cols], psum[0:ID, 6 + a, :].rearrange("p (h t) -> p h t", h=4))
                copy(iqT[:, IH, cols], psum[0:ID, 5, P:2 * P]).then_inc(S["heads_copied"], 1)
            for t in range(2):
                act.wait_ge(S["idx_psum"], t + 1)
                if t:
                    act.wait_ge(S["idx_summed"], 1)
                act.activation(rel_p[:].rearrange("p h k -> p (h k)"),
                               psum[:, 0:4, :].rearrange("p a b -> p (a b)"), ACT.Relu).then_inc(S["idx_relu"], 1)
            for g in range(NG):
                act.wait_ge(S["pool_d_psum"], g + 1)
                copy(dT[:, g, :], psum[:, 4 + g, 0:NT]).then_inc(S["pool_d_copied"], 1)
            for g in range(NG):
                act.wait_ge(S["pool_y_psum"], g + 1)
                act.activation(catT[:, g, :], psum[:, 4 + g, 0:NT], ACT.Copy,
                               scale=gains[:, 2 * KC + g:2 * KC + g + 1]).then_inc(S["pool_y_copied"], 1)
            for b in range(DB):
                act.wait_ge(S["kT_psum"], b + 1)
                if b >= 4:
                    act.wait_ge(S["log_g_done"], 1)
                lo = 4 + 2 * (b % 2)
                copy(kT_s[:, b % 4, :], psum[:, lo:lo + 2, :].rearrange("p a b -> p (a b)")
                     ).then_inc(S["kT_copied"], 1)
                if b % 4 == 3:
                    g = b // 4
                    act.wait_ge(S["log_g_done"], g + 1)
                    copy(log_s[:, g, 0:PAST], psum[:, 0:2, :].rearrange("p a b -> p (a b)"))
                    copy(log_s[:, g, PAST:KEYS], psum[:, 2, 0:DS]).then_inc(S["log_s_copied"], 1)
            for r in range(4):
                act.wait_ge(S["keysT_psum"], r + 1)
                copy(keysT[:, 4 * r:4 * r + 4, :].rearrange("p a b -> p (a b)"), psum[:, 4 + r, :]
                     ).then_inc(S["keysT_copied"], 1)
            for t in range(2):
                act.wait_ge(S["p_max"], t + 1)
                for h in range(NH):
                    a = act.activation(prob_p[:, h, :], psum[:, 2 - 2 * t + h // 2, (h % 2) * SEQ:(h % 2 + 1) * SEQ],
                                       ACT.Exp, bias=small[:, 28 + h:29 + h], scale=SC,
                                       accum_out=small[:, 32 + h:33 + h])
                a.then_inc(S["p_exp"], 1)
                act.wait_ge(S["pT_psum"], t + 1)
                if t:
                    act.wait_ge(S["yb_psum"], 1)
                copy(probT[:].rearrange("p a b -> p (a b)"), psum[:, 4:6, :].rearrange("p a b -> p (a b)")
                     ).then_inc(S["pT_copied"], 1)
                act.wait_ge(S["yb_psum"], t + 1)
                copy(catT[:, NG:NG + NH, t * P:(t + 1) * P], psum[:, 6 + t, :].rearrange("p (h t) -> p h t", h=NH)
                     ).then_inc(S["yb_copied"], 1)
            for c in range(KC):
                act.wait_ge(S["x1_prompt"], c + 1)
                act.activation(sq2[:, c, 0:SEQ], xT[:, c, 0:SEQ], ACT.Square).then_inc(S["sq2_ready"], 1)
            for g in range(2):
                act.wait_ge(S["s_max"], g + 1)
                act.activation(log_s[:, g, :], log_s[:, g, :], ACT.Exp, bias=small[:, 42 + g:43 + g], scale=SC,
                               accum_out=small[:, 44 + g:45 + g]).then_inc(S["s_exp"], 1)
            for g in range(2):
                act.wait_ge(S["sT_psum"], g + 1)
                copy((probT_s, probT)[g][:].rearrange("p a b -> p (a b)"),
                     psum[:, 4:6, :].rearrange("p a b -> p (a b)"))
                copy(pnewT[:, g, :], psum[0:NS, 6 + g, P:2 * P]).then_inc(S["sT_copied"], 1)
            for g in range(2):
                act.wait_ge(S["ys_psum"], g + 1)
                copy(ys_rows[:, g, :], psum[:, g, 0:HD]).then_inc(S["ys_rows_copied"], 1)
            for g in range(2):
                act.wait_ge(S["ysT_psum"], g + 1)
                c0 = SEQ + g * 4 * DS
                copy(catT[:, NG:NG + NH, c0:c0 + 4 * DS].rearrange("p h (j s) -> p h j s", j=4),
                     psum[:, 2 + g, 0:P].rearrange("p (j h s) -> p h j s", j=4, s=DS)[:, 0:NH]
                     ).then_inc(S["ys_copied"], 1)
            act.wait_ge(S["wo_s_psum"], 1)
            copy(wo_rows[:], psum[:, 4, 0:D // 4]).then_inc(S["wo_rows_copied"], 1)
            act.wait_ge(S["x1_ready"], 1)
            act.activation(sq2[:, :, SEQ:NT], xT[:, :, SEQ:NT], ACT.Square).then_inc(S["sq2_ready"], 1)
            act.wait_ge(S["rstd2_half"], 1)
            act.activation(rstd_a[:, :], rstd_b[:, :], ACT.Sqrt).then_inc(S["rstd2_root"], 1)
            act.wait_ge(S["h2_ready"], KC)
            copy(h_hi[:], h2[:]).then_inc(S["h_split"], 1)
            act.wait_ge(S["rows_out"], 16 * (9 + 1 + DB))
            for r in range(RSLOTS):
                act.wait_ge(S["rq_psum"], r + 1)
                if r >= 2:
                    act.wait_ge(S["rs_psum"], r - 1)
                copy(q_ring[:, r % 2, :], psum[:, r % 2, 0:NT]).then_inc(S["rq_copied"], 1)
                if r % 4 == 0 and r:
                    rs_copy(act, copy, r // 4 - 1)
            rs_copy(act, copy, 3)
            def split_u(slot, n, free=True, start=False):
                act.wait_ge(S["tr_done"], n + 1)
                if free:
                    act.wait_ge(S["a_done"], n - 1)
                for half in range(2):
                    chunks = slice(4 * half, 4 * half + 4)
                    part = psum[:, 4 + half, :]
                    a = copy(uT_hi[:, slot % 2, chunks].rearrange("p a b -> p (a b)"), part)
                    if not start and half == 0:
                        act.wait_ge(S["uT_lo_ready"], n)
                    copy(uT_raw[:, chunks].rearrange("p a b -> p (a b)"), part).then_inc(S["uT_raw_ready"], 1)
                    if half:
                        a.then_inc(S["uT_hi_ready"], 1)

            def high_u(slot, n, free=True):
                act.wait_ge(S["tr_done"], n + 1)
                if free:
                    act.wait_ge(S["a_done"], n - 1)
                copy(uT_hi[:, slot % 2].rearrange("p a b -> p (a b)"), psum[:, 4:6, :].rearrange("p a b -> p (a b)")
                     ).then_inc(S["uT_hi_ready"], 1)

            def ahead(m, start=False):
                for s in range(2):
                    n = 2 * m + s
                    split_u(s + 1, n + 1, not (start and s == 0))
                    act.wait_ge(S["a_done"], n + 1)
                    act.activation(g_odd[:, bass.ds(n, 1)].rearrange("p k a b -> p (k a b)"),
                                   psum[:, 2 + s, 0:NT], ACT.Gelu).then_inc(S["act_ready"], 1)

            split_u(0, 0, False, True)
            ahead(0, True)
            with act.Fori(1, EXP_AT // 2) as m:
                ahead(m)
            act.wait_ge(S["rexp_in"], 3)
            for t in range(3):
                H = RH if t < 2 else 2
                a = act.activation(slots[:, t, 2, 0:H], slots[:, t, 2, 0:H], ACT.Exp)
            a.then_inc(S["rexp_out"], 1)
            act.activation(small[:, 63:64], ones[:, 0:1], ACT.Gelu)
            with act.Fori(EXP_AT // 2, SLOTS_AT // 2) as m:
                ahead(m)
            for t in range(3):
                act.wait_ge(S["slots_psum"], t + 1)
                if t < 2:
                    for i, dst in enumerate((iT, jT, wT)):
                        a = copy(dst[:, t * P:(t + 1) * P], psum[:, 7, i * P:(i + 1) * P])
                else:
                    for j in range(4):
                        for i, dst in enumerate((iT, jT, wT)):
                            a = copy(dst[32 * j:32 * j + 32, SEQ:NT],
                                     psum[0:32, 7, i * P + 32 * j:i * P + 32 * j + 32])
                a.then_inc(S["slots_copied"], 1)

            with act.Fori(SLOTS_AT // 2, PH // 2) as m:
                ahead(m)

            def quad(q, ph, start=False, stop=False):
                for s in range(4):
                    n = 4 * q + s
                    if ph > 0 and not (stop and s == 3):
                        high_u(s + 1, n + 1)
                    act.wait_ge(v_tile_in[s], 16 * (q + 1))
                    if not start:
                        act.wait_ge(S["y_psum"], 4 * n - 8)
                    copy(v_hi[:, s, :], v_raw[:, s, :]).then_inc(S["v_hi_ready"], 1)
                    if ph > 0:
                        act.wait_ge(S["a_done"], n + 1)
                        act.wait_ge(S["prod_ready"], n - 1)
                        act.activation(act_g[:, s % 2, :], psum[:, 2 + s % 2, 0:NT], ACT.Gelu
                                       ).then_inc(S["act_ready"], 1)
                    act.wait_ge(S["prod_ready"], n + 1)
                    copy(ag_hi[:, s, :], ag[:, s % 2, :]).then_inc(S["ag_hi_ready"], 1)

            phases(act, quad)
            for t, (t0, n) in enumerate(TILES):
                act.wait_ge(S["yn_psum"], t + 1)
                copy(y_nat[0:n, t, :], psum[0:n, 6:8, :].rearrange("p a b -> p (a b)")).then_inc(S["yn_copied"], 1)

        @block.gpsimd
        def _(pool):
            steps = [0]

            def settle(ins):
                steps[0] += 1
                ins.then_inc(S["pool_step"], 1)
                pool.wait_ge(S["pool_step"], steps[0])

            pool.memset(ones[:, :], 1.0).then_inc(S["ones_set"], 1)
            for dst, src in gain_loads:
                pool.dma_start(dst, src).then_inc(S["gains_in"], 16)
            for dst, src in early_loads:
                pool.dma_start(dst, src).then_inc(S["consts_in"], 16)
            pool.wait_ge(S["consts_in"], 16 * len(early_loads))
            for i, t in enumerate(ORDER):
                n = TILES[t][1]
                pool.wait_ge(S["z_copied"], i + 1)
                if i:
                    pool.wait_ge(S["idx_rope_done"], i)
                x = z[0:n, t, O_IQ:O_IW].rearrange("p (h a d) -> p h a d", a=2, d=ID // 2)
                cos = bc(rope[0:n, t, HD:HD + ID // 2], 1, IH + 1)
                sin = bc(rope[0:n, t, HD + ID // 2:HD + ID], 1, IH + 1)
                tmp = [idx_tmp[0:n, i, :].rearrange("p (h d) -> p h d", h=IH + 1) for i in range(4)]
                pool.tensor_tensor(tmp[0], x[:, :, 0], cos, ALU.mult)
                pool.tensor_tensor(tmp[1], x[:, :, 1], sin, ALU.mult)
                pool.tensor_tensor(tmp[2], x[:, :, 1], cos, ALU.mult)
                settle(pool.tensor_tensor(tmp[3], x[:, :, 0], sin, ALU.mult))
                pool.tensor_tensor(x[:, :, 0], tmp[0], tmp[1], ALU.subtract)
                pool.tensor_tensor(x[:, :, 1], tmp[2], tmp[3], ALU.add)
                pool.tensor_scalar(iw[0:n, t, :], z[0:n, t, O_IW:IN_W], float(IH) ** -0.5, None, ALU.mult
                                   ).then_inc(S["idx_rope_done"], 1)
                if i == 0:
                    pool.wait_ge(S["idx_rope_done"], 1)
                    for g in range(2):
                        pool.tensor_tensor(fold_iw[:, g, :].rearrange("t (j h s) -> t j h s", j=4, s=DS),
                                           fold[:, g, :].rearrange("t (j h s) -> t j h s", j=4, s=DS),
                                           iw[0:NS, 2, :].unsqueeze(1).unsqueeze(3).to_broadcast([NS, 4, IH, DS]),
                                           ALU.mult).then_inc(S["fold_iw_ready"], 1)
            pool.wait_ge(S["score_s_psum"], 1)
            page_loads(pool, 0, cache_v, v_cache[:].rearrange("p b n d -> p (b n d)"), HD, S["v_in"], DB * NPG)
            pool.wait_ge(S["h_split"], 1)
            pool.tensor_tensor(h_lo[:], h2[:], h_hi[:].bitcast(F32), ALU.subtract).then_inc(S["h_split_lo"], 1)

            def low_u(slot, n):
                for half in range(2):
                    chunks = slice(4 * half, 4 * half + 4)
                    pool.wait_ge(S["uT_raw_ready"], 2 * n + (half + 1))
                    p = pool.tensor_tensor(uT_lo[:, slot % 2, chunks], uT_raw[:, chunks],
                                           uT_hi[:, slot % 2, chunks].bitcast(F32), ALU.subtract)
                p.then_inc(S["uT_lo_ready"], 1)

            def odd_weights(pair, token):
                pool.wait_ge(S["i_eq_odd"], pair + 1)
                pool.tensor_tensor(i_hot[:, 1], bc(i_eq[:, 1], 1, 3), bc(w3[:, :, bass.ds(token, NB)], 2, PH),
                                   ALU.mult).then_inc(S["i_ready_odd"], 1)

            low_u(0, 0)
            with pool.Fori(0, SLOTS_AT // 2) as m:
                for s in range(2):
                    low_u(s + 1, 2 * m + (s + 1))
            pool.wait_ge(S["w3_ready"], 1)
            odd_weights(0, NB)
            low_u(1, SLOTS_AT + 1)
            pool.wait_ge(S["g_psum"], 2)
            odd_weights(1, 3 * NB)
            low_u(0, SLOTS_AT + 2)
            with pool.Fori(SLOTS_AT // 2 + 1, PH // 2) as m:
                for s in range(2):
                    pair = 2 * m + (s - SLOTS_AT)
                    pool.wait_ge(S["g_psum"], 2 * pair)
                    odd_weights(pair, 2 * NB * pair + NB)
                    low_u(s + 1, 2 * m + (s + 1))

            def quad(q, ph, start=False, stop=False):
                for s in range(4):
                    n = 4 * q + s
                    pool.wait_ge(S["v_hi_ready"], n + 1)
                    pool.tensor_tensor(v_lo[:, s, :], v_raw[:, s, :], v_hi[:, s, :].bitcast(F32),
                                       ALU.subtract).then_inc(S["v_lo_ready"], 1)
                    pool.wait_ge(S["ag_hi_ready"], n + 1)
                    pool.tensor_tensor(ag_lo[:, s, :], ag[:, s % 2, :], ag_hi[:, s, :].bitcast(F32),
                                       ALU.subtract).then_inc(S["ag_lo_ready"], 1)
                    if ph == 0 and s % 2 == 0:
                        pool.wait_ge(S["g_psum"], n + PH)
                        odd_weights(2 * q + (s // 2 + PH // 2), NB * n + NB)

            phases(pool, quad)

        @block.vector
        def _(dve):
            steps = [0]

            def settle(ins):
                steps[0] += 1
                ins.then_inc(S["dve_step"], 1)
                dve.wait_ge(S["dve_step"], steps[0])

            def inverse_mean(out, in_, n, half):
                settle(dve.tensor_scalar(out, in_, 1.0 / n, EPS, ALU.mult, ALU.add))
                dve.reciprocal(out, out).then_inc(half, 1)

            dve.wait_ge(S["ssq_done"], 1)
            inverse_mean(rstd_b[:, :], psum[:, 4, 0:NT], D, S["rstd_half"])
            dve.wait_ge(S["rstd_root"], 1)
            dve.wait_ge(S["gains_copied"], 1)
            for c in range(KC):
                dve.scalar_tensor_tensor(hT[:, c, :], xT[:, c, :], gains[:, c:c + 1], rstd_a[:, :], ALU.mult,
                                         ALU.mult).then_inc(S["hT_ready"], 1)

            def rope_qk(i):
                dve.wait_ge(S["consts_in"], 16 * len(early_loads))
                t = ORDER[i]
                n = TILES[t][1]
                dve.wait_ge(S["z_copied"], i + 1)
                x = z[0:n, t, O_Q:O_V].rearrange("p (h d) -> p h d", d=HD)
                settle(dve.tensor_tensor(head_sq[0:n], x, x, ALU.mult))
                settle(dve.tensor_reduce(small[0:n, 0:NH + 1], head_sq[0:n], AX, ALU.add))
                inverse_mean(small[0:n, 8:8 + NH + 1], small[0:n, 0:NH + 1], HD, S["head_var"])
                dve.wait_ge(S["head_root"], i + 1)
                settle(dve.tensor_tensor(x, x, bc(small[0:n, 16:16 + NH + 1], 2, HD), ALU.mult))
                settle(dve.tensor_tensor(x, x, gain5[0:n], ALU.mult))
                x = z[0:n, t, O_Q:O_V].rearrange("p (h a d) -> p h a d", a=2, d=HD // 2)
                cos, sin = (bc(rope[0:n, t, o:o + HD // 2], 1, NH + 1) for o in (0, HD // 2))
                tmp = [rope_tmp[0:n, i, :].rearrange("p (h d) -> p h d", h=NH + 1) for i in range(4)]
                dve.tensor_tensor(tmp[0], x[:, :, 0], cos, ALU.mult)
                dve.tensor_tensor(tmp[1], x[:, :, 1], sin, ALU.mult)
                dve.tensor_tensor(tmp[2], x[:, :, 1], cos, ALU.mult)
                settle(dve.tensor_tensor(tmp[3], x[:, :, 0], sin, ALU.mult))
                dve.tensor_tensor(x[:, :, 0], tmp[0], tmp[1], ALU.subtract)
                dve.tensor_tensor(x[:, :, 1], tmp[2], tmp[3], ALU.add).then_inc(S["rope_done"], 1)

            def take_top(score, work, rounds):
                best = top8[0:score.shape[0], :]
                for r in rounds:
                    left = score if r == 0 else work
                    settle(dve.max(best, left))
                    settle(dve.match_replace(work, best, left, TAKEN))

            dve.wait_ge(S["z_done"], 1)
            for j in range(4):
                ins = dve.tensor_copy(z[0:NS, 2, ZQ * j:ZQ * (j + 1)], psum[32 * j:32 * j + 32, 0, 0:ZQ])
            ins.then_inc(S["z_copied"], 1)
            rope_qk(0)
            rope_qk(1)
            for b in range(1, DB, 2):
                dve.wait_ge(S["ikT_psum"], b + 1)
                dve.tensor_copy(ikT[:, b, :], psum[0:ID, 6:8, :].rearrange("p a b -> p (a b)")
                                ).then_inc(S["ikT_odd"], 1)
            rope_qk(2)

            def select_p(t):
                dve.wait_ge(S["idx_relu"], t + 1)
                dve.wait_ge(S["idx_rope_done"], 3)
                settle(dve.tensor_scalar(score_p[:, :], rel_p[:, 0, :], iw[:, t, 0:1], None, ALU.mult))
                for h in range(1, IH):
                    ins = dve.scalar_tensor_tensor(score_p[:, :], rel_p[:, h, :], iw[:, t, h:h + 1], score_p[:, :],
                                                   ALU.mult, ALU.add)
                    if h < IH - 1:
                        settle(ins)
                ins.then_inc(S["idx_summed"], 1)
                dve.wait_ge(S["idx_summed"], t + 1)
                dve.wait_ge(S["late_in"], 16 * len(late_loads))
                settle(dve.tensor_tensor(score_p[:, :], score_p[:, :], causal[:, t, :], ALU.add))
                take_top(score_p[:, :], work_p[:, :], range(KSEL_P // 8))
                settle(dve.tensor_tensor(work_p[:, :], work_p[:, :], score_p[:, :], ALU.is_equal))
                dve.scalar_tensor_tensor(bias_p[:, t, :], work_p[:, :], NEG, causal[:, t, :], ALU.mult, ALU.add
                                         ).then_inc(S["bias_p_ready"], 1)

            def max_p(t):
                dve.wait_ge(S["log_p_psum"], t + 1)
                settle(dve.tensor_reduce(small[:, 24:28],
                                         psum[:, 2 - 2 * t:4 - 2 * t, :].rearrange("p a (h k) -> p (a h) k", h=2),
                                         AX, ALU.max))
                dve.tensor_scalar(small[:, 28:32], small[:, 24:28], -SC, None, ALU.mult).then_inc(S["p_max"], 1)

            def norm_p(t):
                dve.wait_ge(S["p_exp"], t + 1)
                settle(dve.reciprocal(small[:, 36:40], small[:, 32:36]))
                dve.tensor_tensor(prob_p[:], prob_p[:], bc(small[:, 36:40], 2, SEQ), ALU.mult
                                  ).then_inc(S["p_norm"], 1)

            def add_wo(c):
                dve.wait_ge(S["wo_psum"], c + 1)
                dve.tensor_tensor(xT[:, c, 0:SEQ], xT[:, c, 0:SEQ], psum[:, c % 4, 0:SEQ], ALU.add
                                  ).then_inc(S["x1_prompt"], 1)

            dve.wait_ge(S["score_s_copied"], 1)
            settle(dve.tensor_tensor(score_s[:, PAST:KEYS], score_s[:, PAST:KEYS], causal_new[:, :], ALU.add))
            between = {8: (select_p, 0), 9: (select_p, 1), 11: (max_p, 0), 13: (norm_p, 0), 15: (max_p, 1),
                       17: (norm_p, 1)}
            between.update({KSEL_S // 8 - KC + c: (add_wo, c) for c in range(KC)})
            for r in range(KSEL_S // 8):
                if r in between:
                    step, which = between[r]
                    step(which)
                take_top(score_s[:, :], work_s[:, :], [r])
            settle(dve.tensor_tensor(work_s[:, :], work_s[:, :], score_s[:, :], ALU.is_equal))
            dve.tensor_copy(fold16[:], fold[:])
            dve.tensor_scalar(bias_s[:, 0:PAST], work_s[:, 0:PAST], NEG, None, ALU.mult)
            dve.scalar_tensor_tensor(bias_s[:, PAST:KEYS], work_s[:, PAST:KEYS], NEG, causal_new[:, :], ALU.mult,
                                     ALU.add).then_inc(S["bias_s_ready"], 1)
            for g in range(2):
                dve.wait_ge(S["spread_psum"], g + 1)
                dve.tensor_tensor(log_s[:, g, 0:PAST], log_s[:, g, 0:PAST],
                                  psum[:, 2 * g:2 * g + 2, :].rearrange("p a b -> p (a b)"), ALU.add)
                settle(dve.tensor_tensor(log_s[:, g, PAST:KEYS], log_s[:, g, PAST:KEYS], psum[:, 6 + g, 0:DS],
                                         ALU.add))
                settle(dve.tensor_reduce(small[:, 40 + g:41 + g], log_s[:, g, :], AX, ALU.max))
                dve.tensor_scalar(small[:, 42 + g:43 + g], small[:, 40 + g:41 + g], -SC, None, ALU.mult
                                  ).then_inc(S["s_max"], 1)
            for g in range(2):
                dve.wait_ge(S["s_exp"], g + 1)
                settle(dve.reciprocal(small[:, 46 + g:47 + g], small[:, 44 + g:45 + g]))
                settle(dve.tensor_scalar(log_s[:, g, :], log_s[:, g, :], small[:, 46 + g:47 + g], None, ALU.mult))
                dve.tensor_tensor(pnew[:, g, :].rearrange("p (b s) -> p b s", b=DB), bc(own[:, g, :], 2, DS),
                                  bc(log_s[:, g, PAST:KEYS], 1, DB), ALU.mult).then_inc(S["pnew_ready"], 1)
            dve.wait_ge(S["wo_sT_psum"], 1)
            x_s = xT[:, :, SEQ:NT].rearrange("p (j a) t -> p j a t", a=2)
            for a in range(2):
                ins = dve.tensor_tensor(x_s[:, :, a], x_s[:, :, a],
                                        psum[:, 5, a * P:(a + 1) * P].rearrange("p (j t) -> p j t", j=4), ALU.add)
            ins.then_inc(S["x1_ready"], 1)
            dve.wait_ge(S["ssq2_done"], 1)
            inverse_mean(rstd_b[:, :], psum[:, 4, 0:NT], D, S["rstd2_half"])
            dve.wait_ge(S["rstd2_root"], 1)
            for c in range(KC):
                dve.scalar_tensor_tensor(h2[:, c, :], xT[:, c, :], gains[:, KC + c:KC + c + 1], rstd_a[:, :],
                                         ALU.mult, ALU.mult).then_inc(S["h2_ready"], 1)

            def best16(tiles, values, places, left, sources):
                items = [(t, i) for t in tiles for i in range(len(sources[t]))]
                for t, i in items:
                    ins = dve.max(values[t][i][:, 0:8], sources[t][i])
                settle(ins)
                for t, i in items:
                    dve.max_index(places[t][i][:, 0:8], values[t][i][:, 0:8], sources[t][i])
                    ins = dve.match_replace(left[t][i], values[t][i][:, 0:8], sources[t][i], TAKEN)
                settle(ins)
                for t, i in items:
                    ins = dve.max(values[t][i][:, 8:16], left[t][i])
                settle(ins)
                for t, i in items:
                    ins = dve.max_index(places[t][i][:, 8:16], values[t][i][:, 8:16], left[t][i])
                settle(ins)

            def route(tiles, h0, blocks):
                four, two = range(2 * h0, 2 * h0 + 4), (h0, h0 + 1)
                slot = {t: i for i, t in enumerate(tiles)}
                best16(tiles, {t: [sv[:, t, r] for r in four] for t in tiles},
                       {t: [si[:, t, r] for r in four] for t in tiles},
                       {t: [rwork[:, slot[t], i] for i in range(4)] for t in tiles}, blocks)
                for t in tiles:
                    for i, h in enumerate(two):
                        ins = dve.tensor_tensor(cand[:, slot[t], i], bc(sv[:, t, 2 * h], 2, TK),
                                                bc(sv[:, t, 2 * h + 1], 1, TK), ALU.add)
                settle(ins)
                sums = cand[:].rearrange("p t h a b -> p t h (a b)")
                left = rwork[:].rearrange("p t (h b) k -> p t h (b k)", h=2)
                best16(tiles, {t: [fv[:, t, h] for h in two] for t in tiles},
                       {t: [fi[:, t, h] for h in two] for t in tiles},
                       {t: [left[:, slot[t], i] for i in range(2)] for t in tiles},
                       {t: [sums[:, slot[t], i] for i in range(2)] for t in tiles})

            dve.tensor_copy(ranks[:], bc(iota[:, 0:TK], 2, RH * TK))
            for q4 in range(4):
                dve.wait_ge(S["rs_copied"], q4 + 1)
                route((0, 1), 2 * q4, {t: [sr[:, t, 4 * q4 + i, :] for i in range(4)] for t in range(2)})
            route((2,), 0, {2: [sr_s[:, i, :] for i in range(4)]})
            for t in range(3):
                H = RH if t < 2 else 2
                ins = dve.tensor_tensor(slots[:, t, 2, 0:H], fv[:, t, 0:H], fv[:, t, 0:H, 0:1].to_broadcast([P, H, TK]),
                                        ALU.subtract)
                ins.then_inc(S["rexp_in"], 1)
                dve.tensor_copy(sib[:, t, 0:2 * H], si[:, t, 0:2 * H])
            def look_up(t, c):
                H = RH if t < 2 else 2
                n = H * TK
                settle(dve.tensor_tensor(hit[:, :, 0:n], ranks[:, :, 0:n], bc(fabb[:, c, 0:n], 1, TK), ALU.is_equal))
                ranks_of = sib[:, t, 0:2 * H, :].rearrange("p (h c) a -> p c a h", c=2)
                settle(dve.tensor_tensor(picked[:, :, 0:n].rearrange("p a (h k) -> p a h k", k=TK),
                                         hit[:, :, 0:n].rearrange("p a (h k) -> p a h k", k=TK),
                                         bc(ranks_of[:, c], 3, TK), ALU.mult))
                settle(dve.tensor_tensor(half_sum[:, :, 0:n], picked[:, 0:8, 0:n], picked[:, 8:16, 0:n], ALU.add))
                settle(dve.tensor_tensor(half_sum[:, 0:4, 0:n], half_sum[:, 0:4, 0:n], half_sum[:, 4:8, 0:n], ALU.add))
                settle(dve.tensor_tensor(half_sum[:, 0:2, 0:n], half_sum[:, 0:2, 0:n], half_sum[:, 2:4, 0:n], ALU.add))
                settle(dve.tensor_tensor(slots[:, t, c].rearrange("p h k -> p (h k)")[:, 0:n], half_sum[:, 0, 0:n],
                                         half_sum[:, 1, 0:n], ALU.add))

            for t in range(3):
                H = RH if t < 2 else 2
                n = H * TK
                f = fi[:, t].rearrange("p h k -> p (h k)")[:, 0:n]
                dve.tensor_scalar(fab[:, 0, 0:n], f, 4, None, ALU.logical_shift_right)
                settle(dve.tensor_scalar(fab[:, 1, 0:n], f, TK - 1, None, ALU.bitwise_and))
                settle(dve.tensor_copy(fabb[:, :, 0:n], fab[:, :, 0:n]))
                look_up(t, 0)
                look_up(t, 1)
                if t == 0:
                    dve.wait_ge(S["rexp_out"], 1)
                settle(dve.tensor_reduce(ssum[:, 0:H], slots[:, t, 2, 0:H], AX, ALU.add))
                settle(dve.reciprocal(ssum[:, 0:H], ssum[:, 0:H]))
                dve.tensor_tensor(slots[:, t, 2, 0:H], slots[:, t, 2, 0:H], bc(ssum[:, 0:H], 2, TK), ALU.mult
                                  ).then_inc(S["slots_ready"], 1)
            dve.wait_ge(S["slots_copied"], 3)
            settle(dve.tensor_copy(w3[:, 0, :], wT[:, :]))
            settle(dve.tensor_tensor(w_rest[:, :], wT[:, :], w3[:, 0, :], ALU.subtract))
            settle(dve.tensor_copy(w3[:, 1, :], w_rest[:, :]))
            settle(dve.tensor_tensor(w3[:, 2, :], w_rest[:, :], w3[:, 1, :], ALU.subtract))
            settle(dve.tensor_copy(counts[:], bc(iota[:, :], 2, NB)))
            dve.tensor_copy(top8[0:1, 0:1], ssum[0:1, 0:1]).then_inc(S["w3_ready"], 1)
            dve.wait_ge(S["h_split_lo"], 1)

            def find_i(slot, token, ph, ready=S["i_eq_ready"]):
                dve.tensor_tensor(i_eq[:, slot], counts[:, ph * PH:(ph + 1) * PH, :],
                                  bc(iT[:, bass.ds(token, NB)], 1, PH), ALU.is_equal).then_inc(ready, 1)

            def find_j(slot, token):
                dve.tensor_tensor(j_hot[:, slot], counts[:], bc(jT[:, bass.ds(token, NB)], 1, P),
                                  ALU.is_equal).then_inc(S["j_ready"], 1)

            def put_weights(slot, n, token):
                dve.wait_ge(S["i_eq_ready"], n + 1)
                dve.tensor_tensor(i_hot[:, slot], bc(i_eq[:, slot], 1, 3), bc(w3[:, :, bass.ds(token, NB)], 2, PH),
                                  ALU.mult).then_inc(S["i_ready"], 1)

            flat_ps = psum[:].rearrange("p a b -> p (a b)")

            def collect(n, bank0, ph, step):
                dve.wait_ge(S["g_psum"], n + 1)
                dve.tensor_copy(small[0:1, 62:63], iota[0:1, 0:1])
                for b0, nb in ((0, 5), (5, NB - 5)):
                    lo = (bank0 + b0 // 5) * BANK
                    parts = flat_ps[:, lo:lo + nb * 3 * PH].rearrange("p (b a i) -> p b i a", b=nb, a=3)
                    out = g_phase[ph % 2][:, bass.ds(step, 1), :, b0:b0 + nb].rearrange("p k i b -> p (k b) i")
                    ins = dve.tensor_reduce(out, parts, AX, ALU.add)
                ins.then_inc(S["g_copied"], 1)

            def even_hits(pair, token):
                find_i(0, token, 0)
                find_j(0, token)
                put_weights(0, pair, token)

            def pair_of_steps(pair, token, start=False):
                if not start:
                    collect(2 * pair - 1, 6, 0, 2 * pair - 1)
                find_j(1, token + NB)
                dve.wait_ge(S["i_ready_odd"], pair + 1)
                find_i(1, token + 3 * NB, 0, S["i_eq_odd"])
                collect(2 * pair, 6, 0, 2 * pair)
                even_hits(pair + 1, token + 2 * NB)

            even_hits(0, 0)
            find_i(1, NB, 0, S["i_eq_odd"])
            pair_of_steps(0, 0, True)
            with dve.Fori(1, PH // 2 - 1) as pair:
                pair_of_steps(pair, 2 * NB * pair)
            collect(PH - 3, 6, 0, PH - 3)
            find_j(1, NB * (PH - 1))
            collect(PH - 2, 6, 0, PH - 2)
            find_i(0, 0, 1)
            find_j(0, 0)
            put_weights(0, PH // 2, 0)
            collect(PH - 1, 6, 0, PH - 1)
            dve.wait_ge(S["act_ready"], PH)

            def low_u(slot, n):
                dve.wait_ge(S["uT_hi_ready"], n + 1)
                dve.tensor_tensor(uT_lo[:, slot % 2].rearrange("p a b -> p (a b)"), flat_ps[:, 4 * BANK:6 * BANK],
                                  uT_hi[:, slot % 2].rearrange("p a b -> p (a b)").bitcast(F32), ALU.subtract
                                  ).then_inc(S["uT_lo_ready"], 1)

            def add_y(s, n, i):
                c = 4 * (s % 2) + i
                dve.wait_ge(S["y_psum"], 4 * n + (i - 7))
                dve.tensor_tensor(xT[:, c, :], xT[:, c, :], psum[:, i % 2, 0:NT], ALU.add
                                  ).then_inc(S["y_added"], 1)

            def quad(q, ph, start=False, stop=False):
                spreads = ph < NU // PH - 1
                for s in range(4):
                    n = 4 * q + s
                    in_ph = n - ph * PH
                    if spreads and ph > 0:
                        dve.wait_ge(S["g_psum"], n + PH - 1)
                        find_i(s % 2, NB * in_ph, ph + 1)
                        find_j(s % 2, NB * in_ph)
                        put_weights(s % 2, n, NB * in_ph)
                    if ph > 0:
                        if not (stop and s == 3):
                            low_u(s + 1, n + 1)
                        dve.wait_ge(S["act_ready"], n + 1)
                        gelu = act_g[:, s % 2, :]
                    else:
                        gelu = g_odd[:, bass.ds(n, 1)].rearrange("p k a b -> p (k a b)")
                    if not (start and s < 2):
                        dve.wait_ge(S["ag_lo_ready"], n - 1)
                    dve.wait_ge(S["g_copied"], n + PH if spreads else NU)
                    dve.tensor_tensor(ag[:, s % 2, :].rearrange("p (k b) -> p k b", b=NB),
                                      gelu.rearrange("p (k b) -> p k b", b=NB),
                                      g_phase[ph % 2][:, :, bass.ds(in_ph, 1), :].rearrange("p k a b -> p k (a b)"),
                                      ALU.mult).then_inc(S["prod_ready"], 1)
                    if ph > 0:
                        for i in range(4):
                            add_y(s, n, i)
                    else:
                        add = (lambda i: None) if start and s < 2 else (lambda i: add_y(s, n, i))
                        token = NB * n + NB
                        hit = not (stop and s == 3)
                        add(0)
                        if hit:
                            find_i((s + 1) % 2, token, 1, S["i_eq_ready" if s % 2 else "i_eq_odd"])
                        add(1)
                        if hit:
                            find_j((s + 1) % 2, token)
                        add(2)
                        if hit and s % 2:
                            put_weights(0, 2 * q + ((s + 1) // 2 + PH // 2), token)
                        dve.wait_ge(S["prod_ready"], n + 1)
                        dve.tensor_copy(small[0:1, 61:62], iota[0:1, 0:1])
                        add(3)
                    if spreads:
                        collect(n + PH, 6, ph + 1, in_ph)

            phases(dve, quad)
            for s in range(2):
                for i in range(4):
                    add_y(s, NU + s, i)
    ctx.close()


_INS = ["x_prompt", "x_sample", "cache_k", "cache_v", "cache_ik", "state_pool", "page_table", "norm1_g", "w_in",
        "q_norm_g", "k_norm_g", "w_pool", "pool_scale", "w_o", "norm2_g", "w_pq", "sub_keys", "expert_u", "expert_v"]


def kernel(**inputs):
    import concourse.bacc as bacc
    from concourse.bass_utils import run_bass_kernel_spmd

    nc = bacc.Bacc("TRN2", target_bir_lowering=False, num_devices=1)
    a = {n: np.ascontiguousarray(inputs[n]) for n in _INS}
    _, SEQ, D = a["x_prompt"].shape
    DB, DS, _ = a["x_sample"].shape
    HD, ID = a["cache_k"].shape[3], a["cache_ik"].shape[3]
    NST, PW = a["state_pool"].shape[2:]
    IH = (a["w_in"].shape[2] - PW - (D - PW) - 2 * HD - ID) // (ID + 1)
    PAST = a["page_table"].shape[1] * a["cache_k"].shape[2]
    a.update(shape_constants(SEQ, DB, DS, PAST, (D - PW) // HD, HD, IH, ID, NST))
    outs = [("y_prompt", (1, SEQ, D)), ("y_sample", (DB, DS, D)),
            ("k_prompt", (1, 1, SEQ, HD)), ("v_prompt", (1, 1, SEQ, HD)), ("ik_prompt", (1, 1, SEQ, ID)),
            ("pool_prompt", (1, 1, NST, PW)), ("k_sample", (1, DB, DS, HD)), ("v_sample", (1, DB, DS, HD)),
            ("ik_sample", (1, DB, DS, ID)), ("pool_sample", (1, DB, NST, PW))]
    args = {n: nc.dram_tensor(n, v.shape, mybir.dt.from_np(v.dtype), kind="ExternalInput").ap() for n, v in a.items()}
    for n, shape in outs:
        args[n] = nc.dram_tensor(n, shape, F32, kind="ExternalOutput").ap()
    hybrid_kernel(nc, **args)
    r = run_bass_kernel_spmd(nc, [a], core_ids=[0])
    return tuple(r.results[0][n] for n, _ in outs)
```
